# Optimizing a Trainium2 kernel written in Bass

```python
import jax
import jax.numpy as jnp
from jax import lax
import numpy as np

D_MODEL = 1024
BATCH = 1
SEQ = 256
DEPTH = 1

CTX_LEN = 256
GRID_W = 64
D_MIX = D_MODEL
HEAD_DIM = 64
D_POOL = D_MIX // 4
D_RWKV = (D_MIX - D_POOL) // 2
D_HGRN = D_MIX - D_POOL - D_RWKV
POOL_WINDOWS = (2, 4, 8, 16)
N_POOL_GROUPS = len(POOL_WINDOWS)
POOL_GROUP = D_POOL // N_POOL_GROUPS
H_RWKV = D_RWKV // HEAD_DIM
H_HGRN = D_HGRN // HEAD_DIM
LORA_W = 64
LORA_A = 64
N_DIR = 2
HGRN_CHUNK = 32
D_RWKV_IN = 3 * D_RWKV + N_DIR * (LORA_W + LORA_A)
D_IN = D_POOL + D_RWKV_IN + 2 * D_HGRN + N_DIR * D_HGRN + D_MIX
ALPHA = float((2 * DEPTH) ** 0.25)
BETA = float((8 * DEPTH) ** -0.25)
LN_EPS = 1e-5
GN_EPS = 64e-5
RMS_EPS = 1e-6


def _layer_norm(x):
    xf = x.astype(jnp.float32)
    mu = jnp.mean(xf, axis=-1, keepdims=True)
    var = jnp.mean(jnp.square(xf - mu), axis=-1, keepdims=True)
    return (xf - mu) * lax.rsqrt(var + LN_EPS)

def _heads(z):
    return z.reshape(z.shape[:-1] + (z.shape[-1] // HEAD_DIM, HEAD_DIM))

def _split_proj(p):
    o0 = D_POOL
    o1 = o0 + D_RWKV_IN
    o2 = o1 + 2 * D_HGRN + N_DIR * D_HGRN
    return p[..., :o0], p[..., o0:o1], p[..., o1:o2], p[..., o2:]

def _centred_mean(u, axis, window):
    n = u.shape[axis]
    left = window // 2
    right = window - 1 - left
    t = jnp.arange(n)
    lo = jnp.maximum(t - left, 0)
    hi = jnp.minimum(t + right, n - 1) + 1
    pad = [(0, 0)] * u.ndim
    pad[axis] = (1, 0)
    cs = jnp.pad(jnp.cumsum(u, axis=axis), pad)
    total = jnp.take(cs, hi, axis=axis) - jnp.take(cs, lo, axis=axis)
    shape = [1] * u.ndim
    shape[axis] = n
    count = (hi - lo).astype(jnp.float32).reshape(shape)
    return total / count

def _pool_branch(u, grid, pool_w, pool_scale):
    b, n, _ = u.shape
    uf = u.astype(jnp.float32)
    if grid:
        rows = n // GRID_W
        uf = uf.reshape(b, rows, GRID_W, D_POOL)
        axis = 2
    else:
        axis = 1
    groups = []
    for g, win in enumerate(POOL_WINDOWS):
        ch = uf[..., g * POOL_GROUP:(g + 1) * POOL_GROUP]
        groups.append(_centred_mean(ch, axis, win) - ch)
    pooled = jnp.stack(groups, axis=-2)
    mixed = jnp.einsum('...gi,gio->...go', pooled, pool_w)
    return mixed.reshape(b, n, D_POOL) * pool_scale

def _shift3(u, w):
    up = jnp.pad(u, ((0, 0), (1, 1), (0, 0)))
    return w[0] * up[:, :-2] + w[1] * up[:, 1:-1] + w[2] * up[:, 2:]

def _rwkv_dir_inputs(u, d, w0, w_up, a0, a_up, k_k, k_a):
    r = u[..., :D_RWKV]
    k = u[..., D_RWKV:2 * D_RWKV]
    v = u[..., 2 * D_RWKV:3 * D_RWKV]
    o = 3 * D_RWKV
    xw = u[..., o + d * LORA_W:o + (d + 1) * LORA_W]
    o2 = o + N_DIR * LORA_W
    xa = u[..., o2 + d * LORA_A:o2 + (d + 1) * LORA_A]
    w_log = -jax.nn.softplus(-(w0[d] + jnp.tanh(xw) @ w_up[d])) - 0.5
    decay = jnp.exp(-jnp.exp(w_log))
    a = jax.nn.sigmoid(a0[d] + xa @ a_up[d])
    kk = _heads(k * k_k)
    kk = kk * lax.rsqrt(jnp.sum(kk * kk, axis=-1, keepdims=True) + 1e-12)
    k_mod = k * (1.0 + (a - 1.0) * k_a)
    return (_heads(r), _heads(decay), _heads(k_mod), _heads(v), kk, _heads(a))

def _rwkv_bonus(ins, r_k_d):
    r, k_mod, v = ins[0], ins[2], ins[3]
    return jnp.sum(r * k_mod * r_k_d, axis=-1, keepdims=True) * v

def _rwkv_scan(state, ins, emit):
    r, w, k, v, kk, a = (jnp.moveaxis(z, 1, 0) for z in ins)
    xs = (w, k, v, kk, a, r) if emit else (w, k, v, kk, a)

    def step(S, inp):
        w_t, k_t, v_t, kk_t, a_t = inp[:5]
        sa = jnp.einsum('bhvk,bhk->bhv', S, kk_t)
        S = (S * w_t[:, :, None, :] - sa[..., None] * (kk_t * a_t)[:, :, None, :]
             + v_t[..., None] * k_t[:, :, None, :])
        y = jnp.einsum('bhvk,bhk->bhv', S, inp[5]) if emit else None
        return S, y

    state, ys = lax.scan(step, state, xs)
    return state, (jnp.moveaxis(ys, 0, 1) if emit else None)

def _rwkv_readout(y, bonus, gn_g, gn_b):
    mu = jnp.mean(y, axis=-1, keepdims=True)
    var = jnp.mean(jnp.square(y - mu), axis=-1, keepdims=True)
    yn = (y - mu) * lax.rsqrt(var + GN_EPS) * gn_g.reshape(H_RWKV, HEAD_DIM) + gn_b.reshape(H_RWKV, HEAD_DIM)
    out = yn + bonus
    return out.reshape(out.shape[:-2] + (D_RWKV,))

def _rwkv_branch(u_ctx, u_lat, w0, w_up, a0, a_up, k_k, k_a, r_k, gn_g, gn_b, emit_ctx):
    b = u_lat.shape[0]
    y_ctx, y_lat, bonus_ctx, bonus_lat = 0.0, 0.0, 0.0, 0.0
    for d in range(N_DIR):
        ins_c = _rwkv_dir_inputs(u_ctx, d, w0, w_up, a0, a_up, k_k, k_a)
        ins_l = _rwkv_dir_inputs(u_lat, d, w0, w_up, a0, a_up, k_k, k_a)
        bonus_lat = bonus_lat + _rwkv_bonus(ins_l, r_k[d])
        if emit_ctx:
            bonus_ctx = bonus_ctx + _rwkv_bonus(ins_c, r_k[d])
        if d == 1:
            ins_c = tuple(jnp.flip(z, axis=1) for z in ins_c)
            ins_l = tuple(jnp.flip(z, axis=1) for z in ins_l)
        s0 = jnp.zeros((b, H_RWKV, HEAD_DIM, HEAD_DIM), jnp.float32)
        s_c, yc = _rwkv_scan(s0, ins_c, emit_ctx)
        _, yl = _rwkv_scan(s_c, ins_l, True)
        if d == 1:
            yl = jnp.flip(yl, axis=1)
            if emit_ctx:
                yc = jnp.flip(yc, axis=1)
        y_lat = y_lat + yl
        if emit_ctx:
            y_ctx = y_ctx + yc
    out_lat = _rwkv_readout(y_lat, bonus_lat, gn_g, gn_b)
    out_ctx = _rwkv_readout(y_ctx, bonus_ctx, gn_g, gn_b) if emit_ctx else None
    return out_ctx, out_lat

def _hgrn_dir_inputs(fh, d, lb_d):
    q = fh[..., :D_HGRN]
    i = fh[..., D_HGRN:2 * D_HGRN]
    z = fh[..., (2 + d) * D_HGRN:(3 + d) * D_HGRN]
    logf = jnp.logaddexp(jnp.log(lb_d), jnp.log1p(-lb_d) + jax.nn.log_sigmoid(z))
    k = (1.0 - lb_d) * jax.nn.sigmoid(-z)
    return (_heads(k), _heads(i), _heads(logf), _heads(q))

def _hgrn_scan(state, ins, emit):
    k, i, logf, q = ins
    b, n, h, dk = k.shape
    nc = n // HGRN_CHUNK

    def chunks(z):
        return z.reshape(b, nc, HGRN_CHUNK, h, dk).transpose(1, 0, 3, 2, 4)

    causal = jnp.tril(jnp.ones((HGRN_CHUNK, HGRN_CHUNK), dtype=bool))[:, :, None]

    def step(S, inp):
        k_c, i_c, lf_c = inp[:3]
        g = jnp.cumsum(lf_c, axis=2)
        g_last = g[:, :, -1:, :]
        if emit:
            q_c = inp[3]
            inter = jnp.einsum('bhtk,bhkv->bhtv', q_c * jnp.exp(g), S)
            rel = jnp.exp(jnp.where(causal, g[:, :, :, None, :] - g[:, :, None, :, :], -jnp.inf))
            scores = jnp.einsum('bhtk,bhsk,bhtsk->bhts', q_c, k_c, rel)
            o = inter + jnp.einsum('bhts,bhsv->bhtv', scores, i_c)
        else:
            o = None
        S = (jnp.exp(g_last[:, :, 0, :])[..., None] * S
             + jnp.einsum('bhsk,bhsv->bhkv', k_c * jnp.exp(g_last - g), i_c))
        return S, o

    xs = (chunks(k), chunks(i), chunks(logf), chunks(q)) if emit else (chunks(k), chunks(i), chunks(logf))
    state, o = lax.scan(step, state, xs)
    if emit:
        o = o.transpose(1, 0, 3, 2, 4).reshape(b, n, h, dk)
    return state, o

def _rms_heads(o, norm_g):
    on = o * lax.rsqrt(jnp.mean(o * o, axis=-1, keepdims=True) + RMS_EPS) * norm_g.reshape(H_HGRN, HEAD_DIM)
    return on.reshape(on.shape[:-2] + (D_HGRN,))

def _hgrn_branch(fh_ctx, fh_lat, lb, norm_g, emit_ctx):
    b = fh_lat.shape[0]
    o_ctx, o_lat = 0.0, 0.0
    for d in range(N_DIR):
        ins_c = _hgrn_dir_inputs(fh_ctx, d, lb[d])
        ins_l = _hgrn_dir_inputs(fh_lat, d, lb[d])
        if d == 1:
            ins_c = tuple(jnp.flip(z, axis=1) for z in ins_c)
            ins_l = tuple(jnp.flip(z, axis=1) for z in ins_l)
        s0 = jnp.zeros((b, H_HGRN, HEAD_DIM, HEAD_DIM), jnp.float32)
        s_c, oc = _hgrn_scan(s0, ins_c, emit_ctx)
        _, ol = _hgrn_scan(s_c, ins_l, True)
        if d == 1:
            ol = jnp.flip(ol, axis=1)
            if emit_ctx:
                oc = jnp.flip(oc, axis=1)
        o_lat = o_lat + ol
        if emit_ctx:
            o_ctx = o_ctx + oc
    out_ctx = _rms_heads(o_ctx, norm_g) if emit_ctx else None
    return out_ctx, _rms_heads(o_lat, norm_g)

def first_inputs(seed: int = 0) -> dict:
    key = jax.random.key(seed)
    ks = jax.random.split(key, 24)
    f32 = jnp.float32

    def nrm(k, shape, scale):
        return scale * jax.random.normal(k, shape, f32)

    return {
        "x": nrm(ks[0], (BATCH, SEQ, D_MODEL), 1.0),
        "c": nrm(ks[1], (BATCH, D_MODEL), 1.0),
        "ctx": nrm(ks[2], (BATCH, CTX_LEN, D_MODEL), 1.0),
        "c_ctx": nrm(ks[3], (D_MODEL,), 1.0),
        "mod_w": nrm(ks[4], (DEPTH, D_MODEL, 3 * D_MODEL), D_MODEL ** -0.5),
        "mod_b": nrm(ks[5], (DEPTH, 3 * D_MODEL), 0.02),
        "w_in": nrm(ks[6], (DEPTH, D_MODEL, D_IN), D_MODEL ** -0.5),
        "rwkv_shift": jnp.array([0.25, 0.5, 0.25], f32)[None, :, None] + nrm(ks[7], (DEPTH, 3, D_RWKV_IN), 0.05),
        "pool_w": nrm(ks[8], (DEPTH, N_POOL_GROUPS, POOL_GROUP, POOL_GROUP), POOL_GROUP ** -0.5),
        "pool_scale": 1.0 + nrm(ks[9], (DEPTH, D_POOL), 0.1),
        "rwkv_w0": jax.random.uniform(ks[10], (DEPTH, N_DIR, D_RWKV), f32, minval=-5.0, maxval=-0.5),
        "rwkv_w_up": nrm(ks[11], (DEPTH, N_DIR, LORA_W, D_RWKV), 0.5 * LORA_W ** -0.5),
        "rwkv_a0": nrm(ks[12], (DEPTH, N_DIR, D_RWKV), 0.1),
        "rwkv_a_up": nrm(ks[13], (DEPTH, N_DIR, LORA_A, D_RWKV), LORA_A ** -0.5),
        "rwkv_k_k": 0.85 + nrm(ks[14], (DEPTH, D_RWKV), 0.05),
        "rwkv_k_a": 1.0 + nrm(ks[15], (DEPTH, D_RWKV), 0.05),
        "rwkv_r_k": nrm(ks[16], (DEPTH, N_DIR, H_RWKV, HEAD_DIM), 0.1),
        "rwkv_gn_g": 1.0 + nrm(ks[17], (DEPTH, D_RWKV), 0.05),
        "rwkv_gn_b": nrm(ks[18], (DEPTH, D_RWKV), 0.02),
        "hgrn_lb_logits": nrm(ks[19], (N_DIR, DEPTH, D_HGRN), 0.5),
        "hgrn_norm_g": 1.0 + nrm(ks[20], (DEPTH, D_HGRN), 0.05),
        "w_out": nrm(ks[21], (DEPTH, D_MIX, D_MODEL), BETA * D_MIX ** -0.5),
        "ln_g": 1.0 + nrm(ks[22], (DEPTH, D_MODEL), 0.05),
        "ln_b": nrm(ks[23], (DEPTH, D_MODEL), 0.02),
    }

def first_block(x, c, ctx, c_ctx, mod_w, mod_b, w_in, rwkv_shift, pool_w, pool_scale,
              rwkv_w0, rwkv_w_up, rwkv_a0, rwkv_a_up, rwkv_k_k, rwkv_k_a, rwkv_r_k,
              rwkv_gn_g, rwkv_gn_b, hgrn_lb_logits, hgrn_norm_g, w_out, ln_g, ln_b):
    out_dtype = x.dtype
    lb_w = jax.nn.softmax(hgrn_lb_logits.astype(jnp.float32), axis=1)
    lb_all = jnp.maximum(jnp.cumsum(lb_w, axis=1) - lb_w[:, :1], 0.0)
    h_x = x.astype(jnp.float32)
    h_ctx = ctx.astype(jnp.float32)
    for l in range(DEPTH):
        last = l == DEPTH - 1
        mod_lat = jax.nn.silu(c.astype(jnp.float32)) @ mod_w[l] + mod_b[l]
        mod_c = jax.nn.silu(c_ctx.astype(jnp.float32)) @ mod_w[l] + mod_b[l]
        sh_l, sc_l, gt_l = jnp.split(mod_lat, 3, axis=-1)
        sh_c, sc_c, gt_c = jnp.split(mod_c, 3, axis=-1)
        p_lat = (_layer_norm(h_x) * (1.0 + sc_l[:, None]) + sh_l[:, None]) @ w_in[l]
        p_ctx = (_layer_norm(h_ctx) * (1.0 + sc_c) + sh_c) @ w_in[l]
        pv_l, u_l, fh_l, g_l = _split_proj(p_lat)
        pv_c, u_c, fh_c, g_c = _split_proj(p_ctx)
        u_l = _shift3(u_l, rwkv_shift[l])
        u_c = _shift3(u_c, rwkv_shift[l])
        y_rc, y_rl = _rwkv_branch(u_c, u_l, rwkv_w0[l], rwkv_w_up[l], rwkv_a0[l], rwkv_a_up[l],
                                  rwkv_k_k[l], rwkv_k_a[l], rwkv_r_k[l], rwkv_gn_g[l], rwkv_gn_b[l],
                                  not last)
        o_hc, o_hl = _hgrn_branch(fh_c, fh_l, lb_all[:, l], hgrn_norm_g[l], not last)
        pool_l = _pool_branch(pv_l, True, pool_w[l], pool_scale[l])
        mix_l = jnp.concatenate([pool_l, y_rl, o_hl], axis=-1) * jax.nn.silu(g_l)
        new_x = _layer_norm(ALPHA * h_x + gt_l[:, None] * (mix_l @ w_out[l])) * ln_g[l] + ln_b[l]
        if not last:
            pool_c = _pool_branch(pv_c, False, pool_w[l], pool_scale[l])
            mix_c = jnp.concatenate([pool_c, y_rc, o_hc], axis=-1) * jax.nn.silu(g_c)
            h_ctx = _layer_norm(ALPHA * h_ctx + gt_c * (mix_c @ w_out[l])) * ln_g[l] + ln_b[l]
        h_x = new_x
    return h_x.astype(out_dtype)


DEPTH_2 = 2

SB_HEADS = 8
FOX_HEADS = 8
DSA_HEADS = 8
DSA_KV_HEADS = 2
DSA_GROUP = DSA_HEADS // DSA_KV_HEADS
IDX_HEADS = 4
IDX_DIM = 64
BRANCH_WIDTH = SB_HEADS * HEAD_DIM
N_BRANCH = 3
D_FF = 4 * D_MODEL
ROPE_THETA = 500000.0
ROT_DIM = HEAD_DIM // 4
Q_BLOCK = 128
TOPK_MAX = 256
NORM_EPS = 1e-6

COL_SIZES = (
    SB_HEADS * HEAD_DIM, SB_HEADS * HEAD_DIM, SB_HEADS * HEAD_DIM,
    FOX_HEADS * HEAD_DIM, FOX_HEADS * HEAD_DIM, FOX_HEADS * HEAD_DIM,
    FOX_HEADS,
    DSA_HEADS * HEAD_DIM, DSA_KV_HEADS * HEAD_DIM, DSA_KV_HEADS * HEAD_DIM,
    IDX_HEADS * IDX_DIM, IDX_DIM, IDX_HEADS,
    N_BRANCH * D_MODEL,
)
COL_TOTAL = sum(COL_SIZES)
COL_SPLITS = tuple(sum(COL_SIZES[:i + 1]) for i in range(len(COL_SIZES) - 1))


def _rmsnorm(x, g):
    xf = x.astype(jnp.float32)
    y = xf * lax.rsqrt(jnp.mean(xf * xf, axis=-1, keepdims=True) + NORM_EPS)
    return (y * g.astype(jnp.float32)).astype(x.dtype)

def _partial_rope(x, positions):
    half = ROT_DIM // 2
    inv_freq = ROPE_THETA ** (-jnp.arange(0, ROT_DIM, 2, dtype=jnp.float32) / ROT_DIM)
    ang = positions.astype(jnp.float32)[:, :, None] * inv_freq
    cos = jnp.cos(ang)[:, :, None, :]
    sin = jnp.sin(ang)[:, :, None, :]
    xf = x.astype(jnp.float32)
    x1, x2, rest = xf[..., :half], xf[..., half:ROT_DIM], xf[..., ROT_DIM:]
    out = jnp.concatenate([x1 * cos - x2 * sin, x2 * cos + x1 * sin, rest], axis=-1)
    return out.astype(x.dtype)

def _to_blocks(a):
    b, s = a.shape[0], a.shape[1]
    return jnp.moveaxis(a.reshape(b, s // Q_BLOCK, Q_BLOCK, *a.shape[2:]), 1, 0)

def _from_blocks(a):
    a = jnp.moveaxis(a, 0, 1)
    return a.reshape(a.shape[0], a.shape[1] * a.shape[2], *a.shape[3:])

def _stick_breaking_attention(q, k, v):
    b, s, h, dh = q.shape
    scale = dh ** -0.5
    kf = k.astype(jnp.float32)
    vf = v.astype(jnp.float32)
    s_idx = jnp.arange(s)
    t_blk = jnp.arange(s).reshape(s // Q_BLOCK, Q_BLOCK)

    def block(args):
        qb, tb = args
        z = jnp.einsum('bthd,bshd->bhts', qb.astype(jnp.float32), kf) * scale
        strict = s_idx[None, :] < tb[:, None]
        log_beta = jax.nn.log_sigmoid(z)
        log_1m = jnp.where(strict, jax.nn.log_sigmoid(-z), 0.0)
        later = lax.cumsum(log_1m, axis=3, reverse=True) - log_1m
        w = jnp.where(strict, jnp.exp(log_beta + later), 0.0)
        return jnp.einsum('bhts,bshd->bthd', w, vf)

    out = lax.map(block, (_to_blocks(q), t_blk))
    return _from_blocks(out).reshape(b, s, h * dh).astype(q.dtype)

def _forgetting_attention(q, k, v, log_f):
    b, s, h, dh = q.shape
    scale = dh ** -0.5
    kf = k.astype(jnp.float32)
    vf = v.astype(jnp.float32)
    c = jnp.cumsum(log_f, axis=1).transpose(0, 2, 1)
    c_blk = jnp.moveaxis(c.reshape(b, h, s // Q_BLOCK, Q_BLOCK), 2, 0)
    s_idx = jnp.arange(s)
    t_blk = jnp.arange(s).reshape(s // Q_BLOCK, Q_BLOCK)

    def block(args):
        qb, cb, tb = args
        z = jnp.einsum('bthd,bshd->bhts', qb.astype(jnp.float32), kf) * scale
        z = z + cb[..., None] - c[:, :, None, :]
        causal = s_idx[None, :] <= tb[:, None]
        p = jax.nn.softmax(jnp.where(causal, z, -jnp.inf), axis=-1)
        return jnp.einsum('bhts,bshd->bthd', p, vf)

    out = lax.map(block, (_to_blocks(q), c_blk, t_blk))
    return _from_blocks(out).reshape(b, s, h * dh).astype(q.dtype)

def _indexed_sparse_attention(q, k, v, q_idx, k_idx, w_idx, top_k):
    b, s, g, r, dh = q.shape
    scale = dh ** -0.5
    kif = k_idx.astype(jnp.float32)
    s_idx = jnp.arange(s)
    t_blk = jnp.arange(s).reshape(s // Q_BLOCK, Q_BLOCK)
    gather = jax.vmap(lambda a, i: a[i])

    def block(args):
        qb, qib, wb, tb = args
        dots = jnp.einsum('bthi,bsi->bths', qib.astype(jnp.float32), kif) * (IDX_DIM ** -0.5)
        score = jnp.einsum('bth,bths->bts', wb.astype(jnp.float32) * (IDX_HEADS ** -0.5),
                           jax.nn.relu(dots))
        causal = s_idx[None, :] <= tb[:, None]
        score = jnp.where(causal[None], score, -jnp.inf)
        _, sel = lax.top_k(score, top_k)
        valid = sel <= tb[None, :, None]
        k_sel = gather(k, sel).astype(jnp.float32)
        v_sel = gather(v, sel).astype(jnp.float32)
        z = jnp.einsum('btgrd,btkgd->btgrk', qb.astype(jnp.float32), k_sel) * scale
        z = jnp.where(valid[:, :, None, None, :], z, -jnp.inf)
        p = jax.nn.softmax(z, axis=-1)
        return jnp.einsum('btgrk,btkgd->btgrd', p, v_sel)

    out = lax.map(block, (_to_blocks(q), _to_blocks(q_idx), _to_blocks(w_idx), t_blk))
    return _from_blocks(out).reshape(b, s, g * r * dh).astype(q.dtype)

def _layer(x, positions, g_mix, w_in, b_forget, w_branch, w_out, g_mlp, w_up, w_down):
    b, s, _ = x.shape
    h = _rmsnorm(x, g_mix)
    proj = h @ w_in
    (qa, ka, va, qb, kb, vb, fl, qc, kc, vc, qi, ki, wi, gl) = jnp.split(proj, COL_SPLITS, axis=-1)

    def heads(a, n):
        return a.reshape(b, s, n, -1)

    br_a = _stick_breaking_attention(heads(qa, SB_HEADS), heads(ka, SB_HEADS), heads(va, SB_HEADS))
    log_f = jax.nn.log_sigmoid((fl + b_forget).astype(jnp.float32))
    br_b = _forgetting_attention(heads(qb, FOX_HEADS), heads(kb, FOX_HEADS),
                                 heads(vb, FOX_HEADS), log_f)
    qc = _partial_rope(heads(qc, DSA_HEADS), positions).reshape(b, s, DSA_KV_HEADS, DSA_GROUP, HEAD_DIM)
    kc = _partial_rope(heads(kc, DSA_KV_HEADS), positions)
    vc = heads(vc, DSA_KV_HEADS)
    qi = _partial_rope(heads(qi, IDX_HEADS), positions)
    ki = _partial_rope(ki[:, :, None, :], positions)[:, :, 0, :]
    top_k = min(TOPK_MAX, s // 4)
    br_c = _indexed_sparse_attention(qc, kc, vc, qi, ki, wi, top_k)

    gates = jax.nn.sigmoid(gl.reshape(b, s, N_BRANCH, D_MODEL))
    y = (gates[:, :, 0, :] * (br_a @ w_branch[0])
         + gates[:, :, 1, :] * (br_b @ w_branch[1])
         + gates[:, :, 2, :] * (br_c @ w_branch[2]))
    x = x + y @ w_out

    h2 = _rmsnorm(x, g_mlp)
    x = x + jnp.square(jax.nn.relu(h2 @ w_up)) @ w_down
    return x

def second_inputs(seed: int = 0) -> dict:
    key = jax.random.key(seed)
    ks = jax.random.split(key, 12)
    f32 = jnp.float32
    x = jax.random.normal(ks[0], (BATCH, SEQ, D_MODEL), f32)
    positions = jnp.broadcast_to(jnp.arange(SEQ, dtype=jnp.int32), (BATCH, SEQ))
    g_mix = 1.0 + 0.02 * jax.random.normal(ks[1], (DEPTH_2, D_MODEL), f32)
    w_in = jax.random.normal(ks[2], (DEPTH_2, D_MODEL, COL_TOTAL), f32) * D_MODEL ** -0.5
    b_forget = jax.random.uniform(ks[3], (DEPTH_2, FOX_HEADS), f32, minval=1.0, maxval=4.0)
    w_branch = jax.random.normal(ks[4], (DEPTH_2, N_BRANCH, BRANCH_WIDTH, D_MODEL), f32) * BRANCH_WIDTH ** -0.5
    w_out = jax.random.normal(ks[5], (DEPTH_2, D_MODEL, D_MODEL), f32) * D_MODEL ** -0.5
    g_mlp = 1.0 + 0.02 * jax.random.normal(ks[6], (DEPTH_2, D_MODEL), f32)
    w_up = jax.random.normal(ks[7], (DEPTH_2, D_MODEL, D_FF), f32) * D_MODEL ** -0.5
    w_down = jax.random.normal(ks[8], (DEPTH_2, D_FF, D_MODEL), f32) * D_FF ** -0.5
    g_final = 1.0 + 0.02 * jax.random.normal(ks[9], (D_MODEL,), f32)
    return {'x': x, 'positions': positions, 'g_mix': g_mix, 'w_in': w_in,
            'b_forget': b_forget, 'w_branch': w_branch, 'w_out': w_out,
            'g_mlp': g_mlp, 'w_up': w_up, 'w_down': w_down, 'g_final': g_final}

def second_block(x, positions, g_mix, w_in, b_forget, w_branch, w_out, g_mlp, w_up, w_down, g_final):
    for layer in range(DEPTH_2):
        x = _layer(x, positions, g_mix[layer], w_in[layer], b_forget[layer], w_branch[layer],
                   w_out[layer], g_mlp[layer], w_up[layer], w_down[layer])
    return _rmsnorm(x, g_final)


def setup_inputs(seed=0):
    out = dict(first_inputs(seed))
    for name, value in second_inputs(seed + 1).items():
        if name != "x":
            out[name + "_2"] = value
    return out


def reference(
    x, c, ctx, c_ctx, mod_w, mod_b, w_in, rwkv_shift, pool_w, pool_scale, rwkv_w0, rwkv_w_up,
    rwkv_a0, rwkv_a_up, rwkv_k_k, rwkv_k_a, rwkv_r_k, rwkv_gn_g, rwkv_gn_b, hgrn_lb_logits,
    hgrn_norm_g, w_out, ln_g, ln_b, positions_2, g_mix_2, w_in_2, b_forget_2, w_branch_2,
    w_out_2, g_mlp_2, w_up_2, w_down_2, g_final_2,
):
    x = first_block(
        x, c, ctx, c_ctx, mod_w, mod_b, w_in, rwkv_shift, pool_w, pool_scale, rwkv_w0,
        rwkv_w_up, rwkv_a0, rwkv_a_up, rwkv_k_k, rwkv_k_a, rwkv_r_k, rwkv_gn_g, rwkv_gn_b,
        hgrn_lb_logits, hgrn_norm_g, w_out, ln_g, ln_b,
    )
    return second_block(
        x, positions_2, g_mix_2, w_in_2, b_forget_2, w_branch_2, w_out_2, g_mlp_2, w_up_2,
        w_down_2, g_final_2,
    )


_drawn_inputs = setup_inputs


def setup_inputs(seed=0):
    import zlib

    import numpy as np

    out = dict(_drawn_inputs(seed))
    spreads = {}
    factors = {'rwkv_a0': 4.52,
     'rwkv_gn_g': 3.821,
     'rwkv_gn_b': 5.895,
     'hgrn_norm_g': 3.7,
     'g_final_2': 7.443,
     'pool_scale': 3.165}
    for name, (base, spread) in spreads.items():
        noise = np.random.default_rng([zlib.crc32(name.encode()), seed]).standard_normal(out[name].shape)
        drawn = base * np.exp(spread * noise) if base else spread * noise
        out[name] = jnp.asarray(drawn.astype(out[name].dtype))
    for name, factor in factors.items():
        out[name] = (out[name] * factor).astype(out[name].dtype)
    return out
```

```python
from contextlib import ExitStack

import numpy as np

import concourse.bass as bass
from concourse import mybir

F32 = mybir.dt.float32
I32 = mybir.dt.int32
ALU = mybir.AluOpType
ACT = mybir.ActivationFunctionType
AX = mybir.AxisListType.X

P = 128
D = 1024
KT = D // P
T = 256
HALF = 64
MODC = 3 * D
N_RW = 384
JT = N_RW // P
D_IN = 4224
COLS2 = 7244
FF = 4 * D
LAYERS = 2
HEADS = 8
LN_EPS, GN_EPS, RMS_EPS, NORM_EPS = 1e-5, 64e-5, 1e-6, 1e-6
ALPHA = float(2 ** 0.25)
DECAY = float(np.exp(-0.5))
NEG = -1e38
TOPK = 64
TAKEN = -3e38
SLOTS = 3
NB = 8

CONST = {}


def constants():
    parts = []

    def put(name, a):
        CONST[name] = (sum(p.shape[1] for p in parts), a.shape[1])
        parts.append(np.asarray(a, np.float32))

    r, c = np.arange(P)[:, None], np.arange(P)[None, :]
    put("ident", r == c)
    put("ones", np.ones((P, P)))
    put("blocks", r // HALF == c // HALF)
    for l in range(7):
        b = 1 << l
        up = (r // (2 * b) == c // (2 * b)) & (r // b % 2 == 0) & (c // b % 2 == 1)
        put(f"up{l}", up)
        put(f"down{l}", up.T)
    put("before", r < c)
    put("upto", r <= c)
    put("after", r > c)
    for g, win in enumerate((2, 4, 8, 16)):
        left, right = win // 2, win - 1 - win // 2
        row, x = np.arange(P) // 64, np.arange(P) % 64
        lo, hi = np.maximum(x - left, 0), np.minimum(x + right, 63)
        a = (row[:, None] == row[None, :]) & (x[:, None] >= lo[None, :]) & (x[:, None] <= hi[None, :])
        put(f"pool{g}", a / (hi - lo + 1)[None, :] - (r == c))
    s = np.concatenate([np.arange(P), np.arange(T)])[None, :]
    t = np.concatenate([np.arange(P)[:, None].repeat(P, 1), P + np.arange(P)[:, None].repeat(T, 1)], 1)
    put("strict", s < t)
    put("unstrict", s >= t)
    put("causal", np.where(s <= t, 0.0, NEG))
    put("keep", (np.arange(2 * T) % P != 0)[None, :].repeat(P, 0))
    k, m = r % HALF, c % HALF
    same = r // HALF == c // HALF
    put("rot", np.where(same & (m < 8) & (k == m + 8), -1.0, np.where(same & (m >= 8) & (m < 16) & (k == m - 8), 1.0, 0.0)))
    ch = np.arange(P) % HALF
    inv = np.float32(500000.0) ** (-(np.arange(0, 16, 2, dtype=np.float32)) / np.float32(16))
    put("freq", np.where(ch < 16, inv[ch % 8], 0.0)[:, None])
    return np.concatenate(parts, 1)


N_CONST = constants().shape[1]

STACK_A = [("mod_b", 24), ("rwkv_w0", 6), ("rwkv_a0", 6), ("rwkv_k_k", 3), ("rwkv_k_a", 3), ("rwkv_r_k", 6),
           ("rwkv_gn_g", 3), ("rwkv_gn_b", 3), ("hgrn_lb_logits", 6), ("hgrn_norm_g", 3), ("pool_scale", 2),
           ("ln_g", 8), ("ln_b", 8), ("rwkv_shift", 33), ("c", 8)]
STACK_B = [("c_ctx", 8), ("g_mix_2", 16), ("g_mlp_2", 16), ("g_final_2", 8)]
ROWS_A = sum(n for _, n in STACK_A)
ROWS_B = sum(n for _, n in STACK_B)
COL = {}
for _n, (_name, _rows) in enumerate(STACK_A + STACK_B):
    COL[_name] = sum(n for _, n in (STACK_A + STACK_B)[:_n])



def rows_of(w, k0, k1, c0, c1):
    return w[k0 * P:k1 * P, c0:c1].rearrange("(k p) n -> p k n", p=P)


FIRST = ([("mod_w", 512 * n, 512 * n + 512) for n in range(6)]
         + [("w_in", a, b) for a, b in ((1664, 2176), (2176, 2688), (2688, 3200), (256, 768), (768, 1280),
                                        (1280, 1664), (0, 256), (3200, 3712), (3712, 4224))]
         + [("w_out", 0, 512), ("w_out", 512, 1024)])
LAYER_IN = [[(0, 3080, 512)],
            [(0, 3592, 64), (64, 3592, 64), (128, 3656, 64), (192, 3656, 64), (256, 3848, 256)],
            [(0, 3720, 128), (128, 4104, 64), (192, 4104, 64), (256, 4168, 4), (260, 3072, 8)],
            [(0, 0, 512)], [(0, 512, 512)], [(0, 1024, 512)],
            [(0, 1536, 512)], [(0, 2048, 512)], [(0, 2560, 512)]] + [[(0, 4172 + 512 * n, 512)] for n in range(6)]
N_IN = len(LAYER_IN)
LAYER_CHUNKS = N_IN + 3 + 2 + 8 + 8
assert LAYER_CHUNKS % SLOTS == 0
PIECES = [1] * len(FIRST) + [len(x) for x in LAYER_IN] + [1] * (LAYER_CHUNKS - N_IN)


def landed(n):
    return 16 * sum(PIECES[m] for m in range(n % SLOTS, n + 1, SLOTS))


SLOT_PER_LAYER = [16 * sum(PIECES[len(FIRST) + i] for i in range(LAYER_CHUNKS) if (len(FIRST) + i) % SLOTS == s)
                  for s in range(SLOTS)]


class Banks:

    def __init__(self, sem, name, plan, loops=0):
        self.plan, self.loops = plan, loops
        self.filled = sem(name + "_filled")
        self.emptied = {"A": sem(name + "_emptied_act"), "D": sem(name + "_emptied_dve")}
        self.at = {g: k for k, (g, _) in enumerate(plan) if g}
        self.n_filled = sum(1 for g, _ in plan if g)
        self.n_emptied = {e: sum(1 for g, x in plan if g and x == e) for e in "AD"}
        assert not loops or len(plan) % NB == 0

    def bank(self, g):
        return self.at[g] % NB

    def _full(self, g):
        return sum(1 for x, _ in self.plan[:self.at[g] + 1] if x)

    def _empty(self, g):
        e = self.plan[self.at[g]][1]
        return e, sum(1 for x, y in self.plan[:self.at[g] + 1] if x and y == e)

    def start(self, eng, which):
        if self.loops:
            sem, n = (self.filled, self.n_filled) if which == "P" else (self.emptied[which], self.n_emptied[which])
            eng.sem_inc(sem, n)

    def wait_filled(self, eng, g, it=0, before=0):
        n = self._full(g) + (0 if before or not self.loops else self.n_filled)
        eng.wait_ge(self.filled, it * self.n_filled + n)

    def wait_emptied(self, eng, g, it=0, before=0):
        e, n = self._empty(g)
        n += 0 if before or not self.loops else self.n_emptied[e]
        eng.wait_ge(self.emptied[e], it * self.n_emptied[e] + n)

    def wait_free(self, pe, g, it=0):
        k, before = self.at[g] - NB, 0
        while k < 0 or not self.plan[k][0]:
            if k < 0:
                if not self.loops or before:
                    return
                k, before = k + len(self.plan), 1
            else:
                k -= NB
        self.wait_emptied(pe, self.plan[k][0], it, before)

    def wait_all(self, eng):
        for e in "AD":
            if self.n_emptied[e]:
                eng.wait_ge(self.emptied[e], self.n_emptied[e] * (self.loops + 1 if self.loops else 1))


def padded(plan):
    return plan + [(None, None)] * (-len(plan) % NB)


PLAN_SETUP = ([("colsA", "D"), ("colsB", "D")] + [(f"xr{g}", "D") for g in range(4)]
              + [(f"mod{n}", "A") for n in range(6)] + [("modT", "D")] + [(f"xt{k}", "A") for k in range(KT)]
              + [(f"fh{t}", "A") for t in range(12)] + [(f"u{t}", "D") for t in range(11)]
              + [("pv0", "D"), ("pv1", "D")] + [(f"g{n}", "A") for n in range(4)]
              + [(f"pool{n}", "A") for n in range(2)] + [(f"pmix{n}", "D") for n in range(2)])
PLAN_HGRN = padded([x for d in range(2) for x in
                    [(f"itok{d}", "A")] + [(f"diag{h}{d}", "D") for h in range(2)]
                    + [(f"lev{l}{h}{d}", "D") for l in range(7) for h in range(2)]
                    + [(f"cross{h}{d}", "A") for h in range(2)] + [ (f"ktok{d}", "A"), (f"state{d}", "D"), (f"o{d}", "D")]])
PLAN_LORA = [(f"{x}{d}{j}", "A") for d in range(2) for j in range(JT) for x in ("w", "a")]


def plan_rwkv(d):
    p = [(f"kk{d}", "A"), (f"bonus{d}", "D"), (f"ktok{d}", "A"), (f"btok{d}", "A"), (f"vtok{d}", "A")]
    p += [(f"{x}{g}{d}", "D") for x in ("lbT", "lb", "lk", "ak", "ab") for g in range(2)]
    for l in range(1, 7):
        p += [(f"w{l}{g}{d}", "A") for g in range(2)]
        for g in range(2):
            p += [(f"x{l}{g}{d}", "D")] + ([(f"xt{l}{g}{d}", "D")] if l < 6 else [])
    for c in range(4):
        p += [(f"rhs{c}{d}", "A"), (f"u{c}{d}", "A")] + ([(f"y{c}{d}", "D")] if c >= 2 else [])
        p += [(f"s{c}{d}", "D")] if c < 3 else []
    return p


PLAN_RWKV = padded(plan_rwkv(0) + plan_rwkv(1))
PLAN_READ = ([(f"ysum{n}", "D") for n in range(2)] + [(f"yvar{n}", "A") for n in range(2)]
             + [(f"osq{n}", "A") for n in range(2)] + [(f"wo{k}", "D") for k in range(KT)] + [("lnsum", "D"), ("lnvar", "A")])

STEPS = [("B", h) for h in range(HEADS)] + [("A", h) for h in range(HEADS)] + [("C", h) for h in range(HEADS)]


def plan_layer():
    p = [("ss1", "A"), ("qc0", "A"), ("qc1", "A"), ("kc", "A"), ("qi", "A"), ("vc", "A"), ("ki", "A"), ("wi", "D"), ("fl", "A")]
    p += [("rqc0", "D"), ("rqc1", "D"), ("rkc", "D"), ("rqi", "D"), ("rki", "D"), ("dot0", "A"), ("dot1", "A"), ("dot2", "A"), ("dot3", "A")]
    p += [(f"{x}{n}", "A") for x in ("qa", "ka", "va", "qb", "kb", "vb") for n in range(2)]
    for i in range(len(STEPS) + 1):
        if i < len(STEPS):
            p += [(f"z{i}", "A" if STEPS[i][0] == "A" else "D"), (f"gl{i}", "A")]
        if i:
            p += [(f"wT{i - 1}", "A"), (f"o{i - 1}", "A")]
    p += [(f"br{b}{n}", "D") for b in range(3) for n in range(4)] + [(f"out{n}", "D") for n in range(4)] + [("ss2", "A")]
    p += [(f"up{n}", "A") for n in range(16)] + [(f"dn{n}", "D") for n in range(8)]
    return padded(p)


PLAN_LAYER = plan_layer()
PLAN_END = [("ssf", "A")] + [(f"fin{m}{n}", "A") for m in range(2) for n in range(2)]


def build(nc, a, out, first=True, second=True, dump=None):
    ctx = ExitStack()
    with ctx:
        sems = {}

        def sem(name):
            if name not in sems:
                sems[name] = ctx.enter_context(nc.semaphore(name))
            return sems[name]

        arena = ctx.enter_context(nc.sbuf_tensor("arena", [P, 207 * 256], F32))
        top = [0]

        def take(n, shape=None):
            v = arena[:, top[0]:top[0] + n]
            top[0] += n
            assert top[0] <= 207 * 256, top[0]
            if shape:
                names = "abcd"[:len(shape)]
                v = v.rearrange("p (" + " ".join(names) + ") -> p " + " ".join(names),
                                **{x: s for x, s in zip(names, shape)})
            return v

        psum = ctx.enter_context(nc.psum_tensor("psum", [P, NB, 512], F32))

        ring = take(SLOTS * KT * 512, (SLOTS, KT, 512))
        const = take(N_CONST)
        cols = take(ROWS_A + ROWS_B)
        xr = take(KT * T, (KT, T))
        cos, sin = take(T), take(T)
        bf = take(2)
        pos_i = take(T).bitcast(I32)
        silu_c = take(16, (KT, 2))
        rstd4 = take(4)
        bcol, one_, epsc = take(1), take(1), take(6)
        zeros = take(T)
        EPS = [LN_EPS, GN_EPS, RMS_EPS, 1e-12]

        def eps(x):
            return epsc[:, EPS.index(x):EPS.index(x) + 1]

        lbw = take(6)
        omlb = take(6)
        base = top[0]

        def cst(name, rows=P):
            o, n = CONST[name]
            return const[0:rows, o:o + n]

        def cst_int(name):
            return cst(name).bitcast(I32)

        def col(name, n=0):
            return cols[:, COL[name] + n:COL[name] + n + 1]

        us = take(11 * 512, (11, 512))
        mix = take(KT * T, (KT, T))
        yacc = take(JT * T, (JT, T))
        bon = take(JT * T, (JT, T))
        oacc = take(JT * T, (JT, T))
        pv = take(2 * T, (2, T))
        rc = take(JT * 5, (JT, 5))
        pc = take(5)
        wup = take(N_RW)
        aup = take(N_RW)
        pw = take(2 * HALF, (2, HALF))
        pooled = take(2 * T, (2, T))
        modc = take(48, (24, 2))
        share = top[0]
        hq = take(JT * T, (JT, T))
        hi = take(JT * 512, (JT, 512))
        hf = take(6 * 512, (6, 512))
        hk = take(6 * 512, (6, 512))
        after_h = top[0]
        xt = take(KT * 512, (KT, 512))
        top[0] = share
        x4 = take(4 * D, (4, D))
        stackA, stackB = take(P), take(P)
        mrow = take(MODC)
        stats = take(4 * 12, (4, 2, 6))
        mv = take(8, (4, 2))
        assert top[0] <= after_h
        top[0] = after_h
        lq, lk, li, pi, se = take(T), take(512), take(512), take(512), take(512)
        ql, kl = take(2 * T, (2, T)), take(2 * T, (2, T))
        acc = take(512, (4, P))
        cross = take(2 * P, (2, P))
        itok, ktok = take(512, (4, P)), take(2 * P, (2, P))
        hstate = take(P)
        top[0] = share
        sa = take(12 * 512, (2, 6, 512))
        assert top[0] <= after_h
        rlr, rlk, rlv, rsw, rla, rl, pinc, pinv, pexc, kkr, km, rn = (
            take(T), *[take(512) for _ in range(11)])
        nlb, xi, xti, ww, lkm = [take(8 * P, (8, P)) for _ in range(5)]
        akm, abm = take(4 * P, (4, P)), take(4 * P, (4, P))
        rkt, rbt, rvt = [take(512, (4, P)) for _ in range(3)]
        rrhs, ru, rs = take(P), take(P), take(P)
        e1, e2, mid = take(4), take(4), take(4)
        stmp = take(P)
        txw = rl
        sqr = nlb.rearrange("p a b -> p (a b)")[:, 0:JT * T]
        sqo = xi.rearrange("p a b -> p (a b)")[:, 0:JT * T]
        yc = xti.rearrange("p a b -> p (a b)")[:, 0:JT * T]
        rsd = ww.rearrange("p a b -> p (a b)")[:, 0:JT * T]
        rso = lkm.rearrange("p a b -> p (a b)")[:, 0:JT * T]

        top[0] = base
        ht = take(KT * T, (KT, T))
        qa, ka, qb, kb, qc = [take(4 * T, (4, T)) for _ in range(5)]
        kc, qi = take(2 * T, (2, T)), take(2 * T, (2, T))
        ki = take(T)
        va, vb = take(2 * 512, (2, 512)), take(2 * 512, (2, 512))
        vc = take(2 * P, (2, P))
        gt = take(24 * T, (24, T))
        br = take(12 * T, (3, 4, T))
        yy = take(KT * T, (KT, T))
        work0 = top[0]
        zm = take(2 * 384, (2, 384))
        pp = take(2 * 384, (2, 384))
        wgt = take(2 * 384, (2, 384))
        wt = take(2 * 384, (2, 384))
        sg = take(2 * 384, (2, 384))
        rdots = take(4 * 384, (4, 384))
        score = take(384)
        wk = take(384)
        bias_c = take(384)
        rsq = take(T)
        rot_t = take(512)
        nmx, sums, rsum = [take(4, (2, 2)) for _ in range(3)]
        top8 = take(16, (2, 8))
        wi = take(8, (2, 4))
        gcol = take(16, (2, 8))
        fc, fe, fs, fn = [take(T) for _ in range(4)]
        top_attn = top[0]
        top[0] = work0
        sq = take(KT * T, (KT, T))
        assert top[0] <= top_attn
        hff = arena[:, base + KT * T:base + KT * T + 32 * T].rearrange("p (k t) -> p k t", t=T)
        assert KT * T + 32 * T <= work0 - base
        fin = arena[:, base + KT * T:base + KT * T + 2 * D].rearrange("p (m n) -> p m n", m=2)

        setup = Banks(sem, "setup", PLAN_SETUP)
        hg = Banks(sem, "hgrn", PLAN_HGRN, JT)
        lora = Banks(sem, "lora", PLAN_LORA)
        rw = Banks(sem, "rwkv", PLAN_RWKV, JT)
        rd = Banks(sem, "read", PLAN_READ)
        ly = Banks(sem, "layer", PLAN_LAYER, LAYERS)
        en = Banks(sem, "end", PLAN_END)

        s_slot = [sem(f"slot{s}_landed") for s in range(SLOTS)]
        s_used = sem("chunks_used")
        s_const = sem("constants_landed")
        s_in = sem("inputs_landed")
        s_out = sem("out_landed")

        def bank(b, g):
            return psum[:, b.bank(g), :]

        def flip(ap, d):
            v = ap.rearrange("p (s t) -> p s t", t=T)
            return v[:, :, ::-1] if d else v

        def pair(ap, n):
            return seqs(ap[:, bass.ds(n, 1), :].rearrange("p a t -> p (a t)"))

        def flat2_(ap):
            return ap.rearrange("p (u t) -> p u t", t=P)

        def ht_flat(k):
            return ht[:, k, :]

        def seqs(ap):
            return ap.rearrange("p (s t) -> p s t", t=T)

        def use_chunk(pe, n, l=0):
            s = n % SLOTS
            pe.wait_ge(s_slot[s], l * SLOT_PER_LAYER[s] + landed(n))
            return ring[:, s]

        def vars_of():
            return dict(xr=xr, ht=ht)

        N_SMALL = 2 + len(STACK_A) + len(STACK_B) + 6

        block = ctx.enter_context(nc.Block())

        @block.sync
        def _(sp):
            sp.dma_start(const[:, :], a["const"]).then_inc(s_const, 16)
            for n, (w, c0, c1) in enumerate(FIRST):
                if not first:
                    sp.sem_inc(s_slot[n % SLOTS], 16)
                    continue
                if n >= SLOTS:
                    sp.wait_ge(s_used, n - SLOTS + 1)
                sp.dma_start(ring[:, n % SLOTS, :, 0:c1 - c0], rows_of(a[w][0], 0, KT, c0, c1)).then_inc(
                    s_slot[n % SLOTS], 16)

            def chunk(l, i, pieces):
                n = len(FIRST) + i
                sp.wait_ge(s_used, l * LAYER_CHUNKS + n - SLOTS + 1)
                sp.sem_inc(sem("loads_begun"), 1)
                for dst, src in pieces:
                    sp.dma_start(dst, src).then_inc(s_slot[n % SLOTS], 16)

            def slot(i):
                return ring[:, (len(FIRST) + i) % SLOTS]

            def layer_row(w, l, rows, c0, c1, k0=0, k=KT):
                v = w.rearrange("l k n -> (l k) n")
                return v[bass.ds(l * rows + k0 * P, k * P), c0:c1].rearrange("(k p) n -> p k n", p=P)

            if second:
                with sp.Fori(0, LAYERS) as l:
                    for i, pieces in enumerate(LAYER_IN):
                        chunk(l, i, [(slot(i)[:, :, o:o + n], layer_row(a["w_in_2"], l, D, s, s + n))
                                     for o, s, n in pieces])
                    i = N_IN
                    wb = a["w_branch_2"].rearrange("l b k n -> (l b k) n")
                    for b in range(3):
                        src = wb[bass.ds(l * 1536 + b * 512, 512), :].rearrange("(k p) n -> p k n", p=P)
                        chunk(l, i, [(slot(i).rearrange("p k n -> p (k n)").rearrange("p (k n) -> p k n", n=D), src)])
                        i += 1
                    for h in range(2):
                        chunk(l, i, [(slot(i), layer_row(a["w_out_2"], l, D, 512 * h, 512 * h + 512))])
                        i += 1
                    for h in range(8):
                        chunk(l, i, [(slot(i), layer_row(a["w_up_2"], l, D, 512 * h, 512 * h + 512))])
                        i += 1
                    for h in range(2):
                        for q in range(4):
                            chunk(l, i, [(slot(i), layer_row(a["w_down_2"], l, FF, 512 * h, 512 * h + 512, q * KT))])
                            i += 1
            if dump:
                sp.wait_ge(sem("finished"), 1)
                views = dict(vars_of())
                for name in dump:
                    sp.dma_start(a[name], views[name]).then_inc(s_out, 16)
                sp.wait_ge(s_out, 16 * len(dump))
            else:
                for m in range(2):
                    en.wait_emptied(sp, f"fin{m}1")
                    sp.dma_start(out[0, m * P:(m + 1) * P, :], fin[:, m, :]).then_inc(s_out, 16)
                sp.wait_ge(s_out, 32)

        @block.gpsimd
        def _(gp):
            for i, src in enumerate((a["ctx"], a["x"])):
                gp.dma_start(x4[:, 2 * i:2 * i + 2, :], src[0].rearrange("(m p) n -> p m n", p=P)).then_inc(s_in, 16)
            for stack, place in ((STACK_A, stackA), (STACK_B, stackB)):
                r = 0
                for name, n in stack:
                    v = a[name]
                    names = " ".join(f"d{k}" for k in range(len(v.shape)))
                    v = v.rearrange(f"{names} -> ({names})").rearrange("(t p) -> t p", p=P)
                    gp.dma_start(place[r:r + n, :], v).then_inc(s_in, 16)
                    r += n
            gp.dma_start(wup, a["rwkv_w_up"][0].rearrange("d k n -> (d k) n")).then_inc(s_in, 16)
            gp.dma_start(aup, a["rwkv_a_up"][0].rearrange("d k n -> (d k) n")).then_inc(s_in, 16)
            gp.dma_start(pw, a["pool_w"][0].rearrange("(b g) i o -> (g i) b o", g=2)).then_inc(s_in, 16)
            with nc.allow_non_contiguous_dma(reason="sixteen numbers"):
                for r0 in (0, HALF):
                    gp.dma_start(bf[r0:r0 + 8, :], a["b_forget_2"].rearrange("l h -> h l")).then_inc(s_in, 16)
            gp.dma_start(pos_i, a["positions_2"].to_broadcast([P, T])).then_inc(s_in, 16)


        def norm_sum(pe, take_bank, b, g, ready, l):
            pe.wait_ge(sem(ready), l + 1)
            v = take_bank(b, g, l)
            for k in range(KT):
                mm = pe.matmul(v[:, 0:T], cst("ones"), sq[:, k, :], start=k == 0, stop=k == KT - 1)
            mm.then_inc(b.filled, 1)

        def rwkv_tensor(pe, j, d, take_bank, turn):
            blocks = cst("blocks")
            pe.wait_ge(sem(f"r_squared{d}"), j + 1)
            b = take_bank(rw, f"kk{d}", j)
            pe.matmul(b, blocks, rn, start=True, stop=True).then_inc(rw.filled, 1)
            pe.wait_ge(sem(f"r_operands{d}"), j + 1)
            b = take_bank(rw, f"bonus{d}", j)
            pe.matmul(b[:, 0:T], blocks, rn[:, 0:T], start=True, stop=True).then_inc(rw.filled, 1)
            for g, src in (("ktok", km), ("btok", rla), ("vtok", rlv)):
                b = take_bank(rw, f"{g}{d}", j)
                for c in range(4):
                    mm = turn(b[:, c * P:(c + 1) * P], src[:, c * P:(c + 1) * P])
                mm.then_inc(rw.filled, 1)

            def scores(name, left, right, chunks=range(4)):
                for h in range(2):
                    b = take_bank(rw, f"{name}{h}{d}", j)
                    r = slice(h * HALF, (h + 1) * HALF)
                    for i, c in enumerate(chunks):
                        q = (i if right is rlr else c) * P
                        mm = pe.matmul(b[:, i * P:(i + 1) * P], left[r, c * P:(c + 1) * P], right[r, q:q + P], start=True, stop=True)
                    mm.then_inc(rw.filled, 1)

            scores("lbT", rla, pexc)
            scores("lb", pexc, rla)
            scores("lk", km, pexc)
            scores("ak", km, rlr, (2, 3))
            scores("ab", rla, rlr, (2, 3))

            def units(name, left, right, g):
                b = take_bank(rw, name, j)
                for u in range(4):
                    mm = pe.matmul(b[:, u * P:(u + 1) * P], left[:, 4 * g + u, :], right[:, 4 * g + u, :], start=True, stop=True)
                mm.then_inc(rw.filled, 1)

            for l in range(1, 7):
                for g in range(2):
                    rw.wait_emptied(pe, f"x{l - 1}{g}{d}" if l > 1 else f"lbT{g}{d}", j)
                    rw.wait_emptied(pe, f"xt{l - 1}{g}{d}" if l > 1 else f"lb{g}{d}", j)
                    units(f"w{l}{g}{d}", nlb, xi, g)
                for g in range(2):
                    rw.wait_emptied(pe, f"w{l}{g}{d}", j)
                    units(f"x{l}{g}{d}", xti, ww, g)
                    if l < 6:
                        units(f"xt{l}{g}{d}", ww, xti, g)
            rw.wait_emptied(pe, f"vtok{d}", j)
            rw.wait_emptied(pe, f"x61{d}", j)
            for c in range(4):
                if c:
                    rw.wait_emptied(pe, f"s{c - 1}{d}", j)
                else:
                    pe.wait_ge(sem(f"r_state_zero{d}"), j + 1)
                b = take_bank(rw, f"rhs{c}{d}", j)
                pe.matmul(b[:, 0:P], pexc[:, c * P:(c + 1) * P], rs, start=True, stop=False, skip_group_check=True)
                for h in range(2):
                    r = slice(h * HALF, (h + 1) * HALF)
                    mm = pe.matmul(b[:, r], lkm[:, 4 * h + c, :], rvt[:, c, r], start=False, stop=h == 1, skip_group_check=True)
                mm.then_inc(rw.filled, 1)
                rw.wait_emptied(pe, f"rhs{c}{d}", j)
                b = take_bank(rw, f"u{c}{d}", j)
                for h in range(2):
                    r = slice(h * HALF, (h + 1) * HALF)
                    mm = pe.matmul(b[:, r], xi[:, 4 * h + c, :], rrhs[:, r], start=True, stop=True)
                mm.then_inc(rw.filled, 1)
                rw.wait_emptied(pe, f"u{c}{d}", j)
                if c >= 2:
                    b = take_bank(rw, f"y{c}{d}", j)
                    q = c - 2
                    pe.matmul(b[:, 0:P], rs, rlr[:, q * P:(q + 1) * P], start=True, stop=False, skip_group_check=True)
                    for h in range(2):
                        r = slice(h * HALF, (h + 1) * HALF)
                        pe.matmul(b[r, 0:P], rvt[:, c, r], akm[:, 2 * h + q, :], start=False, stop=False, skip_group_check=True)
                        mm = pe.matmul(b[r, 0:P], ru[:, r], abm[:, 2 * h + q, :], start=False, stop=h == 1, skip_group_check=True)
                    mm.then_inc(rw.filled, 1)
                if c < 3:
                    b = take_bank(rw, f"s{c}{d}", j)
                    pe.matmul(b[:, 0:P], rkt[:, c, :], rvt[:, c, :], start=True, stop=False)
                    pe.matmul(b[:, 0:P], rbt[:, c, :], ru, start=False, stop=True).then_inc(rw.filled, 1)

        def layer_tensor(pe, l, take_bank, turn, used):
            ident = cst("ident")
            n0 = len(FIRST)
            norm_sum(pe, take_bank, ly, "ss1", "squares1", l)
            pe.wait_ge(sem("h1_ready"), l + 1)

            def tiles(g, w, cs, n=2, src=ht, k0=0, ks=KT):
                b = take_bank(ly, g, l)
                for i, c in enumerate(cs):
                    for k in range(ks):
                        mm = pe.matmul(b[:, i * T:(i + 1) * T], w[:, k, c:c + P], src[:, k0 + k, :], start=k == 0, stop=k == ks - 1)
                mm.then_inc(ly.filled, 1)

            def tokens(g, w, c, n, m=None):
                b = take_bank(ly, g, l)
                for i, mm_ in enumerate((0, 1) if m is None else (m,)):
                    for k in range(KT):
                        mm = pe.matmul(b[:, i * n:(i + 1) * n], ht[:, k, mm_ * P:(mm_ + 1) * P], w[:, k, c:c + n],
                                       start=k == 0, stop=k == KT - 1)
                mm.then_inc(ly.filled, 1)

            w = use_chunk(pe, n0, l)
            tiles("qc0", w, (0, P))
            tiles("qc1", w, (2 * P, 3 * P))
            used()
            w = use_chunk(pe, n0 + 1, l)
            tiles("kc", w, (0, P))
            tiles("qi", w, (2 * P, 3 * P))
            used()
            w = use_chunk(pe, n0 + 2, l)
            tokens("vc", w, 0, P)
            tiles("ki", w, (P,))
            tokens("wi", w, 2 * P, 4)
            b = take_bank(ly, "fl", l)
            for r0 in (0, HALF):
                for k in range(KT):
                    mm = pe.matmul(b[r0:r0 + 8, 0:T], w[:, k, 260:268], ht[:, k, :], start=k == 0, stop=k == KT - 1)
            mm.then_inc(ly.filled, 1)
            used()
            for g, of, src in (("rqc0", "qc0", qc[:, 0:2]), ("rqc1", "qc1", qc[:, 2:4]), ("rkc", "kc", kc), ("rqi", "qi", qi)):
                ly.wait_emptied(pe, of, l)
                b = take_bank(ly, g, l)
                pe.matmul(b, cst("rot"), src.rearrange("p a t -> p (a t)"), start=True, stop=True).then_inc(ly.filled, 1)
            ly.wait_emptied(pe, "ki", l)
            b = take_bank(ly, "rki", l)
            pe.matmul(b[:, 0:T], cst("rot"), ki, start=True, stop=True).then_inc(ly.filled, 1)
            pe.wait_ge(sem("roped"), l + 1)
            for n, (m, hs) in enumerate(((0, (0, 2)), (0, (1, 3)), (1, (0, 2)), (1, (1, 3)))):
                b = take_bank(ly, f"dot{n}", l)
                width = P if m == 0 else T
                for i, h in enumerate(hs):
                    r = slice(h % 2 * HALF, h % 2 * HALF + HALF)
                    mm = pe.matmul(b[:, i * width:(i + 1) * width], qi[r, h // 2, m * P:(m + 1) * P], ki[r, 0:width],
                                   start=True, stop=True)
                mm.then_inc(ly.filled, 1)
            for i, x in enumerate(("qa", "ka", "va", "qb", "kb", "vb")):
                w = use_chunk(pe, n0 + 3 + i, l)
                for n in range(2):
                    if x[0] == "v":
                        tokens(f"{x}{n}", w, 0, 512, n)
                    else:
                        tiles(f"{x}{n}", w, (2 * n * P, (2 * n + 1) * P))
                used()

            for i in range(len(STEPS) + 1):
                if i < len(STEPS):
                    kind, h = STEPS[i]
                    if i == 0:
                        ly.wait_emptied(pe, "vb1", l)
                        pe.wait_ge(sem("forget_ready"), l + 1)
                    r = slice(h % 2 * HALF, h % 2 * HALF + HALF)
                    q = {"A": qa, "B": qb, "C": qc}[kind][r, h // 2]
                    kk = kc[r, h // 4] if kind == "C" else {"A": ka, "B": kb}[kind][r, h // 2]
                    b = take_bank(ly, f"z{i}", l)
                    for m, o, width in ((0, 0, P), (1, P, T)):
                        z = b[:, o:o + width]
                        mm = pe.matmul(z, q[:, m * P:(m + 1) * P], kk[:, 0:width], start=True, stop=kind != "B")
                        if kind == "B":
                            pick = ident[r, r.start + h:r.start + h + 1]
                            pe.matmul(z, fc[r, m * P:(m + 1) * P], pick.to_broadcast([HALF, width]), start=False, stop=False)
                            mm = pe.matmul(z, pick.to_broadcast([HALF, P]), fn[r, 0:width], start=False, stop=True)
                    mm.then_inc(ly.filled, 1)
                    if i % 4 == 0:
                        w = use_chunk(pe, n0 + 9 + i // 4, l)
                    tiles(f"gl{i}", w, (i % 4 * P,))
                    if i % 4 == 3:
                        used()
                if i:
                    kind, h = STEPS[i - 1]
                    s = (i - 1) % 2
                    pe.wait_ge(sem("weights_ready"), l * len(STEPS) + i)
                    b = take_bank(ly, f"wT{i - 1}", l)
                    for n in range(3):
                        mm = turn(b[:, n * P:(n + 1) * P], wgt[:, s, n * P:(n + 1) * P])
                    mm.then_inc(ly.filled, 1)
                    ly.wait_emptied(pe, f"wT{i - 1}", l)
                    b = take_bank(ly, f"o{i - 1}", l)
                    r = slice(h % 2 * HALF, h % 2 * HALF + HALF)
                    if kind == "C":
                        v = [vc[:, m, h // 4 * HALF:h // 4 * HALF + HALF] for m in range(2)]
                    else:
                        v = [(va if kind == "A" else vb)[:, m, h * HALF:(h + 1) * HALF] for m in range(2)]
                    pe.matmul(b[r, 0:T], v[0], wt[:, s, 0:T], start=True, stop=False, skip_group_check=True)
                    pe.matmul(b[r, P:T], v[1], wt[:, s, T:T + P], start=False, stop=True, skip_group_check=True).then_inc(ly.filled, 1)

            ly.wait_emptied(pe, f"o{len(STEPS) - 1}", l)
            for b_ in range(3):
                w = use_chunk(pe, n0 + N_IN + b_, l).rearrange("p k n -> p (k n)").rearrange("p (k n) -> p k n", n=D)
                for n in range(4):
                    tiles(f"br{b_}{n}", w, (2 * n * P, (2 * n + 1) * P), src=br[:, b_], ks=4)
                used()
            ly.wait_emptied(pe, "br23", l)
            for h in range(2):
                w = use_chunk(pe, n0 + N_IN + 3 + h, l)
                for n in range(2):
                    tiles(f"out{2 * h + n}", w, (2 * n * P, (2 * n + 1) * P), src=yy)
                used()
            norm_sum(pe, take_bank, ly, "ss2", "squares2", l)
            pe.wait_ge(sem("h2_ready"), l + 1)
            for c in range(8):
                w = use_chunk(pe, n0 + N_IN + 5 + c, l)
                for n in range(2):
                    tiles(f"up{2 * c + n}", w, (2 * n * P, (2 * n + 1) * P))
                used()
            pe.wait_ge(sem("hidden_ready"), l + 1)
            for h in range(2):
                bs = [take_bank(ly, f"dn{4 * h + t}", l) for t in range(4)]
                for c in range(4):
                    w = use_chunk(pe, n0 + N_IN + 13 + 4 * h + c, l)
                    for t in range(4):
                        for k in range(KT):
                            mm = pe.matmul(bs[t][:, 0:T], w[:, k, t * P:(t + 1) * P], hff[:, c * KT + k, :],
                                           start=c == 0 and k == 0, stop=c == 3 and k == KT - 1)
                        if c == 3:
                            mm.then_inc(ly.filled, 1)
                    used()

        @block.tensor
        def _(pe):
            ident, ones, blocks = cst("ident"), cst("ones"), cst("blocks")

            def used():
                pe.drain().then_inc(s_used, 1)

            def take_bank(b, g, it=0):
                b.wait_free(pe, g, it)
                return bank(b, g)

            def turn(dst, src):
                n = src.shape[0]
                return pe.transpose(dst, src, ident[0:n, 0:n])

            pe.wait_ge(s_const, 16)
            pe.wait_ge(s_in, 16 * N_SMALL)
            if True:
                for g, st, n in (("colsA", stackA, ROWS_A), ("colsB", stackB, ROWS_B)):
                    turn(take_bank(setup, g)[:, 0:n], st[0:n, :]).then_inc(setup.filled, 1)
                for g in range(4):
                    b = take_bank(setup, f"xr{g}")
                    for k in range(2):
                        for m in range(2):
                            o = k * T + m * P
                            mm = turn(b[:, o:o + P], x4[:, 2 + m, (2 * g + k) * P:(2 * g + k + 1) * P])
                    mm.then_inc(setup.filled, 1)
            if first:
                pe.wait_ge(sem("silu_ready"), 1)
                for n in range(6):
                    w = use_chunk(pe, n)
                    b = take_bank(setup, f"mod{n}")
                    for k in range(KT):
                        mm = pe.matmul(b[0:2, :], silu_c[:, k, :], w[:, k, :], start=k == 0, stop=k == KT - 1)
                    mm.then_inc(setup.filled, 1)
                    used()
                b = take_bank(setup, "modT")
                setup.wait_emptied(pe, "mod5")
                for t in range(24):
                    mm = turn(b[:, 2 * t:2 * t + 2], mrow[0:2, t * P:(t + 1) * P])
                mm.then_inc(setup.filled, 1)
                pe.wait_ge(sem("tokens_normalised"), 1)
                for k in range(KT):
                    b = take_bank(setup, f"xt{k}")
                    for m in range(4):
                        mm = turn(b[:, m * P:(m + 1) * P], x4[:, m, k * P:(k + 1) * P])
                    mm.then_inc(setup.filled, 1)
                setup.wait_emptied(pe, f"xt{KT - 1}")

                def project(g, w, c0, n0=0, n1=512):
                    b = take_bank(setup, g)
                    for k in range(KT):
                        mm = pe.matmul(b[:, 0:n1 - n0], w[:, k, c0:c0 + P], xt[:, k, n0:n1], start=k == 0, stop=k == KT - 1)
                    return mm

                for chunk in range(3):
                    w = use_chunk(pe, 6 + chunk)
                    for t in range(4):
                        project(f"fh{4 * chunk + t}", w, t * P).then_inc(setup.filled, 1)
                    used()
                for chunk in range(3):
                    w = use_chunk(pe, 9 + chunk)
                    for t in range(4 if chunk < 2 else 3):
                        project(f"u{4 * chunk + t}", w, t * P).then_inc(setup.filled, 1)
                    used()
                w = use_chunk(pe, 12)
                for m in range(2):
                    b = take_bank(setup, f"pv{m}")
                    for k in range(KT):
                        mm = pe.matmul(b[:, 0:T], xt[:, k, T + m * P:T + (m + 1) * P], w[:, k, 0:T], start=k == 0, stop=k == KT - 1)
                    mm.then_inc(setup.filled, 1)
                used()
                for chunk in range(2):
                    w = use_chunk(pe, 13 + chunk)
                    for n in range(2):
                        b = take_bank(setup, f"g{2 * chunk + n}")
                        for t in range(2):
                            for k in range(KT):
                                mm = pe.matmul(b[:, t * T:(t + 1) * T], w[:, k, (2 * n + t) * P:(2 * n + t + 1) * P],
                                               xt[:, k, T:2 * T], start=k == 0, stop=k == KT - 1)
                        mm.then_inc(setup.filled, 1)
                    used()
                setup.wait_emptied(pe, "pv1")
                for n in range(2):
                    b = take_bank(setup, f"pool{n}")
                    for gg in range(2):
                        g = 2 * n + gg
                        for m in range(2):
                            mm = pe.matmul(b[gg * HALF:(gg + 1) * HALF, m * P:(m + 1) * P], pv[:, m, g * HALF:(g + 1) * HALF],
                                           cst(f"pool{g}"), start=True, stop=True)
                    mm.then_inc(setup.filled, 1)
                for n in range(2):
                    b = take_bank(setup, f"pmix{n}")
                    setup.wait_emptied(pe, f"pool{n}")
                    for gg in range(2):
                        h = slice(gg * HALF, (gg + 1) * HALF)
                        mm = pe.matmul(b[h, 0:T], pw[h, n, :], pooled[h, n, :], start=True, stop=True)
                    mm.then_inc(setup.filled, 1)
                setup.wait_all(pe)

                hg.start(pe, "P")
                with pe.Fori(0, JT) as j:
                    for d in range(2):
                        pe.wait_ge(sem(f"h_loaded{d}"), j + 1)
                        b = take_bank(hg, f"itok{d}", j)
                        for c in range(4):
                            mm = turn(b[:, c * P:(c + 1) * P], li[:, c * P:(c + 1) * P])
                        mm.then_inc(hg.filled, 1)

                        def pair_scores(g, keys, queries):
                            for h in range(2):
                                b = take_bank(hg, f"{g}{h}{d}", j)
                                r = slice(h * HALF, (h + 1) * HALF)
                                for m in range(2):
                                    mm = pe.matmul(b[:, m * P:(m + 1) * P], keys[r, m * P:(m + 1) * P],
                                                   queries[r, m * P:(m + 1) * P], start=True, stop=True)
                                mm.then_inc(hg.filled, 1)

                        pair_scores("diag", lk[:, T:2 * T], lq)
                        for l in range(7):
                            pe.wait_ge(sem("h_level_ready"), j * 18 + d * 9 + l + 1)
                            pair_scores(f"lev{l}", kl[:, l % 2], ql[:, l % 2])
                        pe.wait_ge(sem("h_level_ready"), j * 18 + d * 9 + 8)
                        for h in range(2):
                            b = take_bank(hg, f"cross{h}{d}", j)
                            r = slice(h * HALF, (h + 1) * HALF)
                            pe.matmul(b[:, 0:P], kl[r, 1, 0:P], ql[r, 1, P:2 * P], start=True, stop=True).then_inc(hg.filled, 1)
                        pe.wait_ge(sem("h_level_ready"), j * 18 + d * 9 + 9)
                        b = take_bank(hg, f"ktok{d}", j)
                        for c in range(2):
                            mm = turn(b[:, c * P:(c + 1) * P], kl[:, 0, c * P:(c + 1) * P])
                        mm.then_inc(hg.filled, 1)
                        hg.wait_emptied(pe, f"ktok{d}", j)
                        b = take_bank(hg, f"state{d}", j)
                        for c in range(2):
                            mm = pe.matmul(b[:, 0:P], ktok[:, c, :], itok[:, c, :], start=c == 0, stop=c == 1)
                        mm.then_inc(hg.filled, 1)
                        hg.wait_emptied(pe, f"cross1{d}", j)
                        hg.wait_emptied(pe, f"state{d}", j)
                        b = take_bank(hg, f"o{d}", j)
                        pe.matmul(b[:, 0:T], hstate, ql[:, 0], start=True, stop=False, skip_group_check=True)
                        for h in range(2):
                            r = slice(h * HALF, (h + 1) * HALF)
                            pe.matmul(b[r, 0:P], itok[:, 2, r], acc[:, 2 * h, :], start=False, stop=False, skip_group_check=True)
                            pe.matmul(b[r, P:2 * P], itok[:, 2, r], cross[:, h, :], start=False, stop=False, skip_group_check=True)
                            mm = pe.matmul(b[r, P:2 * P], itok[:, 3, r], acc[:, 2 * h + 1, :], start=False, stop=h == 1,
                                           skip_group_check=True)
                        mm.then_inc(hg.filled, 1)
                hg.wait_all(pe)

                pe.wait_ge(sem("tanh_ready"), 1)
                for d in range(2):
                    r = slice(d * HALF, (d + 1) * HALF)
                    for jj in range(JT):
                        for x, w, src in (("w", wup, txw), ("a", aup, us[:, 10, :])):
                            b = take_bank(lora, f"{x}{d}{jj}")
                            pe.matmul(b, w[r, jj * P:(jj + 1) * P], src[r, :], start=True, stop=True).then_inc(lora.filled, 1)
                lora.wait_all(pe)

                rw.start(pe, "P")
                with pe.Fori(0, JT) as j:
                    for d in range(2):
                        rwkv_tensor(pe, j, d, take_bank, turn)
                rw.wait_all(pe)

                ys, os_ = [(yacc, 0, 2), (yacc, 2, 1)], [(oacc, 0, 2), (oacc, 2, 1)]
                for n, (src, j0, k) in enumerate(ys):
                    b = take_bank(rd, f"ysum{n}")
                    pe.matmul(b[:, 0:k * T], blocks, src[:, j0:j0 + k, :].rearrange("p j t -> p (j t)"),
                              start=True, stop=True).then_inc(rd.filled, 1)
                pe.wait_ge(sem("y_squared"), 1)
                for n, k in ((0, 2), (1, 1)):
                    b = take_bank(rd, f"yvar{n}")
                    pe.matmul(b[:, 0:k * T], blocks, sqr[:, 2 * n * T:(2 * n + k) * T], start=True, stop=True).then_inc(rd.filled, 1)
                for n, k in ((0, 2), (1, 1)):
                    b = take_bank(rd, f"osq{n}")
                    pe.matmul(b[:, 0:k * T], blocks, sqo[:, 2 * n * T:(2 * n + k) * T], start=True, stop=True).then_inc(rd.filled, 1)
                pe.wait_ge(sem("mix_ready"), 1)
                for chunk in range(2):
                    w = use_chunk(pe, 15 + chunk)
                    for t in range(4):
                        b = take_bank(rd, f"wo{4 * chunk + t}")
                        for k in range(KT):
                            mm = pe.matmul(b[:, 0:T], w[:, k, t * P:(t + 1) * P], mix[:, k, :], start=k == 0, stop=k == KT - 1)
                        mm.then_inc(rd.filled, 1)
                    used()
                rd.wait_emptied(pe, f"wo{KT - 1}")
                b = take_bank(rd, "lnsum")
                for k in range(KT):
                    mm = pe.matmul(b[:, 0:T], ones, xr[:, k, :], start=k == 0, stop=k == KT - 1)
                mm.then_inc(rd.filled, 1)
                pe.wait_ge(sem("ln_squared"), 1)
                b = take_bank(rd, "lnvar")
                for k in range(KT):
                    mm = pe.matmul(b[:, 0:T], ones, mix[:, k, :], start=k == 0, stop=k == KT - 1)
                mm.then_inc(rd.filled, 1)
                rd.wait_all(pe)
            else:
                pe.sem_inc(s_used, len(FIRST))
                setup.wait_emptied(pe, "xr3") if first else pe.wait_ge(setup.emptied["D"], 6)

            if second:
                ly.start(pe, "P")
                with pe.Fori(0, LAYERS) as l:
                    layer_tensor(pe, l, take_bank, turn, used)
                ly.wait_all(pe)
                norm_sum(pe, take_bank, en, "ssf", "squares_f", 0)
                pe.wait_ge(sem("final_ready"), 1)
                for m in range(2):
                    for n in range(2):
                        b = take_bank(en, f"fin{m}{n}")
                        for k in range(4):
                            mm = turn(b[:, k * P:(k + 1) * P], ht[:, 4 * n + k, m * P:(m + 1) * P])
                        mm.then_inc(en.filled, 1)

        def norm_scalar(act, b, g, squares, l, done, emptied):
            act.activation(sq, xr, ACT.Square)
            done(squares)
            b.wait_filled(act, g, l)
            emptied(b, act.activation(rsq, bank(b, g)[:, 0:T], ACT.Sqrt, bias=eps(NORM_EPS), scale=1.0 / D))

        def layer_scalar(act, l, copy, done, emptied):
            def out_of(g, dst, scale=1.0, n=2):
                ly.wait_filled(act, g, l)
                b = bank(ly, g)
                src = b[:, 0:n * T]
                emptied(ly, copy(dst, src.rearrange("p (a t) -> p a t", a=n) if n == 2 else src, scale))

            if True:
                ly_prev = "dn7"
                ly.wait_emptied(act, ly_prev, l, before=1)
            norm_scalar(act, ly, "ss1", "squares1", l, done, emptied)
            out_of("qc0", qc[:, 0:2])
            out_of("qc1", qc[:, 2:4])
            out_of("kc", kc)
            out_of("qi", qi)
            ly.wait_filled(act, "vc", l)
            emptied(ly, copy(vc, bank(ly, "vc")[:, 0:T].rearrange("p (m n) -> p m n", m=2)))
            out_of("ki", ki, n=1)
            ly.wait_filled(act, "fl", l)
            act.wait_ge(sem("bias_column_ready"), l + 1)
            for r0 in (0, HALF):
                f8 = slice(r0, r0 + 8)
                ins = act.activation(fs[f8], bank(ly, "fl")[f8, 0:T], ACT.Identity, bias=bcol[f8])
            emptied(ly, ins)
            act.drain()
            for f8 in (slice(0, 8), slice(HALF, HALF + 8)):
                act.activation(fe[f8], fs[f8], ACT.Abs)
                act.drain()
                act.activation(fe[f8], fe[f8], ACT.Exp, scale=-1.0)
                act.drain()
                act.activation(fe[f8], fe[f8], ACT.Ln, bias=one_[f8])
            done("forget_logs")
            for n, (o, par, width) in enumerate(((0, 0, P), (0, 1, P), (P, 0, T), (P, 1, T))):
                ly.wait_filled(act, f"dot{n}", l)
                b = bank(ly, f"dot{n}")[:, 0:2 * width].rearrange("p (h s) -> p h s", s=width)
                emptied(ly, act.activation(rdots[:, par::2, o:o + width], b, ACT.Relu, scale=0.125))
            done("dots_ready")
            for x, dst, scale in (("qa", qa, 1.0), ("ka", ka, 1.0), ("va", va, 1.0), ("qb", qb, 0.125), ("kb", kb, 1.0), ("vb", vb, 1.0)):
                for n in range(2):
                    if x[0] == "v":
                        ly.wait_filled(act, f"{x}{n}", l)
                        emptied(ly, copy(dst[:, n, :], bank(ly, f"{x}{n}")))
                    else:
                        out_of(f"{x}{n}", dst[:, 2 * n:2 * n + 2], scale)

            def values_out(i):
                kind, h = STEPS[i]
                ly.wait_filled(act, f"wT{i}", l)
                emptied(ly, copy(wt[:, i % 2, :], bank(ly, f"wT{i}")[:, 0:384]))
                ly.wait_filled(act, f"o{i}", l)
                r = slice(h % 2 * HALF, h % 2 * HALF + HALF)
                emptied(ly, copy(br[r, "ABC".index(kind), h // 2, :], bank(ly, f"o{i}")[r, 0:T]))

            for i in range(len(STEPS) + 1):
                if i < len(STEPS):
                    kind, h = STEPS[i]
                    s = i % 2
                    if kind == "A":
                        ly.wait_filled(act, f"z{i}", l)
                        if i >= 2:
                            act.wait_ge(sem("weights_ready"), l * len(STEPS) + i - 1)
                        b = bank(ly, f"z{i}")[:, 0:384]
                        act.activation(pp[:, s, :], b, ACT.Sigmoid, scale=-0.125)
                        emptied(ly, act.activation(sg[:, s, :], b, ACT.Sigmoid, scale=0.125))
                    else:
                        act.wait_ge(sem("scores_ready"), l * 16 + (i + 1 if kind == "B" else i - 7))
                        if i >= 2:
                            act.wait_ge(sem("weights_ready"), l * len(STEPS) + i - 1)
                        act.activation(pp[:, s, 0:P], zm[:, s, 0:P], ACT.Exp, bias=nmx[:, s, 0:1], accum_out=sums[:, s, 0:1])
                        act.activation(pp[:, s, P:384], zm[:, s, P:384], ACT.Exp, bias=nmx[:, s, 1:2], accum_out=sums[:, s, 1:2])
                        done("exps_ready")
                    ly.wait_filled(act, f"gl{i}", l)
                    emptied(ly, act.activation(gt[:, i, :], bank(ly, f"gl{i}")[:, 0:T], ACT.Tanh, scale=0.5))
                if i:
                    values_out(i - 1)
            act.wait_ge(sem("attended"), l + 1)
            norm_scalar(act, ly, "ss2", "squares2", l, done, emptied)
            for n in range(16):
                ly.wait_filled(act, f"up{n}", l)
                emptied(ly, act.activation(hff[:, 2 * n:2 * n + 2, :], bank(ly, f"up{n}").rearrange("p (a t) -> p a t", a=2), ACT.Relu))

        @block.scalar
        def _(act):
            def copy(dst, src, scale=1.0):
                return act.activation(dst, src, ACT.Copy, scale=scale)

            def done(name):
                act.drain().then_inc(sem(name), 1)

            def emptied(b, ins):
                ins.then_inc(b.emptied["A"], 1)

            act.wait_ge(sem("angles_ready"), 1)
            act.activation(sin, ht_flat(0), ACT.Sin)
            act.activation(cos, ht_flat(1), ACT.Sin)
            done("rotary_ready")
            if first:
                act.wait_ge(sem("cols_ready"), 1)
                act.activation(silu_c[:, :, 0:1], cols[:, COL["c"]:COL["c"] + KT].unsqueeze(2), ACT.Silu)
                act.activation(silu_c[:, :, 1:2], cols[:, COL["c_ctx"]:COL["c_ctx"] + KT].unsqueeze(2), ACT.Silu)
                done("silu_ready")
                act.wait_ge(sem("lb_shifted"), 1)
                act.activation(lbw, lbw, ACT.Exp)
                done("lb_exp")
                act.wait_ge(sem("stats_ready"), 1)
                act.activation(rstd4.unsqueeze(2), mv[:, :, 1:2], ACT.Sqrt, bias=eps(LN_EPS))
                done("std_ready")
                for n in range(6):
                    setup.wait_filled(act, f"mod{n}")
                    emptied(setup, copy(mrow[0:2, 512 * n:512 * n + 512], bank(setup, f"mod{n}")[0:2, :]))
                act.wait_ge(sem("modulation_ready"), 1)
                for k in range(KT):
                    setup.wait_filled(act, f"xt{k}")
                    b = bank(setup, f"xt{k}")
                    for s in range(2):
                        ins = act.activation(xt[:, k, s * T:(s + 1) * T], b[:, s * T:(s + 1) * T], ACT.Identity,
                                             bias=modc[:, k, 1 - s:2 - s], scale=modc[:, KT + k, 1 - s:2 - s])
                    emptied(setup, ins)
                for t in range(12):
                    setup.wait_filled(act, f"fh{t}")
                    b = bank(setup, f"fh{t}")
                    if t < 3:
                        ins = copy(hq[:, t, :], b[:, T:2 * T])
                    elif t < 6:
                        ins = copy(hi[:, t - 3, :], b)
                    else:
                        act.activation(hf[:, t - 6, :], b, ACT.Sigmoid)
                        ins = act.activation(hk[:, t - 6, :], b, ACT.Sigmoid, scale=-1.0)
                    emptied(setup, ins)
                for n in range(4):
                    setup.wait_filled(act, f"g{n}")
                    emptied(setup, act.activation(mix[:, 2 * n:2 * n + 2, :], bank(setup, f"g{n}").rearrange("p (a t) -> p a t", a=2), ACT.Silu))
                for n in range(2):
                    setup.wait_filled(act, f"pool{n}")
                    emptied(setup, copy(pooled[:, n, :], bank(setup, f"pool{n}")[:, 0:T]))

                act.wait_ge(sem("gates_bounded"), 1)
                setup.wait_all(act)
                hg.start(act, "A")
                with act.Fori(0, JT) as j:
                    for d in range(2):
                        if d:
                            hg.wait_filled(act, "o0", j)
                        else:
                            hg.wait_filled(act, "o1", j, before=1)
                        act.sem_inc(sem("turns_begun"), 1)
                        copy(flip(lk, d), pair(hk, 3 * d + j))
                        copy(flip(pi, d), pair(hf, 3 * d + j))
                        copy(flip(li, d), pair(hi, j))
                        copy(flip(lq, d), pair(hq, j))
                        done(f"h_loaded{d}")
                        hg.wait_filled(act, f"itok{d}", j)
                        emptied(hg, copy(itok.rearrange("p c t -> p (c t)"), bank(hg, f"itok{d}")))
                        for h in range(2):
                            hg.wait_filled(act, f"cross{h}{d}", j)
                            emptied(hg, copy(cross[:, h, :], bank(hg, f"cross{h}{d}")[:, 0:P]))
                        hg.wait_filled(act, f"ktok{d}", j)
                        emptied(hg, copy(ktok.rearrange("p c t -> p (c t)"), bank(hg, f"ktok{d}")[:, 0:2 * P]))

                hg.wait_all(act)
                act.wait_ge(sem("shifted"), 1)
                act.activation(txw, us[:, 9, :], ACT.Tanh)
                done("tanh_ready")
                for d in range(2):
                    for jj in range(JT):
                        for x, kind, name in (("w", 0, "rwkv_w0"), ("a", 1, "rwkv_a0")):
                            lora.wait_filled(act, f"{x}{d}{jj}")
                            emptied(lora, act.activation(flip(sa[:, kind, 3 * d + jj, :], d), seqs(bank(lora, f"{x}{d}{jj}")),
                                                         ACT.Sigmoid, bias=col(name, 3 * d + jj)))
                act.drain()
                rw.start(act, "A")
                with act.Fori(0, JT) as j:
                    for d in range(2):
                        if d:
                            rw.wait_filled(act, "y30", j)
                        else:
                            rw.wait_filled(act, "y31", j, before=1)
                        act.wait_ge(sem(f"r_columns{d}"), j + 1)
                        act.sem_inc(sem("turns_begun"), 1)
                        copy(flip(rlk, d), pair(us, j + 3))
                        copy(flip(rlv, d), pair(us, j + 6))
                        copy(seqs(rsw), pair(sa[:, 0], 3 * d + j))
                        copy(seqs(rla), pair(sa[:, 1], 3 * d + j))
                        copy(flip(rlr, d), pair(us[:, :, T:2 * T], j))
                        done(f"r_loaded{d}")
                        act.activation(rn, rlk, ACT.Square, scale=pc[:, 0:1])
                        done(f"r_squared{d}")
                        rw.wait_filled(act, f"kk{d}", j)
                        emptied(rw, act.activation(rn, bank(rw, f"kk{d}"), ACT.Ln, bias=eps(1e-12)))
                        act.drain()
                        act.activation(rn, rn, ACT.Exp, scale=-0.5)
                        done(f"r_norm{d}")
                        act.wait_ge(sem(f"r_cumulated{d}"), j + 1)
                        act.activation(pinc, rl, ACT.Exp, scale=-DECAY)
                        act.activation(pinv, rl, ACT.Exp, scale=DECAY)
                        act.activation(pexc, rsw, ACT.Exp, scale=-DECAY)
                        act.activation(e2, mid, ACT.Exp, scale=-DECAY)
                        done(f"r_decays{d}")
                        for g, dst in (("ktok", rkt), ("btok", rbt), ("vtok", rvt)):
                            rw.wait_filled(act, f"{g}{d}", j)
                            emptied(rw, copy(dst.rearrange("p c t -> p (c t)"), bank(rw, f"{g}{d}")))
                        for l in range(1, 7):
                            for g in range(2):
                                rw.wait_filled(act, f"w{l}{g}{d}", j)
                                emptied(rw, copy(ww[:, 4 * g:4 * g + 4, :], bank(rw, f"w{l}{g}{d}").rearrange("p (u t) -> p u t", u=4)))
                        for c in range(4):
                            rw.wait_filled(act, f"rhs{c}{d}", j)
                            emptied(rw, copy(rrhs, bank(rw, f"rhs{c}{d}")[:, 0:P]))
                            rw.wait_filled(act, f"u{c}{d}", j)
                            emptied(rw, copy(ru, bank(rw, f"u{c}{d}")[:, 0:P]))

                rw.wait_all(act)
                act.wait_ge(sem("y_centred"), 1)
                act.activation(sqr, yc, ACT.Square)
                act.activation(sqo, oacc.rearrange("p j t -> p (j t)"), ACT.Square)
                done("y_squared")
                for x, dst, e in (("yvar", rsd, GN_EPS), ("osq", rso, RMS_EPS)):
                    for n, k in ((0, 2), (1, 1)):
                        rd.wait_filled(act, f"{x}{n}")
                        emptied(rd, act.activation(dst[:, 2 * n * T:(2 * n + k) * T], bank(rd, f"{x}{n}")[:, 0:k * T], ACT.Ln,
                                                   bias=eps(e), scale=1.0 / HALF))
                act.drain()
                act.activation(rsd, rsd, ACT.Exp, scale=-0.5)
                act.activation(rso, rso, ACT.Exp, scale=-0.5)
                done("y_scales")
                act.wait_ge(sem("ln_centred"), 1)
                act.activation(mix, xr, ACT.Square)
                done("ln_squared")
                rd.wait_filled(act, "lnvar")
                emptied(rd, act.activation(rl[:, 0:T], bank(rd, "lnvar")[:, 0:T], ACT.Sqrt, bias=eps(LN_EPS), scale=1.0 / D))

            if second:
                act.wait_ge(sem("residual_ready"), 1)
                ly.start(act, "A")
                with act.Fori(0, LAYERS) as l:
                    layer_scalar(act, l, copy, done, emptied)
                act.wait_ge(sem("layers_done"), LAYERS)
                norm_scalar(act, en, "ssf", "squares_f", 0, done, emptied)
                for m in range(2):
                    for n in range(2):
                        en.wait_filled(act, f"fin{m}{n}")
                        emptied(en, copy(fin[:, m, n * 512:(n + 1) * 512], bank(en, f"fin{m}{n}")))

        def normed(dve, gain, fence):
            dve.reciprocal(rsq, rsq)
            fence()
            for k in range(KT):
                dve.scalar_tensor_tensor(ht[:, k, :], xr[:, k, :], gain[:, k:k + 1], rsq, ALU.mult, ALU.mult)

        def first_vector(dve, done, emptied, bc, fence, held):
            lg = cols[:, COL["hgrn_lb_logits"]:COL["hgrn_lb_logits"] + 6]
            dve.tensor_tensor(lbw, lg, lg, ALU.subtract)
            done("lb_shifted")
            for i in range(4):
                for h in range(2):
                    dve.bn_stats(stats[:, i, h, :], x4[:, i, h * 512:(h + 1) * 512])
            fence()
            for i in range(4):
                dve.bn_aggr(mv[:, i, :], stats[:, i].rearrange("p a b -> p (a b)"))
            done("stats_ready")
            dve.wait_ge(sem("lb_exp"), 1)
            dve.reciprocal(omlb, lbw)
            fence()
            dve.tensor_tensor(lbw, lbw, omlb, ALU.mult)
            fence()
            dve.tensor_tensor(lbw, lbw, lbw, ALU.subtract)
            fence()
            dve.tensor_scalar(lbw, lbw, 0.0, None, ALU.max)
            fence()
            dve.tensor_scalar(omlb, lbw, -1.0, 1.0, ALU.mult, ALU.add)
            dve.wait_ge(sem("std_ready"), 1)
            dve.reciprocal(rstd4, rstd4)
            fence()
            for i in range(4):
                dve.tensor_scalar(x4[:, i, :], x4[:, i, :], mv[:, i, 0:1], rstd4[:, i:i + 1], ALU.subtract, ALU.mult)
            done("tokens_normalised")
            setup.wait_filled(dve, "modT")
            mb = cols[:, COL["mod_b"]:COL["mod_b"] + 24]
            emptied(setup, dve.tensor_tensor(modc, bank(setup, "modT")[:, 0:48].rearrange("p (a b) -> p a b", b=2),
                                             mb.unsqueeze(2).to_broadcast([P, 24, 2]), ALU.add))
            fence()
            dve.tensor_scalar(modc[:, KT:2 * KT, :], modc[:, KT:2 * KT, :], 1.0, None, ALU.add)
            done("modulation_ready")
            setup.wait_emptied(dve, "fh11")
            for t in range(6):
                dve.tensor_scalar(hf[:, t, :], hf[:, t, :], omlb[:, t:t + 1], lbw[:, t:t + 1], ALU.mult, ALU.add)
                dve.tensor_scalar(hk[:, t, :], hk[:, t, :], omlb[:, t:t + 1], None, ALU.mult)
            done("gates_bounded")
            for t in range(11):
                setup.wait_filled(dve, f"u{t}")
                b, u = seqs(bank(setup, f"u{t}")), seqs(us[:, t, :])
                dve.tensor_scalar(u, b, col("rwkv_shift", 11 + t), None, ALU.mult)
                fence()
                dve.scalar_tensor_tensor(u[:, :, 1:], b[:, :, :T - 1], col("rwkv_shift", t), u[:, :, 1:], ALU.mult, ALU.add)
                fence()
                emptied(setup, dve.scalar_tensor_tensor(u[:, :, :T - 1], b[:, :, 1:], col("rwkv_shift", 22 + t), u[:, :, :T - 1],
                                                        ALU.mult, ALU.add))
            done("shifted")
            for m in range(2):
                setup.wait_filled(dve, f"pv{m}")
                emptied(setup, dve.tensor_copy(pv[:, m, :], bank(setup, f"pv{m}")[:, 0:T]))
            for n in range(2):
                setup.wait_filled(dve, f"pmix{n}")
                emptied(setup, dve.scalar_tensor_tensor(mix[:, n, :], bank(setup, f"pmix{n}")[:, 0:T], col("pool_scale", n),
                                                        mix[:, n, :], ALU.mult, ALU.mult))
            for n, name in enumerate(("rwkv_k_k", "rwkv_k_a", "rwkv_k_a")):
                dve.tensor_copy(rc[:, :, n:n + 1], cols[:, COL[name]:COL[name] + JT].unsqueeze(2))
            for d in range(2):
                o = COL["rwkv_r_k"] + JT * d
                dve.tensor_copy(rc[:, :, 3 + d:4 + d], cols[:, o:o + JT].unsqueeze(2))
            fence()
            dve.tensor_scalar(rc[:, :, 2:3], rc[:, :, 2:3], -1.0, 1.0, ALU.mult, ALU.add)

            hg.start(dve, "D")
            with dve.Fori(0, JT) as j:
                for d in range(2):
                    dve.wait_ge(sem(f"h_loaded{d}"), j + 1)
                    dve.memset(se, 1.0)
                    for h in range(2):
                        hg.wait_filled(dve, f"diag{h}{d}", j)
                        emptied(hg, dve.tensor_tensor(acc[:, 2 * h:2 * h + 2], flat2_(bank(hg, f"diag{h}{d}")[:, 0:T]),
                                                      bc(cst("ident"), 2), ALU.mult))

                    def operands(l):
                        s = l % 2
                        tok = slice(T, 2 * T) if l < 8 else slice(0, T)
                        dve.tensor_tensor(ql[:, s], lq, pi[:, T:2 * T], ALU.mult)
                        dve.tensor_tensor(kl[:, s], lk[:, tok], se[:, tok], ALU.mult)
                        done("h_level_ready")

                    fence()
                    operands(0)
                    for l in range(8):
                        n = 1 << l
                        pv_ = pi.rearrange("p (n h b) -> p n h b", h=2, b=n)
                        sv_ = se.rearrange("p (n h b) -> p n h b", h=2, b=n)
                        blocks = T // n
                        end = pv_[:, :, 1, n - 1:n].to_broadcast([P, blocks, n])
                        dve.tensor_tensor(sv_[:, :, 0, :], sv_[:, :, 0, :], end, ALU.mult)
                        fence()
                        end = pv_[:, :, 0, n - 1:n].to_broadcast([P, blocks, n])
                        dve.tensor_tensor(pv_[:, :, 1, :], pv_[:, :, 1, :], end, ALU.mult)
                        fence()
                        if l == 7:
                            hg.wait_filled(dve, f"lev61{d}", j)
                        operands(l + 1)
                        if l < 7:
                            for h in range(2):
                                held(hg, f"lev{l}{h}{d}", j)
                                emptied(hg, dve.copy_predicated(acc[:, 2 * h:2 * h + 2], bc(cst_int(f"up{l}"), 2),
                                                                flat2_(bank(hg, f"lev{l}{h}{d}")[:, 0:T])))
                    hg.wait_filled(dve, f"state{d}", j)
                    emptied(hg, dve.tensor_tensor(hstate, bank(hg, f"state{d}")[:, 0:P], cst("blocks"), ALU.mult))
                    hg.wait_filled(dve, f"o{d}", j)
                    o = oacc[:, bass.ds(j, 1), :].rearrange("p a t -> p (a t)")
                    b = bank(hg, f"o{d}")[:, 0:T]
                    if d == 0:
                        emptied(hg, dve.tensor_copy(o, b))
                    else:
                        emptied(hg, dve.tensor_tensor(o, b[:, ::-1], o, ALU.add))
            hg.wait_all(dve)

            for v in (nlb, lkm, akm, abm):
                dve.memset(v, 0.0)
            rw.start(dve, "D")
            with dve.Fori(0, JT) as j:
                for d in range(2):
                    rwkv_vector(dve, j, d, done, emptied, bc, fence, held)

            yflat, bflat = yacc.rearrange("p j t -> p (j t)"), bon.rearrange("p j t -> p (j t)")
            for n, k in ((0, 2), (1, 1)):
                rd.wait_filled(dve, f"ysum{n}")
                r = slice(2 * n * T, (2 * n + k) * T)
                emptied(rd, dve.scalar_tensor_tensor(yc[:, r], bank(rd, f"ysum{n}")[:, 0:k * T], -1.0 / HALF, yflat[:, r], ALU.mult, ALU.add))
            done("y_centred")
            dve.tensor_scalar(xr, xr, ALPHA, None, ALU.mult)
            dve.wait_ge(sem("y_scales"), 1)
            dve.tensor_tensor(yc, yc, rsd, ALU.mult)
            dve.tensor_tensor(rso, rso, oacc.rearrange("p j t -> p (j t)"), ALU.mult)
            fence()
            for jj in range(JT):
                r = slice(jj * T, (jj + 1) * T)
                dve.tensor_scalar(yc[:, r], yc[:, r], col("rwkv_gn_g", jj), col("rwkv_gn_b", jj), ALU.mult, ALU.add)
                dve.scalar_tensor_tensor(mix[:, 5 + jj, :], rso[:, r], col("hgrn_norm_g", jj), mix[:, 5 + jj, :], ALU.mult, ALU.mult)
            fence()
            dve.tensor_tensor(yc, yc, bflat, ALU.add)
            fence()
            dve.tensor_tensor(mix[:, 2:5, :], mix[:, 2:5, :], yc.rearrange("p (j t) -> p j t", t=T), ALU.mult)
            done("mix_ready")
            for k in range(KT):
                rd.wait_filled(dve, f"wo{k}")
                emptied(rd, dve.scalar_tensor_tensor(xr[:, k, :], bank(rd, f"wo{k}")[:, 0:T], modc[:, 2 * KT + k, 0:1], xr[:, k, :],
                                                     ALU.mult, ALU.add))
            rd.wait_filled(dve, "lnsum")
            fence()
            emptied(rd, dve.scalar_tensor_tensor(xr, bc(bank(rd, "lnsum")[:, 0:T], KT), -1.0 / D, xr, ALU.mult, ALU.add))
            done("ln_centred")
            rd.wait_emptied(dve, "lnvar")
            dve.reciprocal(rl[:, 0:T], rl[:, 0:T])
            fence()
            dve.tensor_tensor(xr, xr, bc(rl[:, 0:T], KT), ALU.mult)
            fence()
            for k in range(KT):
                dve.tensor_scalar(xr[:, k, :], xr[:, k, :], col("ln_g", k), col("ln_b", k), ALU.mult, ALU.add)
            done("residual_ready")

        def rwkv_vector(dve, j, d, done, emptied, bc, fence, held):
            dve.tensor_copy(pc, rc[:, bass.ds(j, 1), :].rearrange("p a b -> p (a b)"))
            done(f"r_columns{d}")
            dve.wait_ge(sem(f"r_loaded{d}"), j + 1)
            dve.memset(rs, 0.0)
            done(f"r_state_zero{d}")
            dve.tensor_copy(xi, bc(cst("ident"), 8))
            dve.tensor_copy(xti, bc(cst("ident"), 8))
            dve.tensor_scalar(kkr, rlk, pc[:, 0:1], None, ALU.mult)
            dve.tensor_scalar(km, rla, pc[:, 1:2], pc[:, 2:3], ALU.mult, ALU.add)
            dve.tensor_tensor_scan(rl, cst("keep"), rsw, 0.0, ALU.mult, ALU.add)
            fence()
            dve.tensor_tensor(km, km, rlk, ALU.mult)
            dve.tensor_copy(mid, rl[:, HALF - 1::P])
            fence()
            rlv_ = rl.rearrange("p (c t) -> p c t", t=P)
            dve.tensor_tensor(rlv_, rlv_, mid.unsqueeze(2).to_broadcast([P, 4, P]), ALU.subtract)
            fence()
            dve.tensor_tensor(rsw, rl, rsw, ALU.subtract)
            done(f"r_cumulated{d}")
            dve.wait_ge(sem(f"r_norm{d}"), j + 1)
            dve.tensor_tensor(kkr, kkr, rn, ALU.mult)
            fence()
            dve.tensor_tensor(rla, kkr, rla, ALU.mult)
            dve.scalar_tensor_tensor(rn[:, 0:T], rlr, pc[:, 3 + d:4 + d], km[:, T:2 * T], ALU.mult, ALU.mult)
            fence()
            dve.wait_ge(sem(f"r_decays{d}"), j + 1)
            dve.tensor_tensor(pexc, kkr, pexc, ALU.mult)
            dve.tensor_tensor(km, km, pinv, ALU.mult)
            dve.scalar_tensor_tensor(rla, rla, -1.0, pinv, ALU.mult, ALU.mult)
            dve.tensor_tensor(rlr, rlr, pinc[:, T:2 * T], ALU.mult)
            dve.tensor_tensor(e1[:, 0:3], pinc[:, P - 1:3 * P:P], e2[:, 1:4], ALU.mult)
            done(f"r_operands{d}")
            rw.wait_filled(dve, f"bonus{d}", j)
            b = bank(rw, f"bonus{d}")[:, 0:T]
            o = bon[:, bass.ds(j, 1), :].rearrange("p a t -> p (a t)")
            if d == 0:
                emptied(rw, dve.tensor_tensor(o, b, rlv[:, T:2 * T], ALU.mult))
            else:
                emptied(rw, dve.tensor_tensor(kkr[:, 0:T], b, rlv[:, T:2 * T], ALU.mult))
                fence()
                dve.tensor_tensor(o, kkr[:, 0:T][:, ::-1], o, ALU.add)

            def put(dst, mask, g):
                n = dst.shape[1]
                return dve.copy_predicated(dst, bc(cst_int(mask), n), flat2_(bank(rw, g)[:, 0:n * P]))

            for g in range(2):
                held(rw, f"lbT{g}{d}", j)
                emptied(rw, put(xi[:, 4 * g:4 * g + 4], "up0", f"lbT{g}{d}"))
            for g in range(2):
                held(rw, f"lb{g}{d}", j)
                put(nlb[:, 4 * g:4 * g + 4], "after", f"lb{g}{d}")
                emptied(rw, put(xti[:, 4 * g:4 * g + 4], "down0", f"lb{g}{d}"))
            for g in range(2):
                held(rw, f"lk{g}{d}", j)
                emptied(rw, put(lkm[:, 4 * g:4 * g + 4], "before", f"lk{g}{d}"))
            for name, dst in (("ak", akm), ("ab", abm)):
                for g in range(2):
                    held(rw, f"{name}{g}{d}", j)
                    emptied(rw, put(dst[:, 2 * g:2 * g + 2], "upto", f"{name}{g}{d}"))
            for l in range(1, 7):
                for g in range(2):
                    fence()
                    held(rw, f"x{l}{g}{d}", j)
                    emptied(rw, put(xi[:, 4 * g:4 * g + 4], f"up{l}", f"x{l}{g}{d}"))
                    if l < 6:
                        held(rw, f"xt{l}{g}{d}", j)
                        emptied(rw, put(xti[:, 4 * g:4 * g + 4], f"down{l}", f"xt{l}{g}{d}"))
            for c in range(4):
                if c >= 2:
                    rw.wait_filled(dve, f"y{c}{d}", j)
                    b = bank(rw, f"y{c}{d}")[:, 0:P]
                    q = c - 2 if d == 0 else 3 - c
                    o = yacc[:, bass.ds(j, 1), q * P:(q + 1) * P].rearrange("p a t -> p (a t)")
                    if d == 0:
                        emptied(rw, dve.tensor_copy(o, b))
                    else:
                        emptied(rw, dve.tensor_tensor(o, b[:, ::-1], o, ALU.add))
                if c < 3:
                    fence()
                    rw.wait_filled(dve, f"s{c}{d}", j)
                    dve.tensor_tensor(stmp, bank(rw, f"s{c}{d}")[:, 0:P], rs, ALU.add)
                    fence()
                    emptied(rw, dve.scalar_tensor_tensor(rs, stmp, e1[:, c:c + 1], cst("blocks"), ALU.mult, ALU.mult))

        def layer_vector(dve, l, done, emptied, bc, fence):
            for n, name in enumerate(("g_mix_2", "g_mlp_2")):
                dve.tensor_copy(gcol[:, n, :], cols[:, bass.ds(l * KT + COL[name], KT)])
            for r0 in (0, HALF):
                dve.tensor_copy(bcol[r0:r0 + 8], bf[r0:r0 + 8, bass.ds(l, 1)])
            done("bias_column_ready")
            ly.wait_emptied(dve, "ss1", l)
            normed(dve, gcol[:, 0, :], fence)
            done("h1_ready")
            ly.wait_filled(dve, "wi", l)
            emptied(ly, dve.tensor_scalar(wi, bank(ly, "wi")[:, 0:8].rearrange("p (m h) -> p m h", h=4), 0.5, None, ALU.mult))
            for g, dst, n in (("rqc0", qc[:, 0:2], 2), ("rqc1", qc[:, 2:4], 2), ("rkc", kc, 2), ("rqi", qi, 2), ("rki", ki.unsqueeze(1), 1)):
                ly.wait_filled(dve, g, l)
                rt = rot_t[:, 0:n * T].rearrange("p (a t) -> p a t", t=T)
                emptied(ly, dve.tensor_tensor(rt, bank(ly, g)[:, 0:n * T].rearrange("p (a t) -> p a t", t=T), bc(sin, n), ALU.mult))
                dve.tensor_tensor(dst, dst, bc(cos, n), ALU.mult)
                fence()
                dve.tensor_tensor(dst, dst, rt, ALU.add)
                fence()
            done("roped")
            dve.wait_ge(sem("forget_logs"), l + 1)
            for f8 in (slice(0, 8), slice(HALF, HALF + 8)):
                dve.scalar_tensor_tensor(fe[f8], fs[f8], 0.0, fe[f8], ALU.min, ALU.subtract)
                fence()
                dve.tensor_tensor_scan(fc[f8], fe[f8], zeros[f8], 0.0, ALU.add, ALU.add)
                fence()
                dve.tensor_scalar(fn[f8], fc[f8], -1.0, None, ALU.mult)
            done("forget_ready")
            dve.wait_ge(sem("dots_ready"), l + 1)
            tiles = ((0, 0, P), (1, P, T))
            for h in range(4):
                for m, o, w in tiles:
                    v = score[:, o:o + w]
                    if h == 0:
                        dve.tensor_scalar(v, rdots[:, 0, o:o + w], wi[:, m, 0:1], None, ALU.mult)
                    else:
                        dve.scalar_tensor_tensor(v, rdots[:, h, o:o + w], wi[:, m, h:h + 1], v, ALU.mult, ALU.add)
                fence()
            dve.tensor_tensor(wk, score, cst("causal"), ALU.add)
            for _ in range(TOPK // 8):
                fence()
                for m, o, w in tiles:
                    dve.max(top8[:, m, :], wk[:, o:o + w])
                fence()
                for m, o, w in tiles:
                    dve.match_replace(wk[:, o:o + w], top8[:, m, :], wk[:, o:o + w], TAKEN)
            fence()
            dve.tensor_scalar(bias_c, wk, TAKEN, NEG, ALU.not_equal, ALU.mult)
            fence()
            dve.tensor_tensor(bias_c, bias_c, cst("causal"), ALU.add)

            def masked(i):
                kind, _ = STEPS[i]
                s = i % 2
                ly.wait_filled(dve, f"z{i}", l)
                b = bank(ly, f"z{i}")[:, 0:384]
                if kind == "B":
                    emptied(ly, dve.tensor_tensor(zm[:, s, :], b, cst("causal"), ALU.add))
                else:
                    emptied(ly, dve.scalar_tensor_tensor(zm[:, s, :], b, 0.125, bias_c, ALU.mult, ALU.add))
                fence()
                for m, o, w in tiles:
                    dve.tensor_reduce(nmx[:, s, m:m + 1], zm[:, s, o:o + w], AX, ALU.max, negate=True)
                done("scores_ready")

            def finish(i):
                kind, _ = STEPS[i]
                s = i % 2
                if kind == "A":
                    ly.wait_emptied(dve, f"z{i}", l)
                    dve.tensor_tensor(pp[:, s, :], pp[:, s, :], cst("unstrict"), ALU.max)
                    dve.tensor_tensor(sg[:, s, :], sg[:, s, :], cst("strict"), ALU.mult)
                    fence()
                    for m, o, w in tiles:
                        dve.tensor_tensor_scan(zm[:, s, o:o + w][:, ::-1], pp[:, s, o:o + w][:, ::-1], zeros[:, 0:w], 1.0,
                                               ALU.mult, ALU.add)
                    fence()
                else:
                    dve.wait_ge(sem("exps_ready"), l * 16 + (i + 1 if kind == "B" else i - 7))
                    dve.reciprocal(rsum[:, s, :], sums[:, s, :])
                    fence()
                if i >= 2:
                    ly.wait_filled(dve, f"wT{i - 2}", l)
                if kind == "A":
                    dve.tensor_tensor(wgt[:, s, 0:383], sg[:, s, 0:383], zm[:, s, 1:384], ALU.mult)
                    dve.memset(wgt[:, s, 383:384], 0.0)
                else:
                    for m, o, w in tiles:
                        dve.tensor_scalar(wgt[:, s, o:o + w], pp[:, s, o:o + w], rsum[:, s, m:m + 1], None, ALU.mult)
                done("weights_ready")

            for i in range(len(STEPS) + 1):
                if i < len(STEPS) and STEPS[i][0] != "A":
                    masked(i)
                if i:
                    finish(i - 1)
            for b_ in range(3):
                for n in range(4):
                    g = f"br{b_}{n}"
                    ly.wait_filled(dve, g, l)
                    b = bank(ly, g).rearrange("p (a t) -> p a t", a=2)
                    gate = gt[:, 8 * b_ + 2 * n:8 * b_ + 2 * n + 2, :]
                    y = yy[:, 2 * n:2 * n + 2, :]
                    rt = rot_t.rearrange("p (a t) -> p a t", a=2)
                    if b_ == 0:
                        emptied(ly, dve.scalar_tensor_tensor(y, gate, 1.0, b, ALU.add, ALU.mult))
                    else:
                        dve.scalar_tensor_tensor(rt, gate, 1.0, b, ALU.add, ALU.mult)
                        fence()
                        emptied(ly, dve.tensor_tensor(y, y, rt, ALU.add))
                        fence()
            for n in range(4):
                ly.wait_filled(dve, f"out{n}", l)
                v = xr[:, 2 * n:2 * n + 2, :]
                emptied(ly, dve.scalar_tensor_tensor(v, bank(ly, f"out{n}").rearrange("p (a t) -> p a t", a=2), 0.5, v, ALU.mult, ALU.add))
            done("attended")
            ly.wait_emptied(dve, "ss2", l)
            normed(dve, gcol[:, 1, :], fence)
            done("h2_ready")
            for n in range(16):
                ly.wait_emptied(dve, f"up{n}", l)
                v = hff[:, 2 * n:2 * n + 2, :]
                dve.tensor_tensor(v, v, v, ALU.mult)
            done("hidden_ready")
            for n in range(8):
                ly.wait_filled(dve, f"dn{n}", l)
                emptied(ly, dve.tensor_tensor(xr[:, n, :], xr[:, n, :], bank(ly, f"dn{n}")[:, 0:T], ALU.add))
            done("layers_done")

        @block.vector
        def _(dve):
            def done(name):
                dve.drain().then_inc(sem(name), 1)

            def emptied(b, ins):
                ins.then_inc(b.emptied["D"], 1)

            def bc(ap, n, where=1):
                v = ap.unsqueeze(where)
                shape = list(v.shape)
                shape[where] = n
                return v.to_broadcast(shape)

            fence = dve.drain

            def held(b, g, it):
                b.wait_filled(dve, g, it)
                dve.sem_inc(sem("groups_met"), 1)

            for n, e in enumerate(EPS):
                dve.memset(epsc[:, n:n + 1], e)
            dve.memset(one_, 1.0)
            dve.memset(zeros, 0.0)
            dve.wait_ge(s_const, 16)
            dve.wait_ge(s_in, 16 * N_SMALL)
            ang, turns = ht[:, 0, :], ht[:, 1, :]
            dve.tensor_copy(ang, pos_i)
            fence()
            dve.tensor_scalar(ang, ang, cst("freq"), None, ALU.mult)
            fence()
            dve.tensor_scalar(turns, ang, float(0.5 / np.pi), None, ALU.mult)
            big = float(3 << 22)
            for x in (big, -big):
                fence()
                dve.tensor_scalar(turns, turns, x, None, ALU.add)
            two_pi_hi = 6.28125
            for x in (two_pi_hi, float(2 * np.pi - two_pi_hi)):
                fence()
                dve.scalar_tensor_tensor(ang, turns, -x, ang, ALU.mult, ALU.add)
            fence()
            dve.tensor_scalar(ang, ang, 3.1415925, -3.1415925, ALU.min, ALU.max)
            fence()
            dve.scalar_tensor_tensor(turns, ang, -1.0, ang, ALU.mult, ALU.max)
            fence()
            dve.tensor_scalar(turns, turns, -1.0, float(np.pi / 2), ALU.mult, ALU.add)
            done("angles_ready")
            setup.wait_filled(dve, "colsA")
            emptied(setup, dve.tensor_copy(cols[:, 0:ROWS_A], bank(setup, "colsA")[:, 0:ROWS_A]))
            setup.wait_filled(dve, "colsB")
            emptied(setup, dve.tensor_copy(cols[:, ROWS_A:], bank(setup, "colsB")[:, 0:ROWS_B]))
            done("cols_ready")
            for g in range(4):
                setup.wait_filled(dve, f"xr{g}")
                emptied(setup, dve.tensor_copy(xr[:, 2 * g:2 * g + 2, :], bank(setup, f"xr{g}").rearrange("p (a t) -> p a t", a=2)))
            if first:
                first_vector(dve, done, emptied, bc, fence, held)
            else:
                done("residual_ready")
            if second:
                dve.memset(fc, 0.0)
                dve.memset(fn, 0.0)
                ly.start(dve, "D")
                with dve.Fori(0, LAYERS) as l:
                    layer_vector(dve, l, done, emptied, bc, fence)
                en.wait_emptied(dve, "ssf")
                normed(dve, cols[:, COL["g_final_2"]:COL["g_final_2"] + KT], fence)
                done("final_ready")
            done("finished")

    return nc


_INS = ["x", "c", "ctx", "c_ctx", "mod_w", "mod_b", "w_in", "rwkv_shift", "pool_w", "pool_scale", "rwkv_w0", "rwkv_w_up",
        "rwkv_a0", "rwkv_a_up", "rwkv_k_k", "rwkv_k_a", "rwkv_r_k", "rwkv_gn_g", "rwkv_gn_b", "hgrn_lb_logits",
        "hgrn_norm_g", "w_out", "ln_g", "ln_b", "positions_2", "g_mix_2", "w_in_2", "b_forget_2", "w_branch_2", "w_out_2",
        "g_mlp_2", "w_up_2", "w_down_2", "g_final_2"]


def kernel(**inputs):
    import concourse.bacc as _bacc
    from concourse.bass_utils import run_bass_kernel_spmd as _run

    nc = _bacc.Bacc("TRN2", target_bir_lowering=False, num_devices=1)
    arrays, args = {}, {}
    for name in _INS + ["const"]:
        arr = constants() if name == "const" else np.ascontiguousarray(inputs[name])
        arrays[f"in_{name}"] = arr
        args[name] = nc.dram_tensor(f"in_{name}", arr.shape, mybir.dt.from_np(arr.dtype), kind="ExternalInput").ap()
    out = nc.dram_tensor("out_0", (1, T, D), F32, kind="ExternalOutput").ap()
    build(nc, args, out)
    r = _run(nc, [arrays], core_ids=[0])
    return r.results[0]["out_0"]
```

```python
from contextlib import ExitStack

import numpy as np

import concourse.bass as bass
from concourse import mybir

F32 = mybir.dt.float32
I32 = mybir.dt.int32
ALU = mybir.AluOpType
ACT = mybir.ActivationFunctionType
AX = mybir.AxisListType.X

P = 128
D = 1024
KT = D // P
T = 256
HALF = 64
MODC = 3 * D
N_RW = 384
JT = N_RW // P
D_IN = 4224
COLS2 = 7244
FF = 4 * D
LAYERS = 2
HEADS = 8
LN_EPS, GN_EPS, RMS_EPS, NORM_EPS = 1e-5, 64e-5, 1e-6, 1e-6
ALPHA = float(2 ** 0.25)
DECAY = float(np.exp(-0.5))
NEG = -1e38
TOPK = 64
TAKEN = -3e38
SLOTS = 3
NB = 8

CONST = {}
FIRST_CONST = 3 * P


def constants():
    parts, layer_parts = [], []

    def put(name, a, to=parts):
        CONST[name] = (sum(p.shape[1] for p in to), a.shape[1], to is layer_parts)
        to.append(np.asarray(a, np.float32))

    r, c = np.arange(P)[:, None], np.arange(P)[None, :]
    put("ident", r == c)
    put("ones", np.ones((P, P)))
    put("blocks", r // HALF == c // HALF)
    for l in range(7):
        b = 1 << l
        up = (r // (2 * b) == c // (2 * b)) & (r // b % 2 == 0) & (c // b % 2 == 1)
        put(f"up{l}", up)
        put(f"down{l}", up.T)
    put("before", r < c)
    put("upto", r <= c)
    put("after", r > c)
    for g, win in enumerate((2, 4, 8, 16)):
        left, right = win // 2, win - 1 - win // 2
        row, x = np.arange(P) // 64, np.arange(P) % 64
        lo, hi = np.maximum(x - left, 0), np.minimum(x + right, 63)
        a = (row[:, None] == row[None, :]) & (x[:, None] >= lo[None, :]) & (x[:, None] <= hi[None, :])
        put(f"pool{g}", a / (hi - lo + 1)[None, :] - (r == c))
    s = np.concatenate([np.arange(P), np.arange(T)])[None, :]
    t = np.concatenate([np.arange(P)[:, None].repeat(P, 1), P + np.arange(P)[:, None].repeat(T, 1)], 1)
    put("strict", s < t, layer_parts)
    put("unstrict", s >= t, layer_parts)
    put("causal", np.where(s <= t, 0.0, NEG), layer_parts)
    put("keep", (np.arange(2 * T) % P != 0)[None, :].repeat(P, 0))
    k, m = r % HALF, c % HALF
    same = r // HALF == c // HALF
    put("rot", np.where(same & (m < 8) & (k == m + 8), -1.0, np.where(same & (m >= 8) & (m < 16) & (k == m - 8), 1.0, 0.0)),
        layer_parts)
    ch = np.arange(P) % HALF
    inv = np.float32(500000.0) ** (-(np.arange(0, 16, 2, dtype=np.float32)) / np.float32(16))
    put("freq", np.where(ch < 16, inv[ch % 8], 0.0)[:, None])
    return np.concatenate(parts, 1), np.concatenate(layer_parts, 1)


N_CONST, N_CONST2 = [x.shape[1] for x in constants()]

STACK_A = [("mod_b", 24), ("rwkv_w0", 6), ("rwkv_a0", 6), ("rwkv_k_k", 3), ("rwkv_k_a", 3), ("rwkv_r_k", 6),
           ("rwkv_gn_g", 3), ("rwkv_gn_b", 3), ("hgrn_lb_logits", 6), ("hgrn_norm_g", 3), ("pool_scale", 2),
           ("ln_g", 8), ("ln_b", 8), ("rwkv_shift", 33)]
STACK_B = [("g_mix_2", 16), ("g_mlp_2", 16), ("g_final_2", 8)]
ROWS_A = sum(n for _, n in STACK_A)
ROWS_B = sum(n for _, n in STACK_B)
COL = {}
for _n, (_name, _rows) in enumerate(STACK_A + STACK_B):
    COL[_name] = sum(n for _, n in (STACK_A + STACK_B)[:_n])



def rows_of(w, k0, k1, c0, c1):
    return w[k0 * P:k1 * P, c0:c1].rearrange("(k p) n -> p k n", p=P)


FIRST = ([("mod_w", 512 * n, 512 * n + 512) for n in range(6)]
         + [("w_in", a, b) for a, b in ((1664, 2176), (2176, 2688), (2688, 3200), (256, 768), (768, 1280),
                                        (1280, 1664), (0, 256), (3200, 3712), (3712, 4224))]
         + [("w_out", 0, 512), ("w_out", 512, 1024)])
LAYER_IN = [[(0, 3080, 512)],
            [(0, 3592, 64), (64, 3592, 64), (128, 3656, 64), (192, 3656, 64), (256, 3848, 256)],
            [(0, 3720, 128), (128, 4104, 64), (192, 4104, 64), (256, 4168, 4), (260, 3072, 8)],
            [(0, 0, 512)], [(0, 512, 512)], [(0, 1024, 512)],
            [(0, 1536, 512)], [(0, 2048, 512)], [(0, 2560, 512)]] + [[(0, 4172 + 512 * n, 512)] for n in range(6)]
N_IN = len(LAYER_IN)
LAYER_CHUNKS = N_IN + 3 + 2 + 8 + 8
assert LAYER_CHUNKS % SLOTS == 0
PIECES = [1] * len(FIRST) + [len(x) for x in LAYER_IN] + [1] * (LAYER_CHUNKS - N_IN)


def landed(n):
    return 16 * sum(PIECES[m] for m in range(n % SLOTS, n + 1, SLOTS))


SLOT_PER_LAYER = [16 * sum(PIECES[len(FIRST) + i] for i in range(LAYER_CHUNKS) if (len(FIRST) + i) % SLOTS == s)
                  for s in range(SLOTS)]


class Banks:

    def __init__(self, sem, name, plan, loops=0, first=0, banks=NB):
        self.plan, self.loops, self.first, self.banks = plan, loops, first, banks
        self.filled = sem(name + "_filled")
        self.emptied = {"A": sem(name + "_emptied_act"), "D": sem(name + "_emptied_dve")}
        self.at = {g: k for k, (g, _) in enumerate(plan) if g}
        self.n_filled = sum(1 for g, _ in plan if g)
        self.n_emptied = {e: sum(1 for g, x in plan if g and x == e) for e in "AD"}
        assert not loops or len(plan) % banks == 0

    def bank(self, g):
        return self.first + self.at[g] % self.banks

    def _full(self, g):
        return sum(1 for x, _ in self.plan[:self.at[g] + 1] if x)

    def _empty(self, g):
        e = self.plan[self.at[g]][1]
        return e, sum(1 for x, y in self.plan[:self.at[g] + 1] if x and y == e)

    def start(self, eng, which):
        if self.loops:
            sem, n = (self.filled, self.n_filled) if which == "P" else (self.emptied[which], self.n_emptied[which])
            eng.sem_inc(sem, n)

    def wait_filled(self, eng, g, it=0, before=0):
        n = self._full(g) + (0 if before or not self.loops else self.n_filled)
        eng.wait_ge(self.filled, it * self.n_filled + n)

    def wait_emptied(self, eng, g, it=0, before=0):
        e, n = self._empty(g)
        n += 0 if before or not self.loops else self.n_emptied[e]
        eng.wait_ge(self.emptied[e], it * self.n_emptied[e] + n)

    def wait_free(self, pe, g, it=0):
        k, before = self.at[g] - self.banks, 0
        while k < 0 or not self.plan[k][0]:
            if k < 0:
                if not self.loops or before:
                    return
                k, before = k + len(self.plan), 1
            else:
                k -= self.banks
        self.wait_emptied(pe, self.plan[k][0], it, before)

    def wait_all(self, eng):
        for e in "AD":
            if self.n_emptied[e]:
                eng.wait_ge(self.emptied[e], self.n_emptied[e] * (self.loops + 1 if self.loops else 1))


R_STEPS, H_STEPS = 13, 11
TURN = "RHHRHRHRHRHRHRHRHRHRHRRR"


def interleave(rwkv, hgrn):
    assert TURN.count("R") == R_STEPS and TURN.count("H") == H_STEPS
    for x in TURN:
        next(rwkv if x == "R" else hgrn)
    assert next(rwkv, None) is None and next(hgrn, None) is None


def padded(plan, banks=NB):
    return plan + [(None, None)] * (-len(plan) % banks)


PLAN_SETUP = ([("colsC", "D")] + [(f"mod{n}", "A") for n in range(4)] + [(f"xr{g}", "D") for g in range(4)]
              + [(f"mod{n}", "A") for n in range(4, 6)]
              + [("colsA", "D"), ("colsB", "D"), ("modT", "D")] + [(f"xt{k}", "A") for k in range(KT)]
              + [(f"fh{t}", "A") for t in range(12)] + [(f"u{t}", "D") for t in range(11)]
              + [("pv0", "D"), ("pv1", "D")] + [(f"g{n}", "A") for n in range(4)]
              + [(f"pool{n}", "A") for n in range(2)] + [(f"pmix{n}", "D") for n in range(2)])
H_BANKS, R_BANKS = 3, 5
PLAN_HGRN = padded([x for d in range(2) for x in
                    [(f"itok{d}", "A")] + [(f"diag{h}{d}", "D") for h in range(2)]
                    + [(f"lev{l}{h}{d}", "D") for l in range(7) for h in range(2)]
                    + [(f"cross{h}{d}", "A") for h in range(2)] + [ (f"ktok{d}", "A"), (f"state{d}", "D"), (f"o{d}", "D")]], H_BANKS)
PLAN_LORA = [(f"{x}{d}{j}", "A") for d in range(2) for j in range(JT) for x in ("w", "a")]


def plan_rwkv(d):
    p = [(f"kk{d}", "A"), (f"bonus{d}", "D"), (f"ktok{d}", "A"), (f"btok{d}", "A"), (f"vtok{d}", "A")]
    p += [(f"{x}{g}{d}", "D") for x in ("lbT", "lb", "lk", "ak", "ab") for g in range(2)]
    for l in range(1, 7):
        p += [(f"w{l}{g}{d}", "A") for g in range(2)]
        for g in range(2):
            p += [(f"x{l}{g}{d}", "D")] + ([(f"xt{l}{g}{d}", "D")] if l < 6 else [])
    for c in range(4):
        p += [(f"rhs{c}{d}", "A"), (f"u{c}{d}", "A")] + ([(f"y{c}{d}", "D")] if c >= 2 else [])
        p += [(f"s{c}{d}", "D")] if c < 3 else []
    return p


PLAN_RWKV = padded(plan_rwkv(0) + plan_rwkv(1), R_BANKS)
PLAN_READ = ([(f"ysum{n}", "D") for n in range(2)] + [(f"osq{n}", "A") for n in range(2)]
             + [(f"yvar{n}", "A") for n in range(2)] + [(f"wo{k}", "D") for k in range(KT)] + [("lnsum", "D"), ("lnvar", "A")])

DOTS = ((0, (0, 1, 2, 3)), (1, (0, 1)), (1, (2, 3)))
STEPS = [("B", h) for h in range(HEADS)] + [("A", h) for h in range(HEADS)] + [("C", h) for h in range(HEADS)]


def plan_layer():
    p = [("ss1", "A"), ("qc0", "A"), ("qc1", "A"), ("kc", "A"), ("qi", "A"), ("vc", "A"), ("ki", "A"), ("wi", "D"), ("fl", "A")]
    p += [("rqc0", "D"), ("rqc1", "D"), ("rkc", "D"), ("rqi", "D"), ("rki", "D")]
    p += [(f"{x}{n}", "A") for x in ("qa", "ka") for n in range(2)] + [(f"dot{n}", "A") for n in range(len(DOTS))]
    p += [(f"{x}{n}", "A") for x in ("va", "qb", "kb", "vb") for n in range(2)]
    p += [("fct", "D")]
    for i in range(len(STEPS) + 1):
        if i < len(STEPS):
            p += [(f"z{i}", "A" if STEPS[i][0] == "A" else "D")]
        if i:
            p += [(f"wT{i - 1}", "A")]
        if i < len(STEPS):
            p += [(f"gl{i}", "A")]
        if i:
            p += [(f"o{i - 1}", "A")]
    p += [(f"br{b}{n}", "D") for b in range(3) for n in range(4)] + [(f"out{n}", "D") for n in range(4)] + [("ss2", "A")]
    p += [(f"up{n}", "A") for n in range(16)] + [(f"dn{n}", "D") for n in range(8)]
    return padded(p)


PLAN_LAYER = plan_layer()
PLAN_END = [("ssf", "A")] + [(f"fin{m}{n}", "A") for m in range(2) for n in range(2)]


def build(nc, a, out, first=True, second=True, dump=None):
    ctx = ExitStack()
    with ctx:
        sems = {}

        def sem(name):
            if name not in sems:
                sems[name] = ctx.enter_context(nc.semaphore(name))
            return sems[name]

        arena = ctx.enter_context(nc.sbuf_tensor("arena", [P, 207 * 256], F32))
        top = [0]

        def take(n, shape=None):
            v = arena[:, top[0]:top[0] + n]
            top[0] += n
            assert top[0] <= 207 * 256, top[0]
            if shape:
                names = "abcd"[:len(shape)]
                v = v.rearrange("p (" + " ".join(names) + ") -> p " + " ".join(names),
                                **{x: s for x, s in zip(names, shape)})
            return v

        psum = ctx.enter_context(nc.psum_tensor("psum", [P, NB, 512], F32))

        ring = take(SLOTS * KT * 512, (SLOTS, KT, 512))
        const = take(N_CONST)
        cols = take(ROWS_A + ROWS_B)
        xr = take(KT * T, (KT, T))
        cos, sin = take(T), take(T)
        zeros = take(T)
        bf = take(2)
        bcol, one_, epsc = take(1), take(1), take(4)
        EPS = [LN_EPS, GN_EPS, RMS_EPS, 1e-12]
        base = top[0]

        def eps(x):
            return epsc[:, EPS.index(x):EPS.index(x) + 1]

        def cst(name):
            o, n, of_layers = CONST[name]
            return (const2 if of_layers else const)[:, o:o + n]

        def cst_int(name):
            return cst(name).bitcast(I32)

        def col(name, n=0):
            return cols[:, COL[name] + n:COL[name] + n + 1]

        us = take(11 * 512, (11, 512))
        mix = take(KT * T, (KT, T))
        yacc = take(JT * T, (JT, T))
        bon = take(JT * T, (JT, T))
        oacc = take(JT * T, (JT, T))
        rc = take(JT * 5, (JT, 5))
        pc = take(5)
        lbc = take(12, (6, 2))
        lbp = take(2)
        wup = take(N_RW)
        aup = take(N_RW)
        pw = take(2 * HALF, (2, HALF))
        modc = take(48, (24, 2))
        silu_c = take(16, (KT, 2))
        ccol = take(16, (2, KT))
        rstd4 = take(4)
        lbw = take(6)
        lb_inv = take(6)
        pos_i = take(T).bitcast(I32)
        share = top[0]
        hq = take(JT * T, (JT, T))
        hi = take(JT * 512, (JT, 512))
        hz = take(6 * 512, (6, 512))
        sa = take(12 * 512, (2, 6, 512))
        lq, lk, li, pi, se = take(T), take(512), take(512), take(512), take(512)
        ql, kl = take(2 * T, (2, T)), take(2 * T, (2, T))
        acc = take(512, (4, P))
        cross = take(2 * P, (2, P))
        itok, ktok = take(512, (4, P)), take(2 * P, (2, P))
        hstate = take(P)
        rlr, pinc = take(T), take(512)
        rlkv = take(1024)
        rlk, rlv = rlkv[:, 0:512], rlkv[:, 512:1024]
        rsw, rla, rl, pexc, kkr, km, rn = [take(512) for _ in range(7)]
        pinv = rlk
        slot1 = ring[:, 1].rearrange("p k n -> p (k n)").rearrange("p (u t) -> p u t", t=P)
        nlb, akm, abm, rkt, rbt, rvt = [slot1[:, n:n + k] for n, k in ((0, 8), (8, 4), (12, 4), (16, 4), (20, 4), (24, 4))]
        rrhs, ru, rs, stmp = [slot1[:, n] for n in range(28, 32)]
        xi, xti, ww, lkm = [ring[:, 2, 2 * n:2 * n + 2, :].rearrange("p a b -> p (a b)").rearrange("p (u t) -> p u t", t=P)
                            for n in range(4)]
        e1, e2, mid = take(4), take(4), take(4)
        end_first = top[0]
        txw = rl
        sqr = rlkv[:, 0:JT * T]
        sqo, yc, rsd, rso = [v.rearrange("p a b -> p (a b)")[:, 0:JT * T] for v in (xi, xti, ww, lkm)]
        top[0] = share
        x4 = take(4 * D, (4, D))
        stackA, stackB, stackC = take(P), take(P), take(P)
        mrow = take(MODC)
        stats = take(4 * 12, (4, 2, 6))
        mv = take(8, (4, 2))
        assert top[0] > share + (JT * T + 9 * 512)
        xt = take(KT * 512, (KT, 512))
        pv = take(2 * T, (2, T))
        pooled = take(2 * T, (2, T))

        top[0] = base
        ht = take(KT * T, (KT, T))
        gt = take(24 * T, (24, T))
        br = take(12 * T, (3, 4, T))
        qa, qb, qc = [take(8 * T, (8, T)) for _ in range(3)]
        qi = take(4 * T, (4, T))
        const2 = take(N_CONST2)
        ka, kb = [take(4 * T, (4, T)) for _ in range(2)]
        kc = take(2 * T, (2, T))
        ki = take(T)
        va, vb = take(2 * 512, (2, 512)), take(2 * 512, (2, 512))
        vc = take(2 * P, (2, P))
        yy = take(KT * T, (KT, T))
        work0 = top[0]
        zm = take(2 * 384, (2, 384))
        ppwgt = take(4 * 384, (4, 384))
        pp, wgt = ppwgt[:, 0:2], ppwgt[:, 2:4]
        rdots = ppwgt
        wt = take(2 * 384, (2, 384))
        sg = take(2 * 384, (2, 384))
        score = take(384)
        wk = take(384)
        bias_c = take(384)
        rsq = take(T)
        rot_t = take(512)
        nmx, sums, rsum = [take(4, (2, 2)) for _ in range(3)]
        top8 = take(16, (2, 8))
        wi = take(8, (2, 4))
        gcol = take(16, (2, 8))
        fc, fe, fs, fn = [take(T) for _ in range(4)]
        fct = take(16, (2, 8))
        qcr, qir = yy[:, 0:4], yy[:, 4:6]
        top_attn = top[0]
        top[0] = work0
        sq = take(KT * T, (KT, T))
        assert top[0] <= top_attn
        hff = arena[:, base + KT * T:base + KT * T + 32 * T].rearrange("p (k t) -> p k t", t=T)
        assert KT * T + 32 * T <= (2 * KT + 36) * T
        fin = arena[:, base + KT * T:base + KT * T + 2 * D].rearrange("p (m n) -> p m n", m=2)

        setup = Banks(sem, "setup", PLAN_SETUP)
        hg = Banks(sem, "hgrn", PLAN_HGRN, JT, R_BANKS, H_BANKS)
        lora = Banks(sem, "lora", PLAN_LORA)
        rw = Banks(sem, "rwkv", PLAN_RWKV, JT, 0, R_BANKS)
        rd = Banks(sem, "read", PLAN_READ)
        ly = Banks(sem, "layer", PLAN_LAYER, LAYERS)
        en = Banks(sem, "end", PLAN_END)

        s_slot = [sem(f"slot{s}_landed") for s in range(SLOTS)]
        s_used = sem("chunks_used")
        s_const = sem("constants_landed")
        s_tables = sem("tables_landed")
        s_in = sem("inputs_landed")
        s_out = sem("out_landed")

        def bank(b, g):
            return psum[:, b.bank(g), :]

        def flip(ap, d):
            v = ap.rearrange("p (s t) -> p s t", t=T)
            return v[:, :, ::-1] if d else v

        def pair(ap, n):
            return seqs(ap[:, bass.ds(n, 1), :].rearrange("p a t -> p (a t)"))

        def flat2_(ap):
            return ap.rearrange("p (u t) -> p u t", t=P)

        def ht_flat(k):
            return ht[:, k, :]

        def seqs(ap):
            return ap.rearrange("p (s t) -> p s t", t=T)

        def use_chunk(pe, n, l=0):
            s = n % SLOTS
            pe.wait_ge(s_slot[s], l * SLOT_PER_LAYER[s] + landed(n))
            return ring[:, s]

        def vars_of():
            return dict(xr=xr, ht=ht)

        N_SMALL = len(STACK_A) + len(STACK_B) + 5

        block = ctx.enter_context(nc.Block())

        @block.sync
        def _(sp):
            sp.dma_start(const[:, 0:FIRST_CONST], a["const"][:, 0:FIRST_CONST]).then_inc(s_const, 16)
            for n, (w, c0, c1) in enumerate(FIRST):
                if not first:
                    sp.sem_inc(s_slot[n % SLOTS], 16)
                    if n == 1:
                        sp.dma_start(const[:, FIRST_CONST:], a["const"][:, FIRST_CONST:]).then_inc(s_tables, 16)
                    continue
                if n >= SLOTS:
                    sp.wait_ge(s_used, n - SLOTS + 1)
                if n == 16:
                    sp.wait_ge(sem("heads_done"), 1)
                sp.dma_start(ring[:, n % SLOTS, :, 0:c1 - c0], rows_of(a[w][0], 0, KT, c0, c1)).then_inc(
                    s_slot[n % SLOTS], 16)
                if n == 1:
                    sp.dma_start(const[:, FIRST_CONST:], a["const"][:, FIRST_CONST:]).then_inc(s_tables, 16)

            def chunk(l, i, pieces):
                n = len(FIRST) + i
                sp.wait_ge(s_used, l * LAYER_CHUNKS + n - SLOTS + 1)
                sp.sem_inc(sem("loads_begun"), 1)
                for dst, src in pieces:
                    sp.dma_start(dst, src).then_inc(s_slot[n % SLOTS], 16)

            def slot(i):
                return ring[:, (len(FIRST) + i) % SLOTS]

            def layer_row(w, l, rows, c0, c1, k0=0, k=KT):
                v = w.rearrange("l k n -> (l k) n")
                return v[bass.ds(l * rows + k0 * P, k * P), c0:c1].rearrange("(k p) n -> p k n", p=P)

            if second:
                sp.wait_ge(sem("residual_ready"), 1)
                sp.dma_start(const2, a["const2"]).then_inc(sem("const2_landed"), 16)
                with sp.Fori(0, LAYERS) as l:
                    for i, pieces in enumerate(LAYER_IN):
                        chunk(l, i, [(slot(i)[:, :, o:o + n], layer_row(a["w_in_2"], l, D, s, s + n))
                                     for o, s, n in pieces])
                    i = N_IN
                    wb = a["w_branch_2"].rearrange("l b k n -> (l b k) n")
                    for b in range(3):
                        src = wb[bass.ds(l * 1536 + b * 512, 512), :].rearrange("(k p) n -> p k n", p=P)
                        chunk(l, i, [(slot(i).rearrange("p k n -> p (k n)").rearrange("p (k n) -> p k n", n=D), src)])
                        i += 1
                    for h in range(2):
                        chunk(l, i, [(slot(i), layer_row(a["w_out_2"], l, D, 512 * h, 512 * h + 512))])
                        i += 1
                    for h in range(8):
                        chunk(l, i, [(slot(i), layer_row(a["w_up_2"], l, D, 512 * h, 512 * h + 512))])
                        i += 1
                    for h in range(2):
                        for q in range(4):
                            chunk(l, i, [(slot(i), layer_row(a["w_down_2"], l, FF, 512 * h, 512 * h + 512, q * KT))])
                            i += 1
            if dump:
                sp.wait_ge(sem("finished"), 1)
                views = dict(vars_of())
                for name in dump:
                    sp.dma_start(a[name], views[name]).then_inc(s_out, 16)
                sp.wait_ge(s_out, 16 * len(dump))
            else:
                for m in range(2):
                    en.wait_emptied(sp, f"fin{m}1")
                    sp.dma_start(out[0, m * P:(m + 1) * P, :], fin[:, m, :]).then_inc(s_out, 16)
                sp.wait_ge(s_out, 32)

        @block.gpsimd
        def _(gp):
            for stack, place in ((STACK_A, stackA), (STACK_B, stackB)):
                r = 0
                for name, n in stack:
                    v = a[name]
                    names = " ".join(f"d{k}" for k in range(len(v.shape)))
                    v = v.rearrange(f"{names} -> ({names})").rearrange("(t p) -> t p", p=P)
                    gp.dma_start(place[r:r + n, :], v).then_inc(s_in, 16)
                    r += n
            gp.dma_start(wup, a["rwkv_w_up"][0].rearrange("d k n -> (d k) n")).then_inc(s_in, 16)
            gp.dma_start(aup, a["rwkv_a_up"][0].rearrange("d k n -> (d k) n")).then_inc(s_in, 16)
            gp.dma_start(pw, a["pool_w"][0].rearrange("(b g) i o -> (g i) b o", g=2)).then_inc(s_in, 16)
            with nc.allow_non_contiguous_dma(reason="sixteen numbers"):
                gp.dma_start(bf[0:8, :], a["b_forget_2"].rearrange("l h -> h l")).then_inc(s_in, 16)
            gp.dma_start(pos_i, a["positions_2"].to_broadcast([P, T])).then_inc(s_in, 16)
            if second:
                gp.wait_ge(sem("residual_ready"), 1)
                for v in (qa, qb, qc, qi):
                    gp.memset(v[0:HALF, 1::2], 0.0)
                    gp.memset(v[HALF:P, 0::2], 0.0)
                gp.drain().then_inc(sem("queries_cleared"), 1)

        def norm_sum(pe, take_bank, b, g, ready, l):
            v = take_bank(b, g, l)
            for k in range(KT):
                pe.wait_ge(sem(ready), l * KT + k + 1)
                mm = pe.matmul(v[:, 0:T], cst("ones"), sq[:, k, :], start=k == 0, stop=k == KT - 1)
            mm.then_inc(b.filled, 1)

        def rwkv_tensor(pe, j, d, take_bank, turn):
            blocks = cst("blocks")
            pe.wait_ge(sem(f"r_squared{d}"), j + 1)
            b = take_bank(rw, f"kk{d}", j)
            pe.matmul(b, blocks, rn, start=True, stop=True).then_inc(rw.filled, 1)
            yield
            pe.wait_ge(sem(f"r_operands{d}"), j + 1)
            b = take_bank(rw, f"bonus{d}", j)
            pe.matmul(b[:, 0:T], blocks, rn[:, 0:T], start=True, stop=True).then_inc(rw.filled, 1)
            for g, src in (("ktok", km), ("btok", rla), ("vtok", rlv)):
                b = take_bank(rw, f"{g}{d}", j)
                for c in range(4):
                    mm = turn(b[:, c * P:(c + 1) * P], src[:, c * P:(c + 1) * P])
                mm.then_inc(rw.filled, 1)

            yield

            def scores(name, left, right, chunks=range(4)):
                for h in range(2):
                    b = take_bank(rw, f"{name}{h}{d}", j)
                    r = slice(h * HALF, (h + 1) * HALF)
                    for i, c in enumerate(chunks):
                        q = (i if right is rlr else c) * P
                        mm = pe.matmul(b[:, i * P:(i + 1) * P], left[r, c * P:(c + 1) * P], right[r, q:q + P], start=True, stop=True)
                    mm.then_inc(rw.filled, 1)

            scores("lbT", rla, pexc)
            scores("lb", pexc, rla)
            scores("lk", km, pexc)
            scores("ak", km, rlr, (2, 3))
            scores("ab", rla, rlr, (2, 3))
            yield

            def units(name, left, right, g):
                b = take_bank(rw, name, j)
                for u in range(4):
                    mm = pe.matmul(b[:, u * P:(u + 1) * P], left[:, 4 * g + u, :], right[:, 4 * g + u, :], start=True, stop=True)
                mm.then_inc(rw.filled, 1)

            for l in range(1, 7):
                for g in range(2):
                    rw.wait_emptied(pe, f"x{l - 1}{g}{d}" if l > 1 else f"lbT{g}{d}", j)
                    rw.wait_emptied(pe, f"xt{l - 1}{g}{d}" if l > 1 else f"lb{g}{d}", j)
                    units(f"w{l}{g}{d}", nlb, xi, g)
                for g in range(2):
                    rw.wait_emptied(pe, f"w{l}{g}{d}", j)
                    units(f"x{l}{g}{d}", xti, ww, g)
                    if l < 6:
                        units(f"xt{l}{g}{d}", ww, xti, g)
                yield
            rw.wait_emptied(pe, f"vtok{d}", j)
            rw.wait_emptied(pe, f"x61{d}", j)
            halves = [slice(h * HALF, (h + 1) * HALF) for h in range(2)]
            for c in range(4):
                b = take_bank(rw, f"rhs{c}{d}", j)
                for h, r in enumerate(halves):
                    pe.matmul(b[:, r], lkm[:, 4 * h + c, :], rvt[:, c, r], start=h == 0, stop=False, skip_group_check=True)
                if c:
                    rw.wait_emptied(pe, f"s{c - 1}{d}", j)
                else:
                    pe.wait_ge(sem(f"r_state_zero{d}"), j + 1)
                pe.matmul(b[:, 0:P], pexc[:, c * P:(c + 1) * P], rs, start=False, stop=True, skip_group_check=True).then_inc(rw.filled, 1)
                u = take_bank(rw, f"u{c}{d}", j)
                if c >= 2:
                    q = c - 2
                    y = take_bank(rw, f"y{c}{d}", j)
                    pe.matmul(y[:, 0:P], rs, rlr[:, q * P:(q + 1) * P], start=True, stop=False, skip_group_check=True)
                    for h, r in enumerate(halves):
                        pe.matmul(y[r, 0:P], rvt[:, c, r], akm[:, 2 * h + q, :], start=False, stop=False, skip_group_check=True)
                rw.wait_emptied(pe, f"rhs{c}{d}", j)
                for h, r in enumerate(halves):
                    mm = pe.matmul(u[:, r], xi[:, 4 * h + c, :], rrhs[:, r], start=True, stop=True)
                mm.then_inc(rw.filled, 1)
                if c < 3:
                    b = take_bank(rw, f"s{c}{d}", j)
                    pe.matmul(b[:, 0:P], rkt[:, c, :], rvt[:, c, :], start=True, stop=False)
                rw.wait_emptied(pe, f"u{c}{d}", j)
                if c >= 2:
                    for h, r in enumerate(halves):
                        mm = pe.matmul(y[r, 0:P], ru[:, r], abm[:, 2 * h + q, :], start=False, stop=h == 1, skip_group_check=True)
                    mm.then_inc(rw.filled, 1)
                if c < 3:
                    pe.matmul(b[:, 0:P], rbt[:, c, :], ru, start=False, stop=True).then_inc(rw.filled, 1)
                yield

        def hgrn_tensor(pe, j, d, take_bank, turn):
            pe.wait_ge(sem(f"h_loaded{d}"), j + 1)
            b = take_bank(hg, f"itok{d}", j)
            for c in range(4):
                mm = turn(b[:, c * P:(c + 1) * P], li[:, c * P:(c + 1) * P])
            mm.then_inc(hg.filled, 1)

            def pair_scores(g, keys, queries):
                for h in range(2):
                    b = take_bank(hg, f"{g}{h}{d}", j)
                    r = slice(h * HALF, (h + 1) * HALF)
                    for m in range(2):
                        mm = pe.matmul(b[:, m * P:(m + 1) * P], keys[r, m * P:(m + 1) * P],
                                       queries[r, m * P:(m + 1) * P], start=True, stop=True)
                    mm.then_inc(hg.filled, 1)

            pe.wait_ge(sem("h_level_ready"), j * 18 + d * 9 + 1)
            pair_scores("diag", lk[:, T:2 * T], lq)
            yield
            for l in range(7):
                pe.wait_ge(sem("h_level_ready"), j * 18 + d * 9 + l + 1)
                pair_scores(f"lev{l}", kl[:, l % 2], ql[:, l % 2])
                yield
            pe.wait_ge(sem("h_level_ready"), j * 18 + d * 9 + 8)
            for h in range(2):
                b = take_bank(hg, f"cross{h}{d}", j)
                r = slice(h * HALF, (h + 1) * HALF)
                pe.matmul(b[:, 0:P], kl[r, 1, 0:P], ql[r, 1, P:2 * P], start=True, stop=True).then_inc(hg.filled, 1)
            yield
            pe.wait_ge(sem("h_level_ready"), j * 18 + d * 9 + 9)
            b = take_bank(hg, f"ktok{d}", j)
            for c in range(2):
                mm = turn(b[:, c * P:(c + 1) * P], kl[:, 0, c * P:(c + 1) * P])
            mm.then_inc(hg.filled, 1)
            hg.wait_emptied(pe, f"ktok{d}", j)
            b = take_bank(hg, f"state{d}", j)
            for c in range(2):
                mm = pe.matmul(b[:, 0:P], ktok[:, c, :], itok[:, c, :], start=c == 0, stop=c == 1)
            mm.then_inc(hg.filled, 1)
            yield
            hg.wait_emptied(pe, f"cross1{d}", j)
            hg.wait_emptied(pe, f"state{d}", j)
            b = take_bank(hg, f"o{d}", j)
            pe.matmul(b[:, 0:T], hstate, ql[:, 0], start=True, stop=False, skip_group_check=True)
            for h in range(2):
                r = slice(h * HALF, (h + 1) * HALF)
                pe.matmul(b[r, 0:P], itok[:, 2, r], acc[:, 2 * h, :], start=False, stop=False, skip_group_check=True)
                pe.matmul(b[r, P:2 * P], itok[:, 2, r], cross[:, h, :], start=False, stop=False, skip_group_check=True)
                mm = pe.matmul(b[r, P:2 * P], itok[:, 3, r], acc[:, 2 * h + 1, :], start=False, stop=h == 1,
                               skip_group_check=True)
            mm.then_inc(hg.filled, 1)
            yield

        def layer_tensor(pe, l, take_bank, turn, used):
            ident = cst("ident")
            n0 = len(FIRST)
            norm_sum(pe, take_bank, ly, "ss1", "squares1", l)

            def tiles(g, w, cs, src=ht, ks=KT, ready=None):
                b = take_bank(ly, g, l)
                for i, c in enumerate(cs):
                    for k in range(ks):
                        if ready and i == 0:
                            pe.wait_ge(sem(ready), l * KT + k + 1)
                        mm = pe.matmul(b[:, i * T:(i + 1) * T], w[:, k, c:c + P], src[:, k, :], start=k == 0, stop=k == ks - 1)
                mm.then_inc(ly.filled, 1)

            def tokens(g, w, c, n, m=None):
                b = take_bank(ly, g, l)
                for i, mm_ in enumerate((0, 1) if m is None else (m,)):
                    for k in range(KT):
                        mm = pe.matmul(b[:, i * n:(i + 1) * n], ht[:, k, mm_ * P:(mm_ + 1) * P], w[:, k, c:c + n],
                                       start=k == 0, stop=k == KT - 1)
                mm.then_inc(ly.filled, 1)

            w = use_chunk(pe, n0, l)
            tiles("qc0", w, (0, P), ready="h1_ready")
            tiles("qc1", w, (2 * P, 3 * P))
            used()
            w = use_chunk(pe, n0 + 1, l)
            tiles("kc", w, (0, P))
            tiles("qi", w, (2 * P, 3 * P))
            used()
            w = use_chunk(pe, n0 + 2, l)
            tokens("vc", w, 0, P)
            tiles("ki", w, (P,))
            tokens("wi", w, 2 * P, 4)
            b = take_bank(ly, "fl", l)
            for k in range(KT):
                mm = pe.matmul(b[0:8, 0:T], w[:, k, 260:268], ht[:, k, :], start=k == 0, stop=k == KT - 1)
            mm.then_inc(ly.filled, 1)
            used()
            pe.wait_ge(sem("const2_landed"), 16)
            for g, of, src in (("rqc0", "qc0", qcr[:, 0:2]), ("rqc1", "qc1", qcr[:, 2:4]), ("rkc", "kc", kc), ("rqi", "qi", qir)):
                ly.wait_emptied(pe, of, l)
                b = take_bank(ly, g, l)
                pe.matmul(b, cst("rot"), src.rearrange("p a t -> p (a t)"), start=True, stop=True).then_inc(ly.filled, 1)
            ly.wait_emptied(pe, "ki", l)
            b = take_bank(ly, "rki", l)
            pe.matmul(b[:, 0:T], cst("rot"), ki, start=True, stop=True).then_inc(ly.filled, 1)
            for i, x in enumerate(("qa", "ka", "va", "qb", "kb", "vb")):
                if x == "va":
                    pe.wait_ge(sem("roped"), l + 1)
                    for n, (m, hs) in enumerate(DOTS):
                        b = take_bank(ly, f"dot{n}", l)
                        width = P if m == 0 else T
                        for at, h in enumerate(hs):
                            mm = pe.matmul(b[:, at * width:(at + 1) * width], qi[:, h, m * P:(m + 1) * P], ki[:, 0:width],
                                           start=True, stop=True)
                        mm.then_inc(ly.filled, 1)
                w = use_chunk(pe, n0 + 3 + i, l)
                for n in range(2):
                    if x[0] == "v":
                        tokens(f"{x}{n}", w, 0, 512, n)
                    else:
                        tiles(f"{x}{n}", w, (2 * n * P, (2 * n + 1) * P))
                used()

            for i in range(len(STEPS) + 1):
                if i < len(STEPS):
                    kind, h = STEPS[i]
                    if i == 0:
                        ly.wait_emptied(pe, "vb1", l)
                        pe.wait_ge(sem("forget_ready"), l + 1)
                        b = take_bank(ly, "fct", l)
                        pe.sem_inc(sem("sums_met"), 1)
                        for m in range(2):
                            mm = turn(b[:, 8 * m:8 * m + 8], fc[0:8, m * P:(m + 1) * P])
                        mm.then_inc(ly.filled, 1)
                    q = {"A": qa, "B": qb, "C": qc}[kind][:, h]
                    kk = kc[:, h // 4] if kind == "C" else {"A": ka, "B": kb}[kind][:, h // 2]
                    b = take_bank(ly, f"z{i}", l)
                    for m, o, width in ((0, 0, P), (1, P, T)):
                        z = b[:, o:o + width]
                        mm = pe.matmul(z, q[:, m * P:(m + 1) * P], kk[:, 0:width], start=True, stop=kind != "B")
                        if kind == "B":
                            mm = pe.matmul(z, ident[:, h:h + 1].to_broadcast([P, P]), fn[:, 0:width], start=False, stop=True)
                    mm.then_inc(ly.filled, 1)
                    if i % 4 == 0:
                        w = use_chunk(pe, n0 + 9 + i // 4, l)
                    gate = take_bank(ly, f"gl{i}", l)

                def gate_tile(k0, k1):
                    for k in range(k0, k1):
                        mm = pe.matmul(gate[:, 0:T], w[:, k, i % 4 * P:(i % 4 + 1) * P], ht[:, k, :], start=k == 0, stop=k == KT - 1)
                    return mm

                if i < len(STEPS):
                    gate_tile(0, KT - 2)
                if i:
                    kind, h = STEPS[i - 1]
                    s = (i - 1) % 2
                    pe.wait_ge(sem("weights_ready"), l * len(STEPS) + i)
                    b = take_bank(ly, f"wT{i - 1}", l)
                    for n in range(3):
                        mm = turn(b[:, n * P:(n + 1) * P], wgt[:, s, n * P:(n + 1) * P])
                    mm.then_inc(ly.filled, 1)
                if i < len(STEPS):
                    gate_tile(KT - 2, KT).then_inc(ly.filled, 1)
                    if i % 4 == 3:
                        used()
                if i:
                    ly.wait_emptied(pe, f"wT{i - 1}", l)
                    b = take_bank(ly, f"o{i - 1}", l)
                    r = slice(h % 2 * HALF, h % 2 * HALF + HALF)
                    if kind == "C":
                        v = [vc[:, m, h // 4 * HALF:h // 4 * HALF + HALF] for m in range(2)]
                    else:
                        v = [(va if kind == "A" else vb)[:, m, h * HALF:(h + 1) * HALF] for m in range(2)]
                    pe.matmul(b[r, 0:T], v[0], wt[:, s, 0:T], start=True, stop=False, skip_group_check=True)
                    pe.matmul(b[r, P:T], v[1], wt[:, s, T:T + P], start=False, stop=True, skip_group_check=True).then_inc(ly.filled, 1)

            ly.wait_emptied(pe, f"o{len(STEPS) - 1}", l)
            for b_ in range(3):
                w = use_chunk(pe, n0 + N_IN + b_, l).rearrange("p k n -> p (k n)").rearrange("p (k n) -> p k n", n=D)
                for n in range(4):
                    tiles(f"br{b_}{n}", w, (2 * n * P, (2 * n + 1) * P), src=br[:, b_], ks=4)
                used()
            ly.wait_emptied(pe, "br23", l)
            for h in range(2):
                w = use_chunk(pe, n0 + N_IN + 3 + h, l)
                for n in range(2):
                    tiles(f"out{2 * h + n}", w, (2 * n * P, (2 * n + 1) * P), src=yy)
                used()
            norm_sum(pe, take_bank, ly, "ss2", "squares2", l)
            for c in range(8):
                w = use_chunk(pe, n0 + N_IN + 5 + c, l)
                for n in range(2):
                    tiles(f"up{2 * c + n}", w, (2 * n * P, (2 * n + 1) * P), ready=None if c or n else "h2_ready")
                used()
            pe.wait_ge(sem("hidden_ready"), l + 1)
            for h in range(2):
                bs = [take_bank(ly, f"dn{4 * h + t}", l) for t in range(4)]
                for c in range(4):
                    w = use_chunk(pe, n0 + N_IN + 13 + 4 * h + c, l)
                    for t in range(4):
                        for k in range(KT):
                            mm = pe.matmul(bs[t][:, 0:T], w[:, k, t * P:(t + 1) * P], hff[:, c * KT + k, :],
                                           start=c == 0 and k == 0, stop=c == 3 and k == KT - 1)
                        if c == 3:
                            mm.then_inc(ly.filled, 1)
                    used()

        @block.tensor
        def _(pe):
            ident, ones, blocks = cst("ident"), cst("ones"), cst("blocks")

            def used():
                pe.drain().then_inc(s_used, 1)

            def take_bank(b, g, it=0):
                b.wait_free(pe, g, it)
                return bank(b, g)

            def turn(dst, src):
                n = src.shape[0]
                return pe.transpose(dst, src, ident[0:n, 0:n])

            def parameter_columns():
                pe.wait_ge(s_in, 16 * N_SMALL)
                for g, st, n in (("colsA", stackA, ROWS_A), ("colsB", stackB, ROWS_B)):
                    turn(take_bank(setup, g)[:, 0:n], st[0:n, :]).then_inc(setup.filled, 1)

            def raw_latent():
                pe.wait_ge(sem("x_landed"), 32)
                for g in range(4):
                    b = take_bank(setup, f"xr{g}")
                    for k in range(2):
                        for m in range(2):
                            o = k * T + m * P
                            mm = turn(b[:, o:o + P], x4[:, 2 + m, (2 * g + k) * P:(2 * g + k + 1) * P])
                    mm.then_inc(setup.filled, 1)

            pe.wait_ge(s_const, 16)
            pe.wait_ge(sem("c_landed"), 32)
            turn(take_bank(setup, "colsC")[:, 0:16], stackC[0:16, :]).then_inc(setup.filled, 1)
            if first:
                pe.wait_ge(sem("silu_ready"), 1)
                for n in range(6):
                    if n == 4:
                        raw_latent()
                    w = use_chunk(pe, n)
                    b = take_bank(setup, f"mod{n}")
                    for k in range(KT):
                        mm = pe.matmul(b[0:2, :], silu_c[:, k, :], w[:, k, :], start=k == 0, stop=k == KT - 1)
                    mm.then_inc(setup.filled, 1)
                    used()
                parameter_columns()
                b = take_bank(setup, "modT")
                setup.wait_emptied(pe, "mod5")
                for t in range(24):
                    mm = turn(b[:, 2 * t:2 * t + 2], mrow[0:2, t * P:(t + 1) * P])
                mm.then_inc(setup.filled, 1)
                pe.wait_ge(s_tables, 16)
                pe.wait_ge(sem("tokens_normalised"), 1)
                for k in range(KT):
                    b = take_bank(setup, f"xt{k}")
                    for m in range(4):
                        mm = turn(b[:, m * P:(m + 1) * P], x4[:, m, k * P:(k + 1) * P])
                    mm.then_inc(setup.filled, 1)

                def project(g, w, c0, n0=0, n1=512):
                    b = take_bank(setup, g)
                    for k in range(KT):
                        if g == "fh0":
                            setup.wait_emptied(pe, f"xt{k}")
                        mm = pe.matmul(b[:, n0:n1], w[:, k, c0:c0 + P], xt[:, k, n0:n1], start=k == 0, stop=k == KT - 1)
                    return mm

                for chunk in range(3):
                    w = use_chunk(pe, 6 + chunk)
                    for t in range(4):
                        project(f"fh{4 * chunk + t}", w, t * P, T if 4 * chunk + t < JT else 0).then_inc(setup.filled, 1)
                    used()
                for chunk in range(3):
                    w = use_chunk(pe, 9 + chunk)
                    for t in range(4 if chunk < 2 else 3):
                        project(f"u{4 * chunk + t}", w, t * P, T if 4 * chunk + t < JT else 0).then_inc(setup.filled, 1)
                    used()
                w = use_chunk(pe, 12)
                for m in range(2):
                    b = take_bank(setup, f"pv{m}")
                    for k in range(KT):
                        mm = pe.matmul(b[:, 0:T], xt[:, k, T + m * P:T + (m + 1) * P], w[:, k, 0:T], start=k == 0, stop=k == KT - 1)
                    mm.then_inc(setup.filled, 1)
                used()
                for chunk in range(2):
                    w = use_chunk(pe, 13 + chunk)
                    for n in range(2):
                        b = take_bank(setup, f"g{2 * chunk + n}")
                        for t in range(2):
                            for k in range(KT):
                                mm = pe.matmul(b[:, t * T:(t + 1) * T], w[:, k, (2 * n + t) * P:(2 * n + t + 1) * P],
                                               xt[:, k, T:2 * T], start=k == 0, stop=k == KT - 1)
                        mm.then_inc(setup.filled, 1)
                    used()
                setup.wait_emptied(pe, "pv1")
                for n in range(2):
                    b = take_bank(setup, f"pool{n}")
                    for gg in range(2):
                        g = 2 * n + gg
                        for m in range(2):
                            mm = pe.matmul(b[gg * HALF:(gg + 1) * HALF, m * P:(m + 1) * P], pv[:, m, g * HALF:(g + 1) * HALF],
                                           cst(f"pool{g}"), start=True, stop=True)
                    mm.then_inc(setup.filled, 1)
                for n in range(2):
                    b = take_bank(setup, f"pmix{n}")
                    setup.wait_emptied(pe, f"pool{n}")
                    for gg in range(2):
                        h = slice(gg * HALF, (gg + 1) * HALF)
                        mm = pe.matmul(b[h, 0:T], pw[h, n, :], pooled[h, n, :], start=True, stop=True)
                    mm.then_inc(setup.filled, 1)
                setup.wait_all(pe)

                pe.wait_ge(sem("tanh_ready"), 1)
                for d in range(2):
                    r = slice(d * HALF, (d + 1) * HALF)
                    for jj in range(JT):
                        for x, w, src in (("w", wup, txw), ("a", aup, us[:, 10, :])):
                            b = take_bank(lora, f"{x}{d}{jj}")
                            pe.matmul(b, w[r, jj * P:(jj + 1) * P], src[r, :], start=True, stop=True).then_inc(lora.filled, 1)
                lora.wait_all(pe)

                rw.start(pe, "P")
                hg.start(pe, "P")
                with pe.Fori(0, JT) as j:
                    for d in range(2):
                        interleave(rwkv_tensor(pe, j, d, take_bank, turn), hgrn_tensor(pe, j, d, take_bank, turn))
                rw.wait_all(pe)
                hg.wait_all(pe)

                ys, os_ = [(yacc, 0, 2), (yacc, 2, 1)], [(oacc, 0, 2), (oacc, 2, 1)]
                for n, (src, j0, k) in enumerate(ys):
                    b = take_bank(rd, f"ysum{n}")
                    pe.matmul(b[:, 0:k * T], blocks, src[:, j0:j0 + k, :].rearrange("p j t -> p (j t)"),
                              start=True, stop=True).then_inc(rd.filled, 1)
                pe.wait_ge(sem("o_squared"), 1)
                for n, k in ((0, 2), (1, 1)):
                    b = take_bank(rd, f"osq{n}")
                    pe.matmul(b[:, 0:k * T], blocks, sqo[:, 2 * n * T:(2 * n + k) * T], start=True, stop=True).then_inc(rd.filled, 1)
                pe.wait_ge(sem("y_squared"), 1)
                for n, k in ((0, 2), (1, 1)):
                    b = take_bank(rd, f"yvar{n}")
                    pe.matmul(b[:, 0:k * T], blocks, sqr[:, 2 * n * T:(2 * n + k) * T], start=True, stop=True).then_inc(rd.filled, 1)
                for chunk in range(2):
                    w = use_chunk(pe, 15 + chunk)
                    bs = [take_bank(rd, f"wo{4 * chunk + t}") for t in range(4)]
                    for ks, ready in (((0, 1), None), ((5, 6, 7), "o_mixed"), ((2, 3, 4), "y_mixed")):
                        if ready and chunk == 0:
                            pe.wait_ge(sem(ready), 1)
                        for t in range(4):
                            for k in ks:
                                mm = pe.matmul(bs[t][:, 0:T], w[:, k, t * P:(t + 1) * P], mix[:, k, :], start=k == 0, stop=k == 4)
                            if ready == "y_mixed":
                                mm.then_inc(rd.filled, 1)
                    used()
                rd.wait_emptied(pe, f"wo{KT - 1}")
                b = take_bank(rd, "lnsum")
                for k in range(KT):
                    mm = pe.matmul(b[:, 0:T], ones, xr[:, k, :], start=k == 0, stop=k == KT - 1)
                mm.then_inc(rd.filled, 1)
                pe.wait_ge(sem("ln_squared"), 1)
                b = take_bank(rd, "lnvar")
                for k in range(KT):
                    mm = pe.matmul(b[:, 0:T], ones, mix[:, k, :], start=k == 0, stop=k == KT - 1)
                mm.then_inc(rd.filled, 1)
                rd.wait_all(pe)
            else:
                pe.sem_inc(s_used, len(FIRST))
                pe.wait_ge(setup.emptied["D"], 1)
                pe.sem_inc(setup.filled, 4)
                raw_latent()
                pe.wait_ge(setup.emptied["D"], 5)
                pe.sem_inc(setup.filled, 2)
                parameter_columns()
                pe.wait_ge(setup.emptied["D"], 7)

            if second:
                ly.start(pe, "P")
                with pe.Fori(0, LAYERS) as l:
                    layer_tensor(pe, l, take_bank, turn, used)
                ly.wait_all(pe)
                norm_sum(pe, take_bank, en, "ssf", "squares_f", 0)
                pe.wait_ge(sem("final_ready"), KT)
                for m in range(2):
                    for n in range(2):
                        b = take_bank(en, f"fin{m}{n}")
                        for k in range(4):
                            mm = turn(b[:, k * P:(k + 1) * P], ht[:, 4 * n + k, m * P:(m + 1) * P])
                        mm.then_inc(en.filled, 1)

        def norm_scalar(act, b, g, squares, l, done, emptied, wait):
            act.activation(rsq[:, 0:1], one_, ACT.Sqrt)
            for k in range(KT):
                wait(k)
                act.activation(sq[:, k, :], xr[:, k, :], ACT.Square)
                done(squares)
            b.wait_filled(act, g, l)
            emptied(b, act.activation(rsq, bank(b, g)[:, 0:T], ACT.Sqrt, bias=eps(NORM_EPS), scale=1.0 / D))

        def layer_scalar(act, l, copy, done, emptied):
            def out_of(g, dst, scale=1.0, n=2):
                ly.wait_filled(act, g, l)
                b = bank(ly, g)
                src = b[:, 0:n * T]
                emptied(ly, copy(dst, src.rearrange("p (a t) -> p a t", a=n) if n == 2 else src, scale))

            norm_scalar(act, ly, "ss1", "squares1", l, done, emptied, lambda k: ly.wait_emptied(act, f"dn{k}", l, before=1))
            out_of("qc0", qcr[:, 0:2])
            out_of("qc1", qcr[:, 2:4])
            out_of("kc", kc)
            out_of("qi", qir)
            ly.wait_filled(act, "vc", l)
            emptied(ly, copy(vc, bank(ly, "vc")[:, 0:T].rearrange("p (m n) -> p m n", m=2)))
            out_of("ki", ki, n=1)
            ly.wait_filled(act, "fl", l)
            act.wait_ge(sem("bias_column_ready"), l + 1)
            f8 = slice(0, 8)
            emptied(ly, act.activation(fs[f8], bank(ly, "fl")[f8, 0:T], ACT.Identity, bias=bcol[f8]))
            act.drain()
            act.activation(fe[f8], fs[f8], ACT.Abs)
            act.drain()
            act.activation(fe[f8], fe[f8], ACT.Exp, scale=-1.0)
            act.drain()
            act.activation(fe[f8], fe[f8], ACT.Ln, bias=one_[f8])
            done("forget_logs")
            act.wait_ge(sem("queries_cleared"), 1)
            for x, dst, scale in (("qa", qa, 1.0), ("ka", ka, 1.0), ("va", va, 1.0), ("qb", qb, 0.125), ("kb", kb, 1.0), ("vb", vb, 1.0)):
                if x == "va":
                    for n, (m, hs) in enumerate(DOTS):
                        width = P if m == 0 else T
                        ly.wait_filled(act, f"dot{n}", l)
                        b = bank(ly, f"dot{n}")[:, 0:len(hs) * width].rearrange("p (h s) -> p h s", s=width)
                        emptied(ly, act.activation(rdots[:, hs[0]:hs[-1] + 1, m * P:m * P + width], b, ACT.Relu, scale=0.125))
                    done("dots_ready")
                for n in range(2):
                    if x[0] == "v":
                        ly.wait_filled(act, f"{x}{n}", l)
                        emptied(ly, copy(dst[:, n, :], bank(ly, f"{x}{n}")))
                    elif x[0] == "q":
                        ly.wait_filled(act, f"{x}{n}", l)
                        for par in range(2):
                            r = slice(par * HALF, (par + 1) * HALF)
                            ins = copy(dst[r, 4 * n + par:4 * n + 4:2], bank(ly, f"{x}{n}")[r].rearrange("p (a t) -> p a t", a=2), scale)
                        emptied(ly, ins)
                    else:
                        out_of(f"{x}{n}", dst[:, 2 * n:2 * n + 2], scale)

            def weights_out(i):
                ly.wait_filled(act, f"wT{i}", l)
                emptied(ly, copy(wt[:, i % 2, :], bank(ly, f"wT{i}")[:, 0:384]))

            def values_out(i):
                kind, h = STEPS[i]
                ly.wait_filled(act, f"o{i}", l)
                r = slice(h % 2 * HALF, h % 2 * HALF + HALF)
                emptied(ly, copy(br[r, "ABC".index(kind), h // 2, :], bank(ly, f"o{i}")[r, 0:T]))

            for i in range(len(STEPS) + 1):
                if i < len(STEPS):
                    kind, h = STEPS[i]
                    s = i % 2
                    if kind == "A":
                        ly.wait_filled(act, f"z{i}", l)
                        if i >= 2:
                            act.wait_ge(sem("weights_ready"), l * len(STEPS) + i - 1)
                        b = bank(ly, f"z{i}")[:, 0:384]
                        act.activation(pp[:, s, :], b, ACT.Sigmoid, scale=-0.125)
                        emptied(ly, act.activation(sg[:, s, :], b, ACT.Sigmoid, scale=0.125))
                    else:
                        act.wait_ge(sem("scores_ready"), l * 16 + (i + 1 if kind == "B" else i - 7))
                        if i >= 2:
                            act.wait_ge(sem("weights_ready"), l * len(STEPS) + i - 1)
                        act.activation(pp[:, s, 0:P], zm[:, s, 0:P], ACT.Exp, bias=nmx[:, s, 0:1], accum_out=sums[:, s, 0:1])
                        act.activation(pp[:, s, P:384], zm[:, s, P:384], ACT.Exp, bias=nmx[:, s, 1:2], accum_out=sums[:, s, 1:2])
                        done("exps_ready")
                if i:
                    weights_out(i - 1)
                if i < len(STEPS):
                    ly.wait_filled(act, f"gl{i}", l)
                    emptied(ly, act.activation(gt[:, i, :], bank(ly, f"gl{i}")[:, 0:T], ACT.Tanh, scale=0.5))
                if i:
                    values_out(i - 1)
            norm_scalar(act, ly, "ss2", "squares2", l, done, emptied, lambda k: ly.wait_emptied(act, f"out{k // 2}", l))
            for n in range(16):
                ly.wait_filled(act, f"up{n}", l)
                emptied(ly, act.activation(hff[:, 2 * n:2 * n + 2, :], bank(ly, f"up{n}").rearrange("p (a t) -> p a t", a=2), ACT.Relu))

        def rwkv_scalar(act, j, d, copy, done, emptied):
            if d:
                rw.wait_filled(act, "y30", j)
            else:
                rw.wait_filled(act, "y31", j, before=1)
            act.wait_ge(sem(f"r_columns{d}"), j + 1)
            act.sem_inc(sem("turns_begun"), 1)
            copy(flip(rlk, d), pair(us, j + 3))
            copy(flip(rlv, d), pair(us, j + 6))
            copy(seqs(rsw), pair(sa[:, 0], 3 * d + j))
            copy(seqs(rla), pair(sa[:, 1], 3 * d + j))
            copy(flip(rlr, d), pair(us[:, :, T:2 * T], j))
            done(f"r_loaded{d}")
            act.activation(rn, rlk, ACT.Square, scale=pc[:, 0:1])
            done(f"r_squared{d}")
            yield
            rw.wait_filled(act, f"kk{d}", j)
            emptied(rw, act.activation(rn, bank(rw, f"kk{d}"), ACT.Ln, bias=eps(1e-12)))
            act.drain()
            act.activation(rn, rn, ACT.Exp, scale=-0.5)
            done(f"r_norm{d}")
            act.wait_ge(sem(f"r_cumulated{d}"), j + 1)
            act.activation(pinc, rl, ACT.Exp, scale=-DECAY)
            act.activation(pinv, rl, ACT.Exp, scale=DECAY)
            act.activation(pexc, rsw, ACT.Exp, scale=-DECAY)
            act.activation(e2, mid, ACT.Exp, scale=-DECAY)
            done(f"r_decays{d}")
            for g, dst in (("ktok", rkt), ("btok", rbt), ("vtok", rvt)):
                rw.wait_filled(act, f"{g}{d}", j)
                emptied(rw, copy(dst.rearrange("p c t -> p (c t)"), bank(rw, f"{g}{d}")))
            yield
            yield
            for l in range(1, 7):
                for g in range(2):
                    rw.wait_filled(act, f"w{l}{g}{d}", j)
                    emptied(rw, copy(ww[:, 4 * g:4 * g + 4, :], bank(rw, f"w{l}{g}{d}").rearrange("p (u t) -> p u t", u=4)))
                yield
            for c in range(4):
                rw.wait_filled(act, f"rhs{c}{d}", j)
                emptied(rw, copy(rrhs, bank(rw, f"rhs{c}{d}")[:, 0:P]))
                rw.wait_filled(act, f"u{c}{d}", j)
                emptied(rw, copy(ru, bank(rw, f"u{c}{d}")[:, 0:P]))
                yield

        def hgrn_scalar(act, j, d, copy, done, emptied):
            if d:
                hg.wait_filled(act, "o0", j)
            else:
                hg.wait_filled(act, "o1", j, before=1)
            act.sem_inc(sem("turns_begun"), 1)
            act.activation(flip(lk, d), pair(hz, 3 * d + j), ACT.Sigmoid, scale=-1.0)
            act.activation(flip(pi, d), pair(hz, 3 * d + j), ACT.Sigmoid)
            copy(flip(li, d), pair(hi, j))
            copy(flip(lq, d), pair(hq, j))
            done(f"h_loaded{d}")
            hg.wait_filled(act, f"itok{d}", j)
            emptied(hg, copy(itok.rearrange("p c t -> p (c t)"), bank(hg, f"itok{d}")))
            yield
            for l in range(7):
                yield
            for h in range(2):
                hg.wait_filled(act, f"cross{h}{d}", j)
                emptied(hg, copy(cross[:, h, :], bank(hg, f"cross{h}{d}")[:, 0:P]))
            yield
            hg.wait_filled(act, f"ktok{d}", j)
            emptied(hg, copy(ktok.rearrange("p c t -> p (c t)"), bank(hg, f"ktok{d}")[:, 0:2 * P]))
            yield
            yield

        @block.scalar
        def _(act):
            def copy(dst, src, scale=1.0):
                return act.activation(dst, src, ACT.Copy, scale=scale)

            def done(name):
                act.drain().then_inc(sem(name), 1)

            def emptied(b, ins):
                ins.then_inc(b.emptied["A"], 1)

            def angles():
                act.wait_ge(sem("angles_ready"), 1)
                act.activation(sin, ht_flat(0), ACT.Sin)
                act.activation(cos, ht_flat(1), ACT.Sin)
                done("rotary_ready")

            for n, name in enumerate(("c", "c_ctx")):
                v = a[name] if name == "c_ctx" else a[name].rearrange("b n -> (b n)")
                act.dma_start(stackC[KT * n:KT * (n + 1), :], v.rearrange("(t p) -> t p", p=P)).then_inc(sem("c_landed"), 16)
            for n, name in enumerate(("ctx", "x")):
                act.dma_start(x4[:, 2 * n:2 * n + 2, :], a[name][0].rearrange("(m p) d -> p m d", p=P)).then_inc(sem("x_landed"), 16)
            if first:
                act.wait_ge(sem("c_columns"), 1)
                act.activation(silu_c, ccol.rearrange("p s k -> p k s"), ACT.Silu)
                done("silu_ready")
                act.wait_ge(sem("stats_ready"), 1)
                act.activation(rstd4.unsqueeze(2), mv[:, :, 1:2], ACT.Sqrt, bias=eps(LN_EPS))
                done("std_ready")
                for n in range(6):
                    setup.wait_filled(act, f"mod{n}")
                    emptied(setup, copy(mrow[0:2, 512 * n:512 * n + 512], bank(setup, f"mod{n}")[0:2, :]))
                angles()
                act.wait_ge(sem("modulation_ready"), 1)
                for k in range(KT):
                    setup.wait_filled(act, f"xt{k}")
                    b = bank(setup, f"xt{k}")
                    for s in range(2):
                        ins = act.activation(xt[:, k, s * T:(s + 1) * T], b[:, s * T:(s + 1) * T], ACT.Identity,
                                             bias=modc[:, k, 1 - s:2 - s], scale=modc[:, KT + k, 1 - s:2 - s])
                    emptied(setup, ins)
                act.wait_ge(sem("lb_shifted"), 1)
                act.activation(lbw, lbw, ACT.Exp)
                done("lb_exp")
                for t in range(12):
                    setup.wait_filled(act, f"fh{t}")
                    b = bank(setup, f"fh{t}")
                    if t < 3:
                        ins = copy(hq[:, t, :], b[:, T:2 * T])
                    elif t < 6:
                        ins = copy(hi[:, t - 3, :], b)
                    else:
                        ins = copy(hz[:, t - 6, :], b)
                    emptied(setup, ins)
                for n in range(4):
                    setup.wait_filled(act, f"g{n}")
                    emptied(setup, act.activation(mix[:, 2 * n:2 * n + 2, :], bank(setup, f"g{n}").rearrange("p (a t) -> p a t", a=2), ACT.Silu))
                for n in range(2):
                    setup.wait_filled(act, f"pool{n}")
                    emptied(setup, copy(pooled[:, n, :], bank(setup, f"pool{n}")[:, 0:T]))

                setup.wait_all(act)
                act.wait_ge(sem("shifted"), 1)
                act.activation(txw, us[:, 9, :], ACT.Tanh)
                done("tanh_ready")
                for d in range(2):
                    for jj in range(JT):
                        for x, kind, name in (("w", 0, "rwkv_w0"), ("a", 1, "rwkv_a0")):
                            lora.wait_filled(act, f"{x}{d}{jj}")
                            emptied(lora, act.activation(flip(sa[:, kind, 3 * d + jj, :], d), seqs(bank(lora, f"{x}{d}{jj}")),
                                                         ACT.Sigmoid, bias=col(name, 3 * d + jj)))
                act.drain()
                rw.start(act, "A")
                hg.start(act, "A")
                with act.Fori(0, JT) as j:
                    for d in range(2):
                        interleave(rwkv_scalar(act, j, d, copy, done, emptied), hgrn_scalar(act, j, d, copy, done, emptied))

                rw.wait_all(act)
                hg.wait_all(act)
                act.activation(sqo, oacc.rearrange("p j t -> p (j t)"), ACT.Square)
                done("o_squared")
                act.wait_ge(sem("y_centred"), 1)
                act.activation(sqr, yc, ACT.Square)
                done("y_squared")
                for x, dst, e, ready in (("osq", rso, RMS_EPS, "o_scales"), ("yvar", rsd, GN_EPS, "y_scales")):
                    for n, k in ((0, 2), (1, 1)):
                        rd.wait_filled(act, f"{x}{n}")
                        emptied(rd, act.activation(dst[:, 2 * n * T:(2 * n + k) * T], bank(rd, f"{x}{n}")[:, 0:k * T], ACT.Ln,
                                                   bias=eps(e), scale=1.0 / HALF))
                    act.drain()
                    act.activation(dst, dst, ACT.Exp, scale=-0.5)
                    done(ready)
                act.wait_ge(sem("ln_centred"), 1)
                act.activation(mix, xr, ACT.Square)
                done("ln_squared")
                rd.wait_filled(act, "lnvar")
                emptied(rd, act.activation(rl[:, 0:T], bank(rd, "lnvar")[:, 0:T], ACT.Sqrt, bias=eps(LN_EPS), scale=1.0 / D))

            else:
                angles()

            if second:
                act.wait_ge(sem("residual_ready"), 1)
                ly.start(act, "A")
                with act.Fori(0, LAYERS) as l:
                    layer_scalar(act, l, copy, done, emptied)
                norm_scalar(act, en, "ssf", "squares_f", 0, done, emptied,
                            lambda k: ly.wait_emptied(act, f"dn{k}", LAYERS, before=1))
                for m in range(2):
                    for n in range(2):
                        en.wait_filled(act, f"fin{m}{n}")
                        emptied(en, copy(fin[:, m, n * 512:(n + 1) * 512], bank(en, f"fin{m}{n}")))

        def normed(dve, gain, fence, done, ready):
            dve.reciprocal(rsq, rsq)
            fence()
            for k in range(KT):
                dve.scalar_tensor_tensor(ht[:, k, :], xr[:, k, :], gain[:, k:k + 1], rsq, ALU.mult, ALU.mult)
                done(ready)

        def first_vector(dve, done, emptied, bc, fence, held):
            setup.wait_filled(dve, "modT")
            mb = cols[:, COL["mod_b"]:COL["mod_b"] + 24]
            emptied(setup, dve.tensor_tensor(modc, bank(setup, "modT")[:, 0:48].rearrange("p (a b) -> p a b", b=2),
                                             mb.unsqueeze(2).to_broadcast([P, 24, 2]), ALU.add))
            fence()
            dve.tensor_scalar(modc[:, KT:2 * KT, :], modc[:, KT:2 * KT, :], 1.0, None, ALU.add)
            done("modulation_ready")
            lg = cols[:, COL["hgrn_lb_logits"]:COL["hgrn_lb_logits"] + 6]
            dve.tensor_tensor(lbw, lg, lg, ALU.subtract)
            done("lb_shifted")
            dve.wait_ge(sem("lb_exp"), 1)
            dve.reciprocal(lb_inv, lbw)
            fence()
            dve.tensor_tensor(lbw, lbw, lb_inv, ALU.mult)
            fence()
            dve.tensor_tensor(lbw, lbw, lbw, ALU.subtract)
            fence()
            dve.tensor_scalar(lbc[:, :, 0:1], lbw.unsqueeze(2), 0.0, None, ALU.max)
            fence()
            dve.tensor_scalar(lbc[:, :, 1:2], lbc[:, :, 0:1], -1.0, 1.0, ALU.mult, ALU.add)
            dve.wait_ge(sem("rotary_ready"), 1)
            for t in range(11):
                setup.wait_filled(dve, f"u{t}")
                b, u = seqs(bank(setup, f"u{t}")), seqs(us[:, t, :])
                if t < JT:
                    b, u = b[:, 1:2], u[:, 1:2]
                dve.tensor_scalar(u, b, col("rwkv_shift", 11 + t), None, ALU.mult)
                fence()
                dve.scalar_tensor_tensor(u[:, :, 1:], b[:, :, :T - 1], col("rwkv_shift", t), u[:, :, 1:], ALU.mult, ALU.add)
                fence()
                emptied(setup, dve.scalar_tensor_tensor(u[:, :, :T - 1], b[:, :, 1:], col("rwkv_shift", 22 + t), u[:, :, :T - 1],
                                                        ALU.mult, ALU.add))
            done("shifted")
            for m in range(2):
                setup.wait_filled(dve, f"pv{m}")
                emptied(setup, dve.tensor_copy(pv[:, m, :], bank(setup, f"pv{m}")[:, 0:T]))
            for n in range(2):
                setup.wait_filled(dve, f"pmix{n}")
                emptied(setup, dve.scalar_tensor_tensor(mix[:, n, :], bank(setup, f"pmix{n}")[:, 0:T], col("pool_scale", n),
                                                        mix[:, n, :], ALU.mult, ALU.mult))
            for n, name in enumerate(("rwkv_k_k", "rwkv_k_a", "rwkv_k_a")):
                dve.tensor_copy(rc[:, :, n:n + 1], cols[:, COL[name]:COL[name] + JT].unsqueeze(2))
            for d in range(2):
                o = COL["rwkv_r_k"] + JT * d
                dve.tensor_copy(rc[:, :, 3 + d:4 + d], cols[:, o:o + JT].unsqueeze(2))
            fence()
            dve.tensor_scalar(rc[:, :, 2:3], rc[:, :, 2:3], -1.0, 1.0, ALU.mult, ALU.add)

            for v in (nlb, lkm, akm, abm):
                dve.memset(v, 0.0)
            fence()
            rw.start(dve, "D")
            hg.start(dve, "D")
            with dve.Fori(0, JT) as j:
                for d in range(2):
                    interleave(rwkv_vector(dve, j, d, done, emptied, bc, fence, held),
                               hgrn_vector(dve, j, d, done, emptied, bc, fence, held))

            rw.wait_all(dve)
            done("heads_done")
            yflat, bflat = yacc.rearrange("p j t -> p (j t)"), bon.rearrange("p j t -> p (j t)")
            for n, k in ((0, 2), (1, 1)):
                rd.wait_filled(dve, f"ysum{n}")
                r = slice(2 * n * T, (2 * n + k) * T)
                emptied(rd, dve.scalar_tensor_tensor(yc[:, r], bank(rd, f"ysum{n}")[:, 0:k * T], -1.0 / HALF, yflat[:, r], ALU.mult, ALU.add))
            done("y_centred")
            dve.tensor_scalar(xr, xr, ALPHA, None, ALU.mult)
            dve.wait_ge(sem("o_scales"), 1)
            dve.tensor_tensor(rso, rso, oacc.rearrange("p j t -> p (j t)"), ALU.mult)
            fence()
            for jj in range(JT):
                dve.scalar_tensor_tensor(mix[:, 5 + jj, :], rso[:, jj * T:(jj + 1) * T], col("hgrn_norm_g", jj), mix[:, 5 + jj, :],
                                         ALU.mult, ALU.mult)
            done("o_mixed")
            dve.wait_ge(sem("y_scales"), 1)
            dve.tensor_tensor(yc, yc, rsd, ALU.mult)
            fence()
            for jj in range(JT):
                r = slice(jj * T, (jj + 1) * T)
                dve.tensor_scalar(yc[:, r], yc[:, r], col("rwkv_gn_g", jj), col("rwkv_gn_b", jj), ALU.mult, ALU.add)
            fence()
            dve.tensor_tensor(yc, yc, bflat, ALU.add)
            fence()
            dve.tensor_tensor(mix[:, 2:5, :], mix[:, 2:5, :], yc.rearrange("p (j t) -> p j t", t=T), ALU.mult)
            done("y_mixed")
            for k in range(KT):
                rd.wait_filled(dve, f"wo{k}")
                emptied(rd, dve.scalar_tensor_tensor(xr[:, k, :], bank(rd, f"wo{k}")[:, 0:T], modc[:, 2 * KT + k, 0:1], xr[:, k, :],
                                                     ALU.mult, ALU.add))
            rd.wait_filled(dve, "lnsum")
            fence()
            emptied(rd, dve.scalar_tensor_tensor(xr, bc(bank(rd, "lnsum")[:, 0:T], KT), -1.0 / D, xr, ALU.mult, ALU.add))
            done("ln_centred")
            rd.wait_emptied(dve, "lnvar")
            dve.reciprocal(rl[:, 0:T], rl[:, 0:T])
            fence()
            dve.tensor_tensor(xr, xr, bc(rl[:, 0:T], KT), ALU.mult)
            fence()
            for k in range(KT):
                dve.tensor_scalar(xr[:, k, :], xr[:, k, :], col("ln_g", k), col("ln_b", k), ALU.mult, ALU.add)
            done("residual_ready")

        def hgrn_vector(dve, j, d, done, emptied, bc, fence, held):
            dve.tensor_copy(lbp, lbc[:, bass.ds(3 * d + j, 1), :].rearrange("p a b -> p (a b)"))
            dve.wait_ge(sem(f"h_loaded{d}"), j + 1)
            dve.memset(se, 1.0)
            fence()
            dve.tensor_scalar(pi, pi, lbp[:, 1:2], lbp[:, 0:1], ALU.mult, ALU.add)
            dve.tensor_scalar(lk, lk, lbp[:, 1:2], None, ALU.mult)
            fence()

            def operands(l):
                s = l % 2
                tok = slice(T, 2 * T) if l < 8 else slice(0, T)
                dve.tensor_tensor(ql[:, s], lq, pi[:, T:2 * T], ALU.mult)
                dve.tensor_tensor(kl[:, s], lk[:, tok], se[:, tok], ALU.mult)
                done("h_level_ready")

            operands(0)
            for h in range(2):
                hg.wait_filled(dve, f"diag{h}{d}", j)
                emptied(hg, dve.tensor_tensor(acc[:, 2 * h:2 * h + 2], flat2_(bank(hg, f"diag{h}{d}")[:, 0:T]),
                                              bc(cst("ident"), 2), ALU.mult))
            yield
            for l in range(8):
                n = 1 << l
                pv_ = pi.rearrange("p (n h b) -> p n h b", h=2, b=n)
                sv_ = se.rearrange("p (n h b) -> p n h b", h=2, b=n)
                blocks = T // n
                end = pv_[:, :, 1, n - 1:n].to_broadcast([P, blocks, n])
                dve.tensor_tensor(sv_[:, :, 0, :], sv_[:, :, 0, :], end, ALU.mult)
                fence()
                end = pv_[:, :, 0, n - 1:n].to_broadcast([P, blocks, n])
                dve.tensor_tensor(pv_[:, :, 1, :], pv_[:, :, 1, :], end, ALU.mult)
                fence()
                operands(l + 1)
                if l < 7:
                    for h in range(2):
                        held(hg, f"lev{l}{h}{d}", j)
                        emptied(hg, dve.copy_predicated(acc[:, 2 * h:2 * h + 2], bc(cst_int(f"up{l}"), 2),
                                                        flat2_(bank(hg, f"lev{l}{h}{d}")[:, 0:T])))
                yield
            hg.wait_filled(dve, f"state{d}", j)
            emptied(hg, dve.tensor_tensor(hstate, bank(hg, f"state{d}")[:, 0:P], cst("blocks"), ALU.mult))
            yield
            hg.wait_filled(dve, f"o{d}", j)
            o = oacc[:, bass.ds(j, 1), :].rearrange("p a t -> p (a t)")
            b = bank(hg, f"o{d}")[:, 0:T]
            if d == 0:
                emptied(hg, dve.tensor_copy(o, b))
            else:
                emptied(hg, dve.tensor_tensor(o, b[:, ::-1], o, ALU.add))
            fence()
            yield

        def rwkv_vector(dve, j, d, done, emptied, bc, fence, held):
            dve.tensor_copy(pc, rc[:, bass.ds(j, 1), :].rearrange("p a b -> p (a b)"))
            done(f"r_columns{d}")
            dve.wait_ge(sem(f"r_loaded{d}"), j + 1)
            dve.memset(rs, 0.0)
            done(f"r_state_zero{d}")
            dve.tensor_copy(xi, bc(cst("ident"), 8))
            dve.tensor_copy(xti, bc(cst("ident"), 8))
            dve.tensor_scalar(kkr, rlk, pc[:, 0:1], None, ALU.mult)
            dve.tensor_scalar(km, rla, pc[:, 1:2], pc[:, 2:3], ALU.mult, ALU.add)
            dve.tensor_tensor_scan(rl, cst("keep"), rsw, 0.0, ALU.mult, ALU.add)
            fence()
            dve.tensor_tensor(km, km, rlk, ALU.mult)
            dve.tensor_copy(mid, rl[:, HALF - 1::P])
            fence()
            rlv_ = rl.rearrange("p (c t) -> p c t", t=P)
            dve.tensor_tensor(rlv_, rlv_, mid.unsqueeze(2).to_broadcast([P, 4, P]), ALU.subtract)
            fence()
            dve.tensor_tensor(rsw, rl, rsw, ALU.subtract)
            done(f"r_cumulated{d}")
            yield
            dve.wait_ge(sem(f"r_norm{d}"), j + 1)
            dve.tensor_tensor(kkr, kkr, rn, ALU.mult)
            fence()
            dve.tensor_tensor(rla, kkr, rla, ALU.mult)
            dve.scalar_tensor_tensor(rn[:, 0:T], rlr, pc[:, 3 + d:4 + d], km[:, T:2 * T], ALU.mult, ALU.mult)
            fence()
            dve.wait_ge(sem(f"r_decays{d}"), j + 1)
            dve.tensor_tensor(pexc, kkr, pexc, ALU.mult)
            dve.tensor_tensor(km, km, pinv, ALU.mult)
            dve.scalar_tensor_tensor(rla, rla, -1.0, pinv, ALU.mult, ALU.mult)
            dve.tensor_tensor(rlr, rlr, pinc[:, T:2 * T], ALU.mult)
            dve.tensor_tensor(e1[:, 0:3], pinc[:, P - 1:3 * P:P], e2[:, 1:4], ALU.mult)
            done(f"r_operands{d}")
            rw.wait_filled(dve, f"bonus{d}", j)
            b = bank(rw, f"bonus{d}")[:, 0:T]
            o = bon[:, bass.ds(j, 1), :].rearrange("p a t -> p (a t)")
            if d == 0:
                emptied(rw, dve.tensor_tensor(o, b, rlv[:, T:2 * T], ALU.mult))
            else:
                emptied(rw, dve.tensor_tensor(kkr[:, 0:T], b, rlv[:, T:2 * T], ALU.mult))
                fence()
                dve.tensor_tensor(o, kkr[:, 0:T][:, ::-1], o, ALU.add)
            yield

            def put(dst, mask, g):
                n = dst.shape[1]
                return dve.copy_predicated(dst, bc(cst_int(mask), n), flat2_(bank(rw, g)[:, 0:n * P]))

            for g in range(2):
                held(rw, f"lbT{g}{d}", j)
                emptied(rw, put(xi[:, 4 * g:4 * g + 4], "up0", f"lbT{g}{d}"))
            for g in range(2):
                held(rw, f"lb{g}{d}", j)
                put(nlb[:, 4 * g:4 * g + 4], "after", f"lb{g}{d}")
                emptied(rw, put(xti[:, 4 * g:4 * g + 4], "down0", f"lb{g}{d}"))
            for g in range(2):
                held(rw, f"lk{g}{d}", j)
                emptied(rw, put(lkm[:, 4 * g:4 * g + 4], "before", f"lk{g}{d}"))
            for name, dst in (("ak", akm), ("ab", abm)):
                for g in range(2):
                    held(rw, f"{name}{g}{d}", j)
                    emptied(rw, put(dst[:, 2 * g:2 * g + 2], "upto", f"{name}{g}{d}"))
            yield
            for l in range(1, 7):
                for g in range(2):
                    fence()
                    held(rw, f"x{l}{g}{d}", j)
                    emptied(rw, put(xi[:, 4 * g:4 * g + 4], f"up{l}", f"x{l}{g}{d}"))
                    if l < 6:
                        held(rw, f"xt{l}{g}{d}", j)
                        emptied(rw, put(xti[:, 4 * g:4 * g + 4], f"down{l}", f"xt{l}{g}{d}"))
                yield
            for c in range(4):
                if c >= 2:
                    rw.wait_filled(dve, f"y{c}{d}", j)
                    b = bank(rw, f"y{c}{d}")[:, 0:P]
                    q = c - 2 if d == 0 else 3 - c
                    o = yacc[:, bass.ds(j, 1), q * P:(q + 1) * P].rearrange("p a t -> p (a t)")
                    if d == 0:
                        emptied(rw, dve.tensor_copy(o, b))
                    else:
                        emptied(rw, dve.tensor_tensor(o, b[:, ::-1], o, ALU.add))
                if c < 3:
                    fence()
                    rw.wait_filled(dve, f"s{c}{d}", j)
                    dve.tensor_tensor(stmp, bank(rw, f"s{c}{d}")[:, 0:P], rs, ALU.add)
                    fence()
                    emptied(rw, dve.scalar_tensor_tensor(rs, stmp, e1[:, c:c + 1], cst("blocks"), ALU.mult, ALU.mult))
                yield

        def layer_vector(dve, l, done, emptied, bc, fence):
            for n, name in enumerate(("g_mix_2", "g_mlp_2")):
                dve.tensor_copy(gcol[:, n, :], cols[:, bass.ds(l * KT + COL[name], KT)])
            dve.tensor_copy(bcol[0:8], bf[0:8, bass.ds(l, 1)])
            done("bias_column_ready")
            ly.wait_emptied(dve, "ss1", l)
            normed(dve, gcol[:, 0, :], fence, done, "h1_ready")
            ly.wait_filled(dve, "wi", l)
            emptied(ly, dve.tensor_scalar(wi, bank(ly, "wi")[:, 0:8].rearrange("p (m h) -> p m h", h=4), 0.5, None, ALU.mult))
            dve.wait_ge(sem("const2_landed"), 16)
            dve.wait_ge(sem("queries_cleared"), 1)
            for g, x, n, dst in (("rqc0", qcr[:, 0:2], 2, qc[:, 0:4]), ("rqc1", qcr[:, 2:4], 2, qc[:, 4:8]), ("rkc", kc, 2, None),
                                 ("rqi", qir, 2, qi), ("rki", ki.unsqueeze(1), 1, None)):
                ly.wait_filled(dve, g, l)
                rt = rot_t[:, 0:n * T].rearrange("p (a t) -> p a t", t=T)
                emptied(ly, dve.tensor_tensor(rt, bank(ly, g)[:, 0:n * T].rearrange("p (a t) -> p a t", t=T), bc(sin, n), ALU.mult))
                dve.tensor_tensor(x, x, bc(cos, n), ALU.mult)
                fence()
                if dst is None:
                    dve.tensor_tensor(x, x, rt, ALU.add)
                else:
                    for par in range(2):
                        r = slice(par * HALF, (par + 1) * HALF)
                        dve.tensor_tensor(dst[r, par::2], x[r], rt[r], ALU.add)
                fence()
            done("roped")
            dve.wait_ge(sem("forget_logs"), l + 1)
            f8 = slice(0, 8)
            dve.scalar_tensor_tensor(fe[f8], fs[f8], 0.0, fe[f8], ALU.min, ALU.subtract)
            fence()
            dve.tensor_tensor_scan(fc[f8], fe[f8], zeros[f8], 0.0, ALU.add, ALU.add)
            fence()
            dve.tensor_scalar(fn[f8], fc[f8], -1.0, None, ALU.mult)
            done("forget_ready")
            dve.wait_ge(sem("dots_ready"), l + 1)
            tiles = ((0, 0, P), (1, P, T))
            for h in range(4):
                for m, o, w in tiles:
                    v = score[:, o:o + w]
                    if h == 0:
                        dve.tensor_scalar(v, rdots[:, 0, o:o + w], wi[:, m, 0:1], None, ALU.mult)
                    else:
                        dve.scalar_tensor_tensor(v, rdots[:, h, o:o + w], wi[:, m, h:h + 1], v, ALU.mult, ALU.add)
                fence()
            dve.tensor_tensor(wk, score, cst("causal"), ALU.add)
            for _ in range(TOPK // 8):
                fence()
                for m, o, w in tiles:
                    dve.max(top8[:, m, :], wk[:, o:o + w])
                fence()
                for m, o, w in tiles:
                    dve.match_replace(wk[:, o:o + w], top8[:, m, :], wk[:, o:o + w], TAKEN)
            fence()
            dve.tensor_scalar(bias_c, wk, TAKEN, NEG, ALU.not_equal, ALU.mult)
            fence()
            dve.tensor_tensor(bias_c, bias_c, cst("causal"), ALU.add)
            ly.wait_filled(dve, "fct", l)
            emptied(ly, dve.tensor_copy(fct, bank(ly, "fct")[:, 0:16].rearrange("p (m h) -> p m h", m=2)))
            fence()

            def masked(i):
                kind, h = STEPS[i]
                s = i % 2
                ly.wait_filled(dve, f"z{i}", l)
                b = bank(ly, f"z{i}")[:, 0:384]
                if kind == "B":
                    for m, o, w in tiles:
                        ins = dve.scalar_tensor_tensor(zm[:, s, o:o + w], b[:, o:o + w], fct[:, m, h:h + 1],
                                                       cst("causal")[:, o:o + w], ALU.add, ALU.add)
                    emptied(ly, ins)
                else:
                    emptied(ly, dve.scalar_tensor_tensor(zm[:, s, :], b, 0.125, bias_c, ALU.mult, ALU.add))
                fence()
                for m, o, w in tiles:
                    dve.tensor_reduce(nmx[:, s, m:m + 1], zm[:, s, o:o + w], AX, ALU.max, negate=True)
                done("scores_ready")

            def finish(i):
                kind, _ = STEPS[i]
                s = i % 2
                if kind == "A":
                    ly.wait_emptied(dve, f"z{i}", l)
                    dve.tensor_tensor(pp[:, s, :], pp[:, s, :], cst("unstrict"), ALU.max)
                    dve.tensor_tensor(sg[:, s, :], sg[:, s, :], cst("strict"), ALU.mult)
                    fence()
                    for m, o, w in tiles:
                        dve.tensor_tensor_scan(zm[:, s, o:o + w][:, ::-1], pp[:, s, o:o + w][:, ::-1], zeros[:, 0:w], 1.0,
                                               ALU.mult, ALU.add)
                    fence()
                else:
                    dve.wait_ge(sem("exps_ready"), l * 16 + (i + 1 if kind == "B" else i - 7))
                    dve.reciprocal(rsum[:, s, :], sums[:, s, :])
                    fence()
                if i >= 2:
                    ly.wait_filled(dve, f"wT{i - 2}", l)
                if kind == "A":
                    dve.tensor_tensor(wgt[:, s, 0:383], sg[:, s, 0:383], zm[:, s, 1:384], ALU.mult)
                    dve.memset(wgt[:, s, 383:384], 0.0)
                else:
                    for m, o, w in tiles:
                        dve.tensor_scalar(wgt[:, s, o:o + w], pp[:, s, o:o + w], rsum[:, s, m:m + 1], None, ALU.mult)
                done("weights_ready")

            for i in range(len(STEPS) + 1):
                if i < len(STEPS) and STEPS[i][0] != "A":
                    masked(i)
                if i:
                    finish(i - 1)
            for b_ in range(3):
                for n in range(4):
                    g = f"br{b_}{n}"
                    ly.wait_filled(dve, g, l)
                    b = bank(ly, g).rearrange("p (a t) -> p a t", a=2)
                    gate = gt[:, 8 * b_ + 2 * n:8 * b_ + 2 * n + 2, :]
                    y = yy[:, 2 * n:2 * n + 2, :]
                    rt = rot_t.rearrange("p (a t) -> p a t", a=2)
                    if b_ == 0:
                        emptied(ly, dve.scalar_tensor_tensor(y, gate, 1.0, b, ALU.add, ALU.mult))
                    else:
                        dve.scalar_tensor_tensor(rt, gate, 1.0, b, ALU.add, ALU.mult)
                        fence()
                        emptied(ly, dve.tensor_tensor(y, y, rt, ALU.add))
                        fence()
            for n in range(4):
                ly.wait_filled(dve, f"out{n}", l)
                v = xr[:, 2 * n:2 * n + 2, :]
                emptied(ly, dve.scalar_tensor_tensor(v, bank(ly, f"out{n}").rearrange("p (a t) -> p a t", a=2), 0.5, v, ALU.mult, ALU.add))
            ly.wait_emptied(dve, "ss2", l)
            normed(dve, gcol[:, 1, :], fence, done, "h2_ready")
            for n in range(16):
                ly.wait_emptied(dve, f"up{n}", l)
                v = hff[:, 2 * n:2 * n + 2, :]
                dve.tensor_tensor(v, v, v, ALU.mult)
            done("hidden_ready")
            for n in range(8):
                ly.wait_filled(dve, f"dn{n}", l)
                emptied(ly, dve.tensor_tensor(xr[:, n, :], xr[:, n, :], bank(ly, f"dn{n}")[:, 0:T], ALU.add))
            fence()

        @block.vector
        def _(dve):
            def done(name):
                dve.drain().then_inc(sem(name), 1)

            def emptied(b, ins):
                ins.then_inc(b.emptied["D"], 1)

            def bc(ap, n, where=1):
                v = ap.unsqueeze(where)
                shape = list(v.shape)
                shape[where] = n
                return v.to_broadcast(shape)

            fence = dve.drain

            def held(b, g, it):
                b.wait_filled(dve, g, it)
                dve.sem_inc(sem("groups_met"), 1)

            for n, e in enumerate(EPS):
                dve.memset(epsc[:, n:n + 1], e)
            dve.memset(one_, 1.0)
            dve.memset(zeros, 0.0)
            setup.wait_filled(dve, "colsC")
            emptied(setup, dve.tensor_copy(ccol, bank(setup, "colsC")[:, 0:16].rearrange("p (s k) -> p s k", s=2)))
            done("c_columns")
            dve.wait_ge(sem("x_landed"), 32)
            for i in range(4):
                for h in range(2):
                    dve.bn_stats(stats[:, i, h, :], x4[:, i, h * 512:(h + 1) * 512])
            fence()
            for i in range(4):
                dve.bn_aggr(mv[:, i, :], stats[:, i].rearrange("p a b -> p (a b)"))
            done("stats_ready")
            for g in range(4):
                setup.wait_filled(dve, f"xr{g}")
                emptied(setup, dve.tensor_copy(xr[:, 2 * g:2 * g + 2, :], bank(setup, f"xr{g}").rearrange("p (a t) -> p a t", a=2)))
            if first:
                dve.wait_ge(sem("std_ready"), 1)
                dve.reciprocal(rstd4, rstd4)
                fence()
                for i in range(4):
                    dve.tensor_scalar(x4[:, i, :], x4[:, i, :], mv[:, i, 0:1], rstd4[:, i:i + 1], ALU.subtract, ALU.mult)
                done("tokens_normalised")
            dve.wait_ge(s_tables, 16)
            dve.wait_ge(s_in, 16 * N_SMALL)
            ang, turns = ht[:, 0, :], ht[:, 1, :]
            dve.tensor_copy(ang, pos_i)
            fence()
            dve.tensor_scalar(ang, ang, cst("freq"), None, ALU.mult)
            fence()
            dve.tensor_scalar(turns, ang, float(0.5 / np.pi), None, ALU.mult)
            big = float(3 << 22)
            for x in (big, -big):
                fence()
                dve.tensor_scalar(turns, turns, x, None, ALU.add)
            two_pi_hi = 6.28125
            for x in (two_pi_hi, float(2 * np.pi - two_pi_hi)):
                fence()
                dve.scalar_tensor_tensor(ang, turns, -x, ang, ALU.mult, ALU.add)
            fence()
            dve.tensor_scalar(ang, ang, 3.1415925, -3.1415925, ALU.min, ALU.max)
            fence()
            dve.scalar_tensor_tensor(turns, ang, -1.0, ang, ALU.mult, ALU.max)
            fence()
            dve.tensor_scalar(turns, turns, -1.0, float(np.pi / 2), ALU.mult, ALU.add)
            done("angles_ready")
            setup.wait_filled(dve, "colsA")
            emptied(setup, dve.tensor_copy(cols[:, 0:ROWS_A], bank(setup, "colsA")[:, 0:ROWS_A]))
            setup.wait_filled(dve, "colsB")
            emptied(setup, dve.tensor_copy(cols[:, ROWS_A:], bank(setup, "colsB")[:, 0:ROWS_B]))
            fence()
            if first:
                first_vector(dve, done, emptied, bc, fence, held)
            else:
                done("residual_ready")
            if second:
                dve.memset(fn, 0.0)
                fence()
                ly.start(dve, "D")
                with dve.Fori(0, LAYERS) as l:
                    layer_vector(dve, l, done, emptied, bc, fence)
                en.wait_emptied(dve, "ssf")
                normed(dve, cols[:, COL["g_final_2"]:COL["g_final_2"] + KT], fence, done, "final_ready")
            done("finished")

    return nc


_INS = ["x", "c", "ctx", "c_ctx", "mod_w", "mod_b", "w_in", "rwkv_shift", "pool_w", "pool_scale", "rwkv_w0", "rwkv_w_up",
        "rwkv_a0", "rwkv_a_up", "rwkv_k_k", "rwkv_k_a", "rwkv_r_k", "rwkv_gn_g", "rwkv_gn_b", "hgrn_lb_logits",
        "hgrn_norm_g", "w_out", "ln_g", "ln_b", "positions_2", "g_mix_2", "w_in_2", "b_forget_2", "w_branch_2", "w_out_2",
        "g_mlp_2", "w_up_2", "w_down_2", "g_final_2"]


def kernel(**inputs):
    import concourse.bacc as _bacc
    from concourse.bass_utils import run_bass_kernel_spmd as _run

    nc = _bacc.Bacc("TRN2", target_bir_lowering=False, num_devices=1)
    arrays, args = {}, {}
    tables = dict(zip(("const", "const2"), constants()))
    for name in _INS + ["const", "const2"]:
        arr = tables[name] if name in tables else np.ascontiguousarray(inputs[name])
        arrays[f"in_{name}"] = arr
        args[name] = nc.dram_tensor(f"in_{name}", arr.shape, mybir.dt.from_np(arr.dtype), kind="ExternalInput").ap()
    out = nc.dram_tensor("out_0", (1, T, D), F32, kind="ExternalOutput").ap()
    build(nc, args, out)
    r = _run(nc, [arrays], core_ids=[0])
    return r.results[0]["out_0"]
```
